# Optimizing a Trainium2 kernel written in Bass

```python
import math, functools
import jax, jax.numpy as jnp
from jax import lax
import numpy as np

D_MODEL = 2048
BATCH = 1
SEQ = 256
DEPTH = 1
DEC_BATCH = 8
DEC_SEQ = 8
PAST_LEN = 2048
PAGE_SIZE = 128

ATT_HEADS = 8
HEAD_DIM = 128
D_ATT = ATT_HEADS * HEAD_DIM
D_CONV = D_MODEL - D_ATT
CONV_WIDTH = 3
DIL_PAIRS = ((128, 1), (512, 4), (2048, 16))
ATT_WINDOW = max(w for w, _ in DIL_PAIRS)
BAND_BLOCK = 128
ROPE_THETA = 10000.0
PEER_HEADS = 8
N_SUBKEYS = 128
N_EXPERTS = N_SUBKEYS * N_SUBKEYS
PEER_KEY_DIM = 256
PEER_TOPK = 16
PEER_TOKEN_BLOCK = 128
PLE_DIM = 256
DEEPNORM_ALPHA = (2.0 * DEPTH) ** 0.25
DEEPNORM_BETA = (8.0 * DEPTH) ** -0.25
LN_EPS = 1e-5

kernel_name = "hymba_dilated_conv_peer_decoder_step"

def layer_norm(x, g, b):
    xf = x.astype(jnp.float32)
    mu = jnp.mean(xf, -1, keepdims=True)
    var = jnp.mean(jnp.square(xf - mu), -1, keepdims=True)
    return ((xf - mu) * lax.rsqrt(var + LN_EPS) * g + b).astype(x.dtype)

def rope(x, pos):
    half = HEAD_DIM // 2
    inv = ROPE_THETA ** (-jnp.arange(half, dtype=jnp.float32) / half)
    ang = pos.astype(jnp.float32)[:, None] * inv[None, :]
    cos = jnp.cos(ang)[None, :, None, :]
    sin = jnp.sin(ang)[None, :, None, :]
    xf = x.astype(jnp.float32)
    x1, x2 = xf[..., :half], xf[..., half:]
    return jnp.concatenate([x1 * cos - x2 * sin, x2 * cos + x1 * sin], -1).astype(x.dtype)

def split_projection(x, w_in):
    h = jnp.einsum('btd,de->bte', x, w_in)
    q, k, v, u, gb, gc = jnp.split(
        h, [D_ATT, 2 * D_ATT, 3 * D_ATT, 3 * D_ATT + D_CONV, 3 * D_ATT + 2 * D_CONV], axis=-1)
    B, T = x.shape[:2]
    heads = lambda a: a.reshape(B, T, ATT_HEADS, HEAD_DIM)
    return heads(q), heads(k), heads(v), gc * u, gb

def short_conv(z_ext, conv_w, T):
    return sum(conv_w[j] * z_ext[:, j:j + T] for j in range(CONV_WIDTH))

def dilated_branch_prompt(q, k, v, sub_w, d):
    B, T, H, Dh = q.shape
    L = T // d
    nb = -(-L // BAND_BLOCK)
    Lp = nb * BAND_BLOCK
    G = B * d

    def to_sub(a):
        return a.reshape(B, L, d, H, Dh).transpose(0, 2, 1, 3, 4).reshape(G, L, H, Dh)

    qs = jnp.pad(to_sub(q), ((0, 0), (0, Lp - L), (0, 0), (0, 0))).reshape(G, nb, BAND_BLOCK, H, Dh)

    def band_keys(a):
        a = jnp.pad(to_sub(a), ((0, 0), (BAND_BLOCK, Lp - L), (0, 0), (0, 0)))
        a = a.reshape(G, nb + 1, BAND_BLOCK, H, Dh)
        return jnp.concatenate([a[:, :-1], a[:, 1:]], axis=2)

    ks, vs = band_keys(k), band_keys(v)
    s = jnp.einsum('gnqhd,gnkhd->gnqhk', qs, ks,
                   preferred_element_type=jnp.float32) * (HEAD_DIM ** -0.5)
    qi = jnp.arange(BAND_BLOCK)[:, None]
    kj = jnp.arange(2 * BAND_BLOCK)[None, :]
    dist = BAND_BLOCK + qi - kj
    kpos = (jnp.arange(nb)[:, None] - 1) * BAND_BLOCK + jnp.arange(2 * BAND_BLOCK)[None, :]
    valid = ((dist >= 0) & (dist <= sub_w))[None] & (kpos >= 0)[:, None, :]
    s = jnp.where(valid[None, :, :, None, :], s, -jnp.inf)
    m = jnp.max(s, axis=-1)
    p = jnp.exp(s - m[..., None])
    l = jnp.sum(p, axis=-1)
    acc = jnp.einsum('gnqhk,gnkhd->gnqhd', p, vs.astype(jnp.float32))

    def from_sub(a):
        tail = a.shape[3:]
        a = a.reshape((B, d, Lp) + tail)[:, :, :L]
        return jnp.moveaxis(a, 1, 2).reshape((B, T) + tail)

    return from_sub(acc), from_sub(m), from_sub(l)

def dilated_branch_sample(q, k_all, v_all, sub_w, d):
    S = q.shape[1]
    n_buf = k_all.shape[1] - S
    idx = n_buf + jnp.arange(S)[:, None] - d * jnp.arange(sub_w + 1)[None, :]
    valid = idx >= 0
    idx = jnp.maximum(idx, 0)
    kg = k_all[:, idx]
    vg = v_all[:, idx]
    s = jnp.einsum('bshd,bsjhd->bshj', q, kg,
                   preferred_element_type=jnp.float32) * (HEAD_DIM ** -0.5)
    s = jnp.where(valid[None, :, None, :], s, -jnp.inf)
    m = jnp.max(s, axis=-1)
    p = jnp.exp(s - m[..., None])
    l = jnp.sum(p, axis=-1)
    acc = jnp.einsum('bshj,bsjhd->bshd', p, vg.astype(jnp.float32))
    return acc, m, l

def combine_branches(parts):
    big_m = functools.reduce(jnp.maximum, [m for _, m, _ in parts])
    num = sum(jnp.exp(m - big_m)[..., None] * acc for acc, m, _ in parts)
    den = sum(jnp.exp(m - big_m) * l for _, m, l in parts)
    return num / den[..., None]

def peer_ffn(x, w_q, sub_keys, u_tab, v_tab):
    B, T, D = x.shape
    N = B * T
    xf = x.reshape(N, D)
    q = jnp.einsum('nd,de->ne', xf, w_q).reshape(N, PEER_HEADS, 2, PEER_KEY_DIM // 2)
    sc = jnp.einsum('nhpc,pkc->nhpk', q, sub_keys, preferred_element_type=jnp.float32)
    s_top, i_top = lax.top_k(sc, PEER_TOPK)
    cand = s_top[:, :, 0, :, None] + s_top[:, :, 1, None, :]
    c_top, c_idx = lax.top_k(cand.reshape(N, PEER_HEADS, PEER_TOPK * PEER_TOPK), PEER_TOPK)
    e1 = jnp.take_along_axis(i_top[:, :, 0], c_idx // PEER_TOPK, axis=-1)
    e2 = jnp.take_along_axis(i_top[:, :, 1], c_idx % PEER_TOPK, axis=-1)
    experts = (e1 * N_SUBKEYS + e2).reshape(N, PEER_HEADS * PEER_TOPK)
    gates = jax.nn.softmax(c_top, axis=-1).reshape(N, PEER_HEADS * PEER_TOPK)
    n_blk = -(-N // PEER_TOKEN_BLOCK)
    pad = n_blk * PEER_TOKEN_BLOCK - N
    xb = jnp.pad(xf, ((0, pad), (0, 0))).reshape(n_blk, PEER_TOKEN_BLOCK, D)
    eb = jnp.pad(experts, ((0, pad), (0, 0))).reshape(n_blk, PEER_TOKEN_BLOCK, -1)
    gb = jnp.pad(gates, ((0, pad), (0, 0))).reshape(n_blk, PEER_TOKEN_BLOCK, -1)

    def block(args):
        xt, et, gt = args
        u = u_tab[et]
        h = jnp.einsum('nd,nkd->nk', xt, u, preferred_element_type=jnp.float32)
        a = (gt * jax.nn.gelu(h, approximate=False)).astype(v_tab.dtype)
        return jnp.einsum('nk,nkd->nd', a, v_tab[et])

    y = lax.map(block, (xb, eb, gb))
    return y.reshape(-1, D)[:N].reshape(B, T, D).astype(x.dtype)

def layer_tail(h, att, conv, p_i, w_out, ln1_g, ln1_b, peer_wq, peer_subkeys, peer_u, peer_v,
               ln2_g, ln2_b, ple_gate, ple_proj):
    B, T, _ = h.shape
    mixed = jnp.concatenate([att.reshape(B, T, D_ATT).astype(h.dtype), conv], axis=-1)
    mixed = jnp.einsum('bte,ed->btd', mixed, w_out)
    h = layer_norm(DEEPNORM_ALPHA * h + mixed, ln1_g, ln1_b)
    h = layer_norm(DEEPNORM_ALPHA * h + peer_ffn(h, peer_wq, peer_subkeys, peer_u, peer_v), ln2_g, ln2_b)
    gate = jax.nn.sigmoid(jnp.einsum('btd,de->bte', h, ple_gate))
    return h + gate * jnp.einsum('btp,pd->btd', p_i, ple_proj)

def setup_inputs(seed: int = 0) -> dict:
    key = jax.random.key(seed)
    ks = jax.random.split(key, 24)
    nrm = lambda k, shape, s: jax.random.normal(k, shape, jnp.float32) * s
    n_buf = min(ATT_WINDOW, PAST_LEN)
    d_in = 3 * D_ATT + 3 * D_CONV
    return {
        "x_prompt": nrm(ks[0], (BATCH, SEQ, D_MODEL), 1.0),
        "x_sample": nrm(ks[1], (DEC_BATCH, DEC_SEQ, D_MODEL), 1.0),
        "state_attn_k": nrm(ks[2], (DEPTH, DEC_BATCH, n_buf, ATT_HEADS, HEAD_DIM), 1.0),
        "state_attn_v": nrm(ks[3], (DEPTH, DEC_BATCH, n_buf, ATT_HEADS, HEAD_DIM), 1.0),
        "state_conv": nrm(ks[4], (DEPTH, DEC_BATCH, CONV_WIDTH - 1, D_CONV), 1.0),
        "p_prompt": nrm(ks[5], (DEPTH, BATCH, SEQ, PLE_DIM), 1.0),
        "p_sample": nrm(ks[6], (DEPTH, DEC_BATCH, DEC_SEQ, PLE_DIM), 1.0),
        "w_in": nrm(ks[7], (DEPTH, D_MODEL, d_in), D_MODEL ** -0.5),
        "w_conv": nrm(ks[8], (DEPTH, CONV_WIDTH, D_CONV), CONV_WIDTH ** -0.5),
        "w_out": nrm(ks[9], (DEPTH, D_MODEL, D_MODEL), D_MODEL ** -0.5 * DEEPNORM_BETA),
        "ln1_g": 1.0 + nrm(ks[10], (DEPTH, D_MODEL), 0.01),
        "ln1_b": nrm(ks[11], (DEPTH, D_MODEL), 0.01),
        "peer_wq": nrm(ks[12], (DEPTH, D_MODEL, PEER_HEADS * PEER_KEY_DIM), D_MODEL ** -0.5),
        "peer_subkeys": nrm(ks[13], (DEPTH, 2, N_SUBKEYS, PEER_KEY_DIM // 2), (PEER_KEY_DIM // 2) ** -0.5),
        "peer_u": nrm(ks[14], (DEPTH, N_EXPERTS, D_MODEL), D_MODEL ** -0.5),
        "peer_v": nrm(ks[15], (DEPTH, N_EXPERTS, D_MODEL), DEEPNORM_BETA),
        "ln2_g": 1.0 + nrm(ks[16], (DEPTH, D_MODEL), 0.01),
        "ln2_b": nrm(ks[17], (DEPTH, D_MODEL), 0.01),
        "ple_gate": nrm(ks[18], (DEPTH, D_MODEL, D_MODEL), D_MODEL ** -0.5),
        "ple_proj": nrm(ks[19], (DEPTH, PLE_DIM, D_MODEL), PLE_DIM ** -0.5),
    }

def reference(x_prompt, x_sample, state_attn_k, state_attn_v, state_conv, p_prompt, p_sample,
              w_in, w_conv, w_out, ln1_g, ln1_b, peer_wq, peer_subkeys, peer_u, peer_v,
              ln2_g, ln2_b, ple_gate, ple_proj):
    t_p = x_prompt.shape[1]
    t_s = x_sample.shape[1]
    pos_p = jnp.arange(t_p)
    pos_s = PAST_LEN + jnp.arange(t_s)
    h_p, h_s = x_prompt, x_sample
    kp, vp, cp, ksl, vsl, csl = [], [], [], [], [], []
    for i in range(DEPTH):
        tail = (w_out[i], ln1_g[i], ln1_b[i], peer_wq[i], peer_subkeys[i], peer_u[i], peer_v[i],
                ln2_g[i], ln2_b[i], ple_gate[i], ple_proj[i])
        q, k, v, z, gb = split_projection(h_p, w_in[i])
        q, k = rope(q, pos_p), rope(k, pos_p)
        att = combine_branches([dilated_branch_prompt(q, k, v, w // d, d) for w, d in DIL_PAIRS])
        z_ext = jnp.pad(z, ((0, 0), (CONV_WIDTH - 1, 0), (0, 0)))
        conv = gb * short_conv(z_ext, w_conv[i], t_p)
        keep_p = min(ATT_WINDOW, t_p)
        kp.append(k[:, t_p - keep_p:])
        vp.append(v[:, t_p - keep_p:])
        cp.append(z_ext[:, -(CONV_WIDTH - 1):])
        h_p = layer_tail(h_p, att, conv, p_prompt[i], *tail)
        q, k, v, z, gb = split_projection(h_s, w_in[i])
        q, k = rope(q, pos_s), rope(k, pos_s)
        k_all = jnp.concatenate([state_attn_k[i].astype(k.dtype), k], axis=1)
        v_all = jnp.concatenate([state_attn_v[i].astype(v.dtype), v], axis=1)
        att = combine_branches([dilated_branch_sample(q, k_all, v_all, w // d, d) for w, d in DIL_PAIRS])
        z_ext = jnp.concatenate([state_conv[i].astype(z.dtype), z], axis=1)
        conv = gb * short_conv(z_ext, w_conv[i], t_s)
        n_all = k_all.shape[1]
        keep_s = min(ATT_WINDOW, n_all)
        ksl.append(k_all[:, n_all - keep_s:])
        vsl.append(v_all[:, n_all - keep_s:])
        csl.append(z_ext[:, -(CONV_WIDTH - 1):])
        h_s = layer_tail(h_s, att, conv, p_sample[i], *tail)
    y_prompt, y_sample = h_p, h_s
    new_k_prompt, new_v_prompt, new_conv_prompt = jnp.stack(kp), jnp.stack(vp), jnp.stack(cp)
    new_k_sample, new_v_sample, new_conv_sample = jnp.stack(ksl), jnp.stack(vsl), jnp.stack(csl)
    return (y_prompt, y_sample, new_k_prompt, new_v_prompt, new_conv_prompt,
            new_k_sample, new_v_sample, new_conv_sample)


_drawn_inputs = setup_inputs


def setup_inputs(seed=0):
    import zlib

    import numpy as np

    out = dict(_drawn_inputs(seed))
    spreads = {}
    factors = {}
    for name, (base, spread) in spreads.items():
        noise = np.random.default_rng([zlib.crc32(name.encode()), seed]).standard_normal(out[name].shape)
        drawn = base * np.exp(spread * noise) if base else spread * noise
        out[name] = __import__('jax').numpy.asarray(drawn.astype(out[name].dtype))
    for name, factor in factors.items():
        out[name] = (out[name] * factor).astype(out[name].dtype)
    return out
```

```python
import concourse.bass as bass
from concourse import mybir
from contextlib import ExitStack

D = 2048
HEADS, DH = 8, 128
DA = HEADS * DH
DC = D - DA
TP, NB, NS = 256, 8, 8
TS = NB * NS
N = TS + TP
PAST = 2048
KT = D // 128
SCALE = float(DH) ** -0.5
ALPHA = 2.0 ** 0.25
EPS = 1e-5
TILES = [(0, TS), (TS, 128), (TS + 128, 128)]
PH, NK, TOPK = 8, 128, 16
NF = 2 * PH
PLE = 256
CW = 512
KP = 4
PPC = KT // KP
GA, RA = 96, 8
OLD = 16 * GA
GB, RB = 128, 4
SCOLS = GA * RA + TS + GB * RB
ZW = 2 + TP + NB * (2 + NS)
Z0 = 2 + TP
NSLOT = 8
PHASES = [("u", 1, 8), ("u", 2, 8), ("v", 1, 8), ("u", 0, 4), ("v", 2, 8), ("v", 0, 4)]
STARTS = [sum(p[2] for p in PHASES[:n]) for n in range(len(PHASES))]
BLOCKS = sum(p[2] for p in PHASES)


def decoder_step(nc, x_p, x_s, st_k, st_v, st_c, p_p, p_s, w_in, w_conv, w_out, ln1_g, ln1_b,
                 wq, subkeys, peer_u, peer_v, ln2_g, ln2_b, w_gate, w_ple,
                 c_ident, c_cos, c_sin, c_mp_add, c_mp_mul, c_ms_add, c_ms_mul, c_mc_add, c_mc_mul,
                 c_iota,
                 y_p, y_s, o_kp, o_vp, o_cp, o_ks, o_vs, o_cs):
    f32, f32r, bf16, u32, i32 = (mybir.dt.float32, mybir.dt.float32r, mybir.dt.bfloat16,
                                 mybir.dt.uint32, mybir.dt.int32)
    ALU = mybir.AluOpType
    ACT = mybir.ActivationFunctionType
    AX = mybir.AxisListType.X
    ds = bass.ds
    KB = 1024

    xp_v = x_p.rearrange("a (t p) d -> p (a t) d", p=128)
    xs_v = x_s.rearrange("b s d -> (b s) d")
    pp_v = p_p.rearrange("a b (t p) d -> p (a b t) d", p=128)
    ps_v = p_s.rearrange("a b s d -> (a b s) d")
    kst = st_k.rearrange("a b n h d -> (a b) n (h d)")
    vst = st_v.rearrange("a b n h d -> (a b) n (h d)")
    oks = o_ks.rearrange("a b n h d -> (a b) n (h d)")
    ovs = o_vs.rearrange("a b n h d -> (a b) n (h d)")
    okp = o_kp.rearrange("a b (t p) h d -> p (a b t) (h d)", p=128)
    ovp = o_vp.rearrange("a b (t p) h d -> p (a b t) (h d)", p=128)
    wiew = lambda w: w.rearrange("a (k p) e -> p (a k) e", p=128)
    win_v, wout_v, wq_v, wg_v, wple_v = map(wiew, (w_in, w_out, wq, w_gate, w_ple))
    u_tab = peer_u.rearrange("a n d -> (a n) d")
    v_tab = peer_v.rearrange("a n d -> (a n) d")
    yp_v = y_p.rearrange("a (t p) d -> p (a t) d", p=128)
    ys_v = y_s.rearrange("b s d -> (b s) d")

    BASE = 16512
    used = []

    def at(name, shape, dt, off):
        used.append(name)
        return nc.alloc_sbuf_tensor_at(name, shape, dt, offset=BASE + off)

    raw = at("w_raw", [128, 2, KP, CW], f32, 0)
    whi = at("w_hi", [128, 2, KP, CW], f32r, 16 * KB)
    wlo = at("w_lo", [128, 2, KP, CW], f32r, 32 * KB)
    ka = at("keys_old", [GA, RA, DA], f32, 0)
    kb = at("keys_last", [GB, RB, DA], f32, 32 * KB)
    zrows = at("conv_rows_out", [2 + 2 * NB, DC], f32, 0)
    sc = at("peer_scores", [128, 3, NF, NK], f32, 0)
    cand = at("candidates", [128, PH, TOPK, TOPK], f32, 24 * KB)
    hot = at("one_hot", [128, PH, TOPK, TOPK], f32, 32 * KB)

    qkv_p = at("qkv_prompt", [128, 2, 3 * DA], f32, 48 * KB)
    ubuf = at("conv_u", [128, 8, ZW], f32, 72 * KB)
    zbuf = at("conv_z", [128, 8, ZW], f32, 72 * KB + 8 * ZW * 4)
    crow = at("conv_state_rows", [2 * NB, DC], f32, 72 * KB)
    va = at("values_old", [GA, RA, DA], f32, 48 * KB)
    vb = at("values_last", [GB, RB, DA], f32, 80 * KB)
    ln1 = at("ln1_gain_bias", [128, 2, D], f32, 48 * KB)
    qpt = at("peer_queries", [128, NF, N], f32, 64 * KB)
    ring = at("expert_rows", [128, NSLOT, D], f32, 48 * KB)
    plew = at("ple_weights", [128, 2, D], f32, 96 * KB)
    pleo = at("ple_out", [128, 3, D], f32, 48 * KB)
    gsig = at("gate_sigmoid", [128, 3, CW], f32, 72 * KB)

    qkv_s = at("qkv_decode", [TS, 3 * DA], f32, 96 * KB)
    qt = at("q_T", [128, HEADS, N], f32, 108 * KB)
    kt_ = at("k_T", [128, HEADS, N], f32, 118 * KB)
    ln2 = at("ln2_gain_bias", [128, 2, D], f32, 112 * KB)

    xt = at("x_tokens", [128, 3, D], f32, 128 * KB)
    rtmp = at("rope_products", [128, 4, DA], f32, 128 * KB)
    psm = at("prompt_scores", [128, 2, 3, 128], f32, 144 * KB)
    ppt = at("prompt_probs_T", [128, 2, 3, 128], f32, 147 * KB)
    ktb = at("old_k_T", [128, 2, 512], f32, 128 * KB)
    ssm = at("decode_scores", [64, SCOLS], f32, 132 * KB)
    pta = at("probs_T_old", [GA, RA, 64], f32, 138 * KB)
    ptb = at("probs_T_last", [GB, RB, 64], f32, 140 * KB)
    ptc = at("probs_T_new", [TS, 64], f32, 141 * KB)
    qpad = at("q_padded", [128, HEADS, 64], f32, 142 * KB)

    thi = at("act_T_hi", [128, KT, N], f32r, 152 * KB)
    tlo = at("act_T_lo", [128, KT, N], f32r, 172 * KB)
    yacc = at("expert_sums", [128, 3, D], f32, 152 * KB)
    yhalf = at("expert_sums_half", [TS, D], f32, 176 * KB)
    S0 = 184 * KB
    top = at("top_values", [128, NF, TOPK], f32, S0)
    topi = at("top_keys", [128, NF, TOPK], u32, S0 + 1 * KB)
    topf = at("top_keys_f", [128, NF, TOPK], f32, S0 + 2 * KB)
    ctop = at("cand_top", [128, PH, TOPK], f32, S0 + 3 * KB)
    cidx = at("cand_index", [128, PH, TOPK], u32, S0 + 3 * KB + 512)
    cint = at("cand_rank_int", [128, 2, PH, TOPK], u32, S0 + 4 * KB)
    cflt = at("cand_rank", [128, 2, PH, TOPK], f32, S0 + 5 * KB)
    esel = at("expert_part", [128, 2, PH, TOPK], f32, S0 + 6 * KB)

    M0 = 192 * KB
    off = [M0]

    def small(name, shape, dt, size):
        n = size
        for s in shape[1:]:
            n *= s
        t = at(name, shape, dt, off[0])
        off[0] += (n + 31) // 32 * 32
        return t

    ident = small("identity", [128, 128], f32, 4)
    subT = small("subkeys_T", [128, 2, NK], f32, 4)
    cosb = small("rope_cos", [128, 3, DH // 2], f32, 4)
    sinb = small("rope_sin", [128, 3, DH // 2], f32, 4)
    cw = small("conv_weights", [128, 3, 8], f32, 4)
    mx = small("row_max", [128, 4], f32, 4)
    nmx = small("neg_row_max", [128, 2, 2], f32, 4)
    rs = small("row_sum", [128, 4], f32, 4)
    bst = small("ln_stats", [128, 4, 6], f32, 4)
    mv = small("ln_mean_var", [128, 2], f32, 4)
    vst_ = small("ln_var_eps", [128, 1], f32, 4)
    std = small("ln_std", [128, 2], f32, 4)
    iota = small("iota16", [128, TOPK], f32, 4)
    tok = small("pool_token", [128, 1], f32, 4)
    idxc = small("block_experts", [128, 2, TOPK], u32, 4)
    hblk = small("block_dots", [128, 2 * TOPK], f32, 4)
    ablk = small("block_gates", [128, 2 * TOPK], f32, 4)
    zl = small("conv_last_rows_T", [128, 8, 2 + 2 * NB], f32, 4)
    mp_add = small("prompt_mask_add", [128, 384], bf16, 2)
    mp_mul = small("prompt_mask_mul", [128, 384], bf16, 2)
    shared = off[0]
    ms_add = small("decode_mask_add", [64, SCOLS], bf16, 2)
    ms_mul = small("decode_mask_mul", [64, SCOLS], bf16, 2)
    mc_add = small("new_mask_add", [64, NB, TS], bf16, 2)
    mc_mul = small("new_mask_mul", [64, NB, TS], bf16, 2)
    assert BASE + off[0] <= 229344, off[0]
    end_masks = off[0]
    off[0] = shared
    idx_all = small("experts", [128, (BLOCKS + 1) * TOPK], u32, 4)
    idx_s = small("experts_decode", [64, 2, 64], u32, 4)
    gates = small("gates", [128, 3, 128], f32, 4)
    hdot = small("dots", [128, 3, 128], f32, 4)
    assert off[0] <= end_masks
    pnat = at("ple_tokens", [128, 3, PLE], f32, 80 * KB)
    pT = at("ple_T", [128, 2, N], f32, 84 * KB)
    subn = at("subkeys_rows", [128, 2, 128], f32, 76 * KB + 512)

    ctx = ExitStack()
    with ctx:
        PS = ctx.enter_context(nc.psum_tensor("psum", [128, 8, 512], f32))
        sem = lambda name: ctx.enter_context(nc.semaphore(name))
        x_in, c_in, c2_in = sem("x_in"), sem("consts_in"), sem("late_consts_in")
        w_in_s = [sem("w_slot0_in"), sem("w_slot1_in")]
        w_hi_ready, w_lo_ready, w_used = sem("w_hi_ready"), sem("w_lo_ready"), sem("w_used")
        acc_free = sem("acc_free")
        tp_done, th_ready, tl_ready = sem("transposed"), sem("t_hi_ready"), sem("t_lo_ready")
        small_T, small_ok = sem("small_transposed"), sem("small_copied")
        dstep = sem("dve_step")
        z_pad = sem("z_pad_set")
        rope_ok = sem("rope_done")
        zl_ready, zl_T, zl_out = sem("conv_rows_ready"), sem("conv_rows_T"), sem("conv_rows_copied")
        conv_m, conv_hi = sem("conv_ready"), sem("conv_hi_ready")
        qk_T, qk_ok = sem("qk_transposed"), sem("qk_copied")
        s_score, s_neg, s_exp, s_prob = sem("p_scores"), sem("p_negmax"), sem("p_exp"), sem("p_probs")
        s_pT, s_pok, s_pv, s_po = sem("p_probs_T"), sem("p_probs_T_ok"), sem("p_out"), sem("p_out_copied")
        k_in, v_in, v_used = sem("keys_in"), sem("values_in"), sem("values_used")
        q_pad, kT_raw, kT_ok = sem("q_pad_ready"), sem("old_kT_psum"), sem("old_kT_copied")
        d_score, d_neg, d_exp, d_prob = sem("d_scores"), sem("d_negmax"), sem("d_exp"), sem("d_probs")
        d_pT, d_pok = sem("d_probs_T"), sem("d_probs_T_ok")
        att_ok = sem("decode_att_done")
        var_ok, std_ok = sem("ln_var_ready"), sem("ln_std_ready")
        ln_ok = sem("ln_done")
        ln1_in, ln2_in = sem("ln1_in"), sem("ln2_in")
        sc_psum, sc_ok = sem("scores_psum"), sem("scores_copied")
        g_sub, g_exp = sem("gate_logits"), sem("gate_exp")
        g_free, g_token = sem("ring_free"), sem("pool_token_done")
        g_in = [sem(f"row_slot{i}_in") for i in range(NSLOT)]
        idx_st = sem("block_staged")
        dots, gelu_ok = sem("dots_ready"), sem("gelu_ready")
        pack_rd, pack_in = sem("pack_ready"), sem("packed_in")
        fold_rd, fold_in = sem("fold_ready"), sem("folded_in")
        ring_done = sem("ring_done")
        ple_in, pT_psum, pT_ok, ple_ps, ple_ok = (sem("ple_in"), sem("ple_T_psum"), sem("ple_T_ok"),
                                                  sem("ple_psum"), sem("ple_copied"))
        sig_ok, fin_ok = sem("sigmoid_ready"), sem("final_ready")
        out_s, kvcopy = sem("outputs_written"), sem("cache_copied")
        zrow_s = sem("conv_rows_written")

        def rows_of(buf, t):
            return buf[0:TILES[t][1], t, :]

        block = ctx.enter_context(nc.Block())

        @block.sync
        def _(sp):
            copies = [0]

            def copy_part(src, dst, b, j):
                n = (PAST - NS) * DA // 128
                s = src[b, NS:PAST, :] if isinstance(b, int) else src[ds(b, 1), NS:PAST, :].rearrange("a n d -> (a n) d")
                o = dst[b, 0:PAST - NS, :] if isinstance(b, int) else dst[ds(b, 1), 0:PAST - NS, :].rearrange("a n d -> (a n) d")
                s = s.rearrange("n d -> (n d)").rearrange("(p m) -> p m", m=n)
                o = o.rearrange("n d -> (n d)").rearrange("(p m) -> p m", m=n)
                sp.dma_start(o[16 * j:16 * j + 16, :], s[16 * j:16 * j + 16, :]).then_inc(kvcopy, 16)

            def load_piece(view, cols, pc, k):
                slot = k % 2
                if not (isinstance(pc, int) and pc < 2):
                    sp.wait_ge(w_lo_ready, pc - 1)
                sp.dma_start(raw[:, slot, :, :], view[:, k * KP:(k + 1) * KP, cols]).then_inc(w_in_s[slot], 16)

            def load_chunks(view, col0, pc0, pairs, src=None, dst=None, b0=0, peel=False):
                if peel:
                    for h in range(2):
                        for k in range(PPC):
                            load_piece(view, slice(col0 + h * CW, col0 + (h + 1) * CW), pc0 + h * PPC + k, k)
                            copy_part(src, dst, b0, PPC * h + k)
                    col0, pc0, b0, pairs = col0 + 2 * CW, pc0 + 2 * PPC, b0 + 1, pairs - 1
                if pairs == 1:
                    for h in range(2):
                        for k in range(PPC):
                            load_piece(view, slice(col0 + h * CW, col0 + (h + 1) * CW), pc0 + h * PPC + k, k)
                            if src is not None:
                                copy_part(src, dst, b0, PPC * h + k)
                    return
                with sp.Fori(0, pairs) as i:
                    for h in range(2):
                        for k in range(PPC):
                            load_piece(view, ds(i * (2 * CW) + (col0 + h * CW), CW),
                                       i * (2 * PPC) + (pc0 + h * PPC + k), k)
                            if src is not None:
                                copy_part(src, dst, i + b0, PPC * h + k)

            sp.dma_start(ident[:, :], c_ident).then_inc(x_in, 16)
            sp.dma_start(xt[:, 1:3, :], xp_v).then_inc(x_in, 16)
            sp.dma_start(xt[0:TS, 0, :], xs_v).then_inc(x_in, 16)
            sp.dma_start(crow[:, :], st_c.rearrange("a b j d -> (a b j) d")).then_inc(c_in, 16)
            sp.dma_start(subn[:, :, :], subkeys.rearrange("a q k c -> k (a q) c")).then_inc(c_in, 16)
            for dst, src in ((cosb, c_cos), (sinb, c_sin), (mp_add, c_mp_add), (mp_mul, c_mp_mul),
                             (ms_add, c_ms_add), (ms_mul, c_ms_mul), (mc_add, c_mc_add),
                             (mc_mul, c_mc_mul), (iota, c_iota)):
                sp.dma_start(dst[...], src).then_inc(c2_in, 16)
            with nc.allow_non_contiguous_dma(reason="3072 weights, once"):
                sp.dma_start(cw[:, :, :], w_conv.rearrange("a j (f p) -> p (a j) f", p=128)).then_inc(c2_in, 16)
            load_chunks(win_v, 0, 0, 3, kst, oks, 0, peel=True)
            load_chunks(win_v, 3 * DA, 24, 1, kst, oks, 3)
            load_chunks(win_v, 3 * DA + 2 * DC, 32, 1, kst, oks, 4)
            load_chunks(win_v, 3 * DA + DC, 40, 1, kst, oks, 5)
            sp.wait_ge(rope_ok, 1)
            sp.dma_start(okp, qkv_p[:, :, DA:2 * DA]).then_inc(out_s, 16)
            sp.dma_start(ovp, qkv_p[:, :, 2 * DA:3 * DA]).then_inc(out_s, 16)
            for b in range(NB):
                sp.dma_start(oks[b, PAST - NS:PAST, :], qkv_s[b * NS:(b + 1) * NS, DA:2 * DA]).then_inc(out_s, 16)
                sp.dma_start(ovs[b, PAST - NS:PAST, :], qkv_s[b * NS:(b + 1) * NS, 2 * DA:3 * DA]).then_inc(out_s, 16)
            sp.wait_ge(zl_out, 1)
            sp.dma_start(o_cp.rearrange("a b j d -> (a b j) d"), zrows[0:2, :]).then_inc(zrow_s, 16)
            sp.dma_start(o_cs.rearrange("a b j d -> (a b j) d"), zrows[2:2 + 2 * NB, :]).then_inc(zrow_s, 16)
            sp.wait_ge(zrow_s, 32)

            def load_k(b):
                bb = ds(b, 1)
                sp.dma_start(ka[:, :, :], kst[bb, 0:OLD, :].rearrange("a (g r) d -> (a g) r d", r=16)[:, 0:RA, :]).then_inc(k_in, 16)
                sp.dma_start(kb[:, :, :], kst[bb, OLD:PAST, :].rearrange("a (g r) d -> (a g) r d", r=RB)).then_inc(k_in, 16)

            def load_v(b):
                bb = ds(b, 1)
                sp.dma_start(va[:, :, :], vst[bb, 0:OLD, :].rearrange("a (g r) d -> (a g) r d", r=16)[:, 0:RA, :]).then_inc(v_in, 16)
                sp.dma_start(vb[:, :, :], vst[bb, OLD:PAST, :].rearrange("a (g r) d -> (a g) r d", r=RB)).then_inc(v_in, 16)

            load_k(0)
            sp.wait_ge(out_s, 16 * (2 + 2 * NB))
            for j in range(8):
                copy_part(vst, ovs, 2, j)
            sp.wait_ge(s_po, HEADS)
            load_v(0)
            with sp.Fori(1, NB) as b:
                sp.wait_ge(kT_raw, b * 24)
                load_k(b)
                sp.wait_ge(v_used, b)
                load_v(b)
            sp.wait_ge(att_ok, 1)
            sp.dma_start(xt[:, 1:3, :], xp_v).then_inc(x_in, 16)
            sp.dma_start(xt[0:TS, 0, :], xs_v).then_inc(x_in, 16)
            sp.dma_start(ln1[:, 0, :], ln1_g.rearrange("a d -> (a d)").partition_broadcast(128)).then_inc(ln1_in, 16)
            sp.dma_start(ln1[:, 1, :], ln1_b.rearrange("a d -> (a d)").partition_broadcast(128)).then_inc(ln1_in, 16)
            load_chunks(wout_v, 0, 48, 2, kst, oks, 6)
            load_chunks(wq_v, 0, 64, 2, vst, ovs, 0)
            for b in range(3, 8):
                for j in range(8):
                    copy_part(vst, ovs, b, j)
            sp.dma_start(xt[TS:128, 0, :], xt[0:TS, 0, :]).then_inc(pack_in, 16)
            sp.wait_ge(sc_ok, 12)
            sp.dma_start(ln2[:, 0, :], ln2_g.rearrange("a d -> (a d)").partition_broadcast(128)).then_inc(ln2_in, 16)
            sp.dma_start(ln2[:, 1, :], ln2_b.rearrange("a d -> (a d)").partition_broadcast(128)).then_inc(ln2_in, 16)
            sp.wait_ge(pack_rd, 1)
            for n, s in enumerate([k for k, p in zip(STARTS, PHASES) if p[1] == 0]):
                for half in range(2):
                    sp.dma_start(idx_all[half * TS:(half + 1) * TS, s * TOPK:(s + 4) * TOPK],
                                 idx_s[:, half, :]).then_inc(pack_in, 16)
            sp.dma_start(gates[TS:128, 0, 0:64], gates[0:TS, 0, 64:128]).then_inc(pack_in, 16)
            sp.wait_ge(fold_rd, 1)
            sp.dma_start(yhalf[:, :], yacc[TS:128, 0, :]).then_inc(fold_in, 16)
            sp.dma_start(plew[:, :, :], wple_v).then_inc(ple_in, 16)
            sp.dma_start(pnat[:, 1:3, :], pp_v).then_inc(ple_in, 16)
            sp.dma_start(pnat[0:TS, 0, :], ps_v).then_inc(ple_in, 16)
            load_chunks(wg_v, 0, 80, 2)
            for c in range(4):
                sp.wait_ge(fin_ok, c + 1)
                cc = slice(c * CW, (c + 1) * CW)
                sp.dma_start(yp_v[:, :, cc], xt[:, 1:3, cc]).then_inc(out_s, 16)
                sp.dma_start(ys_v[:, cc], xt[0:TS, 0, cc]).then_inc(out_s, 16)
            sp.wait_ge(out_s, 16 * (2 + 2 * NB + 8))
            sp.wait_ge(kvcopy, 16 * 8 * 2 * NB)

        @block.gpsimd
        def _(pool):
            nc.gpsimd.memset(tok[:, :], 0.0).then_inc(g_token, 1)

            def low(pc, slot):
                pool.wait_ge(w_hi_ready, pc + 1)
                nc.gpsimd.tensor_tensor(wlo[:, slot, :, :], raw[:, slot, :, :],
                                        whi[:, slot, :, :].bitcast(f32), ALU.subtract).then_inc(w_lo_ready, 1)

            def lows(first, count):
                with pool.Fori(0, count // 2) as i:
                    for slot in range(2):
                        low(i * 2 + (first + slot), slot)

            lows(0, 48)
            pool.wait_ge(att_ok, 1)
            lows(48, 32)

            def gathers(k, half, table):
                for j in range(TOPK):
                    if j % 4 == 0:
                        pool.wait_ge(g_token, k * 4 + (j // 4 + 1))
                        pool.wait_ge(idx_st, k + 1)
                        pool.wait_ge(g_free, k * TOPK + (j + 4))
                        nc.gpsimd.tensor_tensor(tok[:, :], tok[:, :], tok[:, :], ALU.add).then_inc(g_token, 1)
                    pool.indirect_dma_start(ring[:, j % NSLOT, :], None, table,
                                            bass.IndirectOffsetOnAxis(idxc[:, half, j:j + 1], 0)).then_inc(g_in[j % NSLOT], 16)

            for (kind, t, nb), k0 in zip(PHASES, STARTS):
                with pool.Fori(0, nb // 2) as i:
                    for half in range(2):
                        gathers(i * 2 + (k0 + half), half, u_tab if kind == "u" else v_tab)
            pool.wait_ge(fold_rd, 1)
            lows(80, 16)

        @block.scalar
        def _(act):
            A = nc.scalar.activation

            def hi(pc, slot):
                act.wait_ge(w_in_s[slot], (pc - slot) * 8 + 16)
                if not (isinstance(pc, int) and pc < 2):
                    act.wait_ge(w_used, pc - 1)
                A(whi[:, slot, :, :], raw[:, slot, :, :], ACT.Copy).then_inc(w_hi_ready, 1)

            def his(first, count):
                with act.Fori(0, count // 2) as i:
                    for slot in range(2):
                        hi(i * 2 + (first + slot), slot)

            def transposed_hi(use):
                for n in range(12):
                    t, g = divmod(n, 4)
                    c0, r = TILES[t]
                    act.wait_ge(tp_done, use * 12 + n + 1)
                    A(thi[:, 4 * g:4 * g + 4, c0:c0 + r],
                      PS[:, n % 8, :].rearrange("p (a c) -> p a c", a=4)[:, :, 0:r], ACT.Copy).then_inc(th_ready, 1)

            transposed_hi(0)
            act.wait_ge(small_T, 1)
            A(zbuf[:, :, Z0:ZW].rearrange("p f (b j) -> p f b j", b=NB)[:, :, :, 0:2],
              PS[:, 4, 0:128].rearrange("p (f b j) -> p f b j", f=8, b=NB), ACT.Copy).then_inc(small_ok, 1)
            act.wait_ge(small_T, 2)
            A(subT[:, :, :], PS[:, 5, 0:256].rearrange("p (a c) -> p a c", a=2), ACT.Copy).then_inc(small_ok, 1)
            hi(0, 0)
            hi(1, 1)
            his(2, 46)
            act.wait_ge(zl_T, 1)
            act.wait_ge(w_lo_ready, 48)
            A(zrows[:, :], PS[0:2 + 2 * NB, 0:2, :].rearrange("p a c -> p (a c)"), ACT.Copy).then_inc(zl_out, 1)
            act.wait_ge(conv_m, 1)
            A(thi[:, 8:16, TS:N], ubuf[:, :, 0:TP], ACT.Copy).then_inc(conv_hi, 1)
            for b in range(NB):
                A(thi[:, 8:16, b * NS:(b + 1) * NS], ubuf[:, :, Z0 + 10 * b:Z0 + 10 * b + NS], ACT.Copy).then_inc(conv_hi, 1)
            for j in range(16):
                act.wait_ge(qk_T, j + 1)
                dst = (qt, kt_)[j % 2]
                A(dst[:, j // 2, :], PS[:, 2 + j % 6, 0:N], ACT.Copy).then_inc(qk_ok, 1)
            for h in range(HEADS):
                e = h % 2
                act.wait_ge(s_neg, h + 1)
                A(psm[:, e, 0, :], psm[:, e, 0, :], ACT.Exp, bias=nmx[:, e, 0:1], scale=SCALE)
                A(psm[:, e, 1:3, :], psm[:, e, 1:3, :], ACT.Exp, bias=nmx[:, e, 1:2], scale=SCALE).then_inc(s_exp, 1)
                act.wait_ge(s_pT, h + 1)
                A(ppt[:, e, :, :].rearrange("p a c -> p (a c)"), PS[:, 2 + e, 0:384], ACT.Copy).then_inc(s_pok, 1)
            with act.Fori(0, NB) as b:
                for n in range(24):
                    act.wait_ge(kT_raw, b * 24 + (n + 1))
                    w = 4 * (GA if n < 16 else GB)
                    A(ktb[:, n % 2, 0:w], PS[:, 3 + n % 3, 0:w], ACT.Copy).then_inc(kT_ok, 1)
                act.wait_ge(d_neg, b + 1)
                A(ssm[:, :], ssm[:, :], ACT.Exp, bias=nmx[0:64, 0, 0:1], scale=SCALE).then_inc(d_exp, 1)
                act.wait_ge(d_pT, b + 1)
                A(pta[:, :, :].rearrange("p a c -> p (a c)"), PS[0:GA, 6, :], ACT.Copy)
                A(ptb[:, :, :].rearrange("p a c -> p (a c)"), PS[:, 7, 0:256], ACT.Copy)
                A(ptc[:, :], PS[0:TS, 7, 256:320], ACT.Copy).then_inc(d_pok, 1)

            def layer_norm_root(n):
                act.wait_ge(var_ok, n + 1)
                A(std[:, 0:1], vst_[:, :], ACT.Sqrt).then_inc(std_ok, 1)

            act.wait_ge(att_ok, 1)
            his(48, 16)
            for n in range(3):
                layer_norm_root(n)
            transposed_hi(1)
            his(64, 16)
            for n in range(12):
                act.wait_ge(sc_psum, n + 1)
                t, g = divmod(n, 4)
                r = TILES[(1, 2, 0)[t]][1]
                A(sc[0:r, (1, 2, 0)[t], 4 * g:4 * g + 4, :].rearrange("p a c -> p (a c)"),
                  PS[0:r, n % 8, :], ACT.Copy).then_inc(sc_ok, 1)
            for n, t in enumerate((1, 2, 0)):
                r = TILES[t][1]
                act.wait_ge(g_sub, n + 1)
                A(gates[0:r, t, :], gates[0:r, t, :], ACT.Exp).then_inc(g_exp, 1)
            for n, (t, w) in enumerate(((1, 128), (2, 128), (0, 64))):
                act.wait_ge(dots, n + 1)
                A(hdot[:, t, 0:w], hdot[:, t, 0:w], ACT.Gelu).then_inc(gelu_ok, 1)
            for n in range(3, 6):
                layer_norm_root(n)
            transposed_hi(2)
            for t in range(3):
                c0, r = TILES[t]
                act.wait_ge(pT_psum, t + 1)
                A(pT[:, :, c0:c0 + r], PS[:, 4 + t, 0:256].rearrange("p (a c) -> p a c", a=2)[:, :, 0:r], ACT.Copy).then_inc(pT_ok, 1)

            def sigmoids(c, bank):
                act.wait_ge(w_used, c * PPC + 84)
                if not (isinstance(c, int) and c == 0):
                    act.wait_ge(fin_ok, c)
                for t in range(3):
                    r = TILES[t][1]
                    m = A(gsig[0:r, t, :], PS[0:r, bank + t, :], ACT.Sigmoid)
                m.then_inc(sig_ok, 1)

            act.wait_ge(fold_rd, 1)
            for c in range(4):
                for k in range(PPC):
                    hi(80 + c * PPC + k, k % 2)
                    if k == 1 and c > 0:
                        sigmoids(c - 1, 4 * ((c - 1) % 2))
            sigmoids(3, 4)

        @block.vector
        def _(dve):
            V = nc.vector
            step = [0]

            def link(ins, base=None, inc=True):
                step[0] += 1
                ins.then_inc(dstep, 1)
                dve.wait_ge(dstep, step[0] if base is None else base + step[0])

            def transposed_lo(use):
                for n in range(12):
                    t, g = divmod(n, 4)
                    c0, r = TILES[t]
                    dve.wait_ge(th_ready, use * 12 + n + 1)
                    V.tensor_tensor(tlo[:, 4 * g:4 * g + 4, c0:c0 + r],
                                    PS[:, n % 8, :].rearrange("p (a c) -> p a c", a=4)[:, :, 0:r],
                                    thi[:, 4 * g:4 * g + 4, c0:c0 + r].bitcast(f32), ALU.subtract).then_inc(tl_ready, 1)

            def prompt_out(h):
                e = h % 2
                dve.wait_ge(s_pv, h + 1)
                link(V.tensor_scalar(thi[:, h, TS:N], PS[:, 4 + e, 0:TP], 1.0, None, ALU.mult))
                V.tensor_tensor(tlo[:, h, TS:N], PS[:, 4 + e, 0:TP], thi[:, h, TS:N].bitcast(f32), ALU.subtract).then_inc(s_po, 1)

            V.memset(zbuf[:, :, 0:2], 0.0).then_inc(z_pad, 1)
            transposed_lo(0)
            with dve.Fori(0, 3) as i:
                for h in range(2):
                    dve.wait_ge(w_used, i * 8 + 4 * (h + 1))
                    for t in range(3):
                        dst = (qkv_s[:, ds(i * DA + h * CW, CW)] if t == 0
                               else qkv_p[:, t - 1, ds(i * DA + h * CW, CW)])
                        m = V.tensor_scalar(dst, PS[0:TILES[t][1], 4 * h + t, :], 1.0, None, ALU.mult)
                    m.then_inc(acc_free, 1)
            dve.wait_ge(acc_free, 6)
            dve.wait_ge(c2_in, 160)
            for t in range(3):
                r = TILES[t][1]
                hd = 2 * HEADS
                src = (qkv_s[:, 0:2 * DA] if t == 0 else qkv_p[:, t - 1, 0:2 * DA]).rearrange("p (h d) -> p h d", h=hd)
                x1, x2 = src[:, :, 0:DH // 2], src[:, :, DH // 2:DH]
                cb = cosb[0:r, t, :].unsqueeze(1).broadcast_to([r, hd, DH // 2])
                sb_ = sinb[0:r, t, :].unsqueeze(1).broadcast_to([r, hd, DH // 2])
                tm = [rtmp[0:r, j, :].rearrange("p (h d) -> p h d", h=hd) for j in range(4)]
                for j, (a, b) in enumerate(((x1, cb), (x2, sb_), (x2, cb), (x1, sb_))):
                    m = V.tensor_tensor(tm[j], a, b, ALU.mult)
                link(m)
                V.tensor_tensor(x1, tm[0], tm[1], ALU.subtract)
                link(V.tensor_tensor(x2, tm[2], tm[3], ALU.add))
            V.memset(nmx[:, :, :], 0.0).then_inc(rope_ok, 1)
            for c in range(6, 8):
                dve.wait_ge(w_used, 4 * (c + 1))
                if c == 6:
                    dve.wait_ge(small_ok, 1)
                for j in range(4):
                    m = V.tensor_scalar(ubuf[:, 4 * (c - 6) + j, 0:N], PS[:, 4 * (c % 2) + j, 0:N], 1.0, None, ALU.mult)
                m.then_inc(acc_free, 1)
            dve.wait_ge(acc_free, 8)
            for c in range(8, 10):
                dve.wait_ge(w_used, 4 * (c + 1))
                for j in range(4):
                    f = 4 * (c - 8) + j
                    ps = PS[:, 4 * (c % 2) + j, :]
                    V.tensor_tensor(zbuf[:, f, 2:Z0], ps[:, TS:N], ubuf[:, f, TS:N], ALU.mult)
                    m = V.tensor_tensor(zbuf[:, f, Z0:ZW].rearrange("p (b j) -> p b j", b=NB)[:, :, 2:2 + NS],
                                        ps[:, 0:TS].rearrange("p (b s) -> p b s", b=NB),
                                        ubuf[:, f, 0:TS].rearrange("p (b s) -> p b s", b=NB), ALU.mult)
                m.then_inc(acc_free, 1)
            dve.wait_ge(acc_free, 10)
            V.tensor_copy(zl[:, :, 0:2], zbuf[:, :, TP:TP + 2])
            V.tensor_copy(zl[:, :, 2:2 + 2 * NB].rearrange("p f (b j) -> p f b j", b=NB),
                          zbuf[:, :, Z0:ZW].rearrange("p f (b j) -> p f b j", b=NB)[:, :, :, NS:NS + 2]).then_inc(zl_ready, 1)
            W2 = ZW - 2
            for j in range(3):
                for f in range(8):
                    o = ubuf[:, f, 0:W2]
                    if j == 0:
                        m = V.tensor_scalar(o, zbuf[:, f, 0:W2], cw[:, 0, f:f + 1], None, ALU.mult)
                    else:
                        m = V.scalar_tensor_tensor(out=o, in0=zbuf[:, f, j:j + W2], scalar=cw[:, j, f:f + 1], in1=o,
                                                   op0=ALU.mult, op1=ALU.add)
                link(m)
            for c in range(10, 12):
                dve.wait_ge(w_used, 4 * (c + 1))
                for j in range(4):
                    f = 4 * (c - 10) + j
                    ps = PS[:, 4 * (c % 2) + j, :]
                    V.tensor_tensor(ubuf[:, f, 0:TP], ps[:, TS:N], ubuf[:, f, 0:TP], ALU.mult)
                    o = ubuf[:, f, Z0:ZW].rearrange("p (b j) -> p b j", b=NB)[:, :, 0:NS]
                    m = V.tensor_tensor(o, ps[:, 0:TS].rearrange("p (b s) -> p b s", b=NB), o, ALU.mult)
                m.then_inc(acc_free, 1)
            dve.wait_ge(acc_free, 12)
            V.memset(rs[:, :], 0.0).then_inc(conv_m, 1)
            dve.wait_ge(conv_hi, 1 + NB)
            V.tensor_tensor(tlo[:, 8:16, TS:N], ubuf[:, :, 0:TP], thi[:, 8:16, TS:N].bitcast(f32), ALU.subtract)
            for b in range(NB):
                cc = slice(b * NS, (b + 1) * NS)
                m = V.tensor_tensor(tlo[:, 8:16, cc], ubuf[:, :, Z0 + 10 * b:Z0 + 10 * b + NS],
                                    thi[:, 8:16, cc].bitcast(f32), ALU.subtract)
            link(m)
            for h in range(HEADS):
                e = h % 2
                dve.wait_ge(s_score, h + 1)
                w = psm[:, e, :, :].rearrange("p a c -> p (a c)")
                link(V.tensor_tensor(w, PS[:, e, 0:384], mp_add[:, :], ALU.add))
                V.reduce_max(mx[:, 0:1], w[:, 0:128], AX)
                link(V.reduce_max(mx[:, 1:2], w[:, 128:384], AX))
                V.tensor_scalar(nmx[:, e, :], mx[:, 0:2], -SCALE, None, ALU.mult).then_inc(s_neg, 1)
                dve.wait_ge(s_exp, h + 1)
                for q, (a, b) in enumerate(((0, 128), (128, 384))):
                    m = V.scalar_tensor_tensor(out=w[:, a:b], in0=w[:, a:b], scalar=1.0, in1=mp_mul[:, a:b],
                                               op0=ALU.mult, op1=ALU.mult, accum_out=rs[:, q:q + 1])
                link(m)
                link(V.reciprocal(rs[:, 2:4], rs[:, 0:2]))
                V.tensor_scalar(w[:, 0:128], w[:, 0:128], rs[:, 2:3], None, ALU.mult)
                link(V.tensor_scalar(w[:, 128:384], w[:, 128:384], rs[:, 3:4], None, ALU.mult))
                V.memset(mx[:, 3:4], 0.0).then_inc(s_prob, 1)
                if h > 0:
                    prompt_out(h - 1)
            prompt_out(HEADS - 1)
            V.memset(qpad[:, :, :], 0.0).then_inc(dstep, 1)
            step[0] += 1
            dve.wait_ge(dstep, step[0])
            base0, PER = step[0], 12
            with dve.Fori(0, NB) as b:
                step[0] = base0
                ib = b * PER
                for h in range(1):
                    pass
                q_diag = qpad[:, :, :].rearrange("p h c -> p (h c)")
                for h in range(HEADS):
                    m = V.tensor_scalar(qpad[:, h, h * NS:(h + 1) * NS], qt[:, h, ds(b * NS, NS)], 1.0, None, ALU.mult)
                V.tensor_scalar(ms_add[:, GA * RA:GA * RA + TS], mc_add[:, ds(b, 1), :].rearrange("p a c -> p (a c)"), 1.0, None, ALU.mult)
                m = V.tensor_scalar(ms_mul[:, GA * RA:GA * RA + TS], mc_mul[:, ds(b, 1), :].rearrange("p a c -> p (a c)"), 1.0, None, ALU.mult)
                link(m, ib)
                V.memset(mx[:, 2:3], 0.0).then_inc(q_pad, 1)
                dve.wait_ge(d_score, b + 1)
                V.tensor_tensor(ssm[:, 0:480], PS[0:64, 0, 0:480], ms_add[:, 0:480], ALU.add)
                V.tensor_tensor(ssm[:, 480:832], PS[0:64, 1, 0:352], ms_add[:, 480:832], ALU.add)
                link(V.tensor_tensor(ssm[:, 832:SCOLS], PS[0:64, 2, :], ms_add[:, 832:SCOLS], ALU.add), ib)
                link(V.reduce_max(mx[0:64, 0:1], ssm[:, :], AX), ib)
                V.tensor_scalar(nmx[0:64, 0, 0:1], mx[0:64, 0:1], -SCALE, None, ALU.mult).then_inc(d_neg, 1)
                dve.wait_ge(d_exp, b + 1)
                link(V.scalar_tensor_tensor(out=ssm[:, :], in0=ssm[:, :], scalar=1.0, in1=ms_mul[:, :],
                                            op0=ALU.mult, op1=ALU.mult, accum_out=rs[0:64, 0:1]), ib)
                link(V.reciprocal(rs[0:64, 1:2], rs[0:64, 0:1]), ib)
                link(V.tensor_scalar(ssm[:, :], ssm[:, :], rs[0:64, 1:2], None, ALU.mult), ib)
                V.memset(mx[:, 3:4], 0.0).then_inc(d_prob, 1)
                dve.wait_ge(v_used, b + 1)
                o = PS[:, 7, 384:448].rearrange("p (h s) -> p h s", h=HEADS)
                hi_ = thi[:, 0:8, ds(b * NS, NS)]
                link(V.tensor_scalar(hi_, o, 1.0, None, ALU.mult), ib)
                link(V.tensor_tensor(tlo[:, 0:8, ds(b * NS, NS)], o, hi_.bitcast(f32), ALU.subtract), ib)
                for _ in range(4):
                    link(V.memset(mx[:, 2:3], 0.0), ib)
            step[0] = base0 + NB * PER
            V.memset(mx[:, 0:4], 0.0).then_inc(att_ok, 1)
            dve.wait_ge(x_in, 16 * 5)
            with dve.Fori(0, 2) as i:
                for h in range(2):
                    dve.wait_ge(w_used, i * 8 + (48 + 4 * (h + 1)))
                    for t in range(3):
                        o = xt[0:TILES[t][1], t, ds(i * (2 * CW) + h * CW, CW)]
                        m = V.scalar_tensor_tensor(out=o, in0=o, scalar=ALPHA, in1=PS[0:TILES[t][1], 4 * h + t, :],
                                                   op0=ALU.mult, op1=ALU.add)
                    m.then_inc(acc_free, 1)
            dve.wait_ge(acc_free, 16)

            def layer_norm(n, t, gb):
                r = TILES[t][1]
                x = xt[0:r, t, :]
                for c in range(4):
                    m = V.bn_stats(bst[0:r, c, :], x[:, c * 512:(c + 1) * 512])
                link(m)
                link(V.bn_aggr(mv[0:r, :], bst[0:r, :, :].rearrange("p a c -> p (a c)")))
                link(V.memset(vst_[:, :], 1.0))
                V.tensor_scalar(vst_[0:r, :], mv[0:r, 1:2], EPS, None, ALU.add).then_inc(var_ok, 1)
                dve.wait_ge(std_ok, n + 1)
                link(V.reciprocal(std[0:r, 1:2], std[0:r, 0:1]))
                link(V.tensor_scalar(x, x, mv[0:r, 0:1], std[0:r, 1:2], ALU.subtract, ALU.mult))
                link(V.tensor_tensor(x, x, gb[0:r, 0, :], ALU.mult))
                V.tensor_tensor(x, x, gb[0:r, 1, :], ALU.add).then_inc(ln_ok, 1)

            dve.wait_ge(ln1_in, 32)
            for n in range(3):
                layer_norm(n, n, ln1)
            transposed_lo(1)
            for c in range(4):
                dve.wait_ge(w_used, 64 + 4 * (c + 1))
                for j in range(4):
                    m = V.tensor_scalar(qpt[:, 4 * c + j, :], PS[:, 4 * (c % 2) + j, 0:N], 1.0, None, ALU.mult)
                m.then_inc(acc_free, 1)

            def top16(n, t):
                r = TILES[t][1]
                s = lambda f: sc[0:r, t, f, :]
                a8, b8 = slice(0, 8), slice(8, 16)
                for f in range(NF):
                    m = V.max(top[0:r, f, a8], s(f))
                link(m)
                for f in range(NF):
                    m = V.max_index(topi[0:r, f, a8], top[0:r, f, a8], s(f))
                link(m)
                for f in range(NF):
                    m = V.match_replace(s(f), top[0:r, f, a8], s(f), -3e38)
                link(m)
                for f in range(NF):
                    m = V.max(top[0:r, f, b8], s(f))
                link(m)
                for f in range(NF):
                    m = V.max_index(topi[0:r, f, b8], top[0:r, f, b8], s(f))
                link(m)
                V.tensor_copy(topf[0:r, :, :], topi[0:r, :, :])
                tv = top[0:r, :, :].rearrange("p (h q) k -> p h q k", q=2)
                full = [r, PH, TOPK, TOPK]
                link(V.tensor_tensor(cand[0:r, :, :, :], tv[:, :, 0, :].unsqueeze(3).broadcast_to(full),
                                     tv[:, :, 1, :].unsqueeze(2).broadcast_to(full), ALU.add))
                cf = lambda h: cand[0:r, h, :, :].rearrange("p a c -> p (a c)")
                for h in range(PH):
                    m = V.max(ctop[0:r, h, a8], cf(h))
                link(m)
                for h in range(PH):
                    m = V.max_index(cidx[0:r, h, a8], ctop[0:r, h, a8], cf(h))
                link(m)
                for h in range(PH):
                    m = V.match_replace(cf(h), ctop[0:r, h, a8], cf(h), -3e38)
                link(m)
                for h in range(PH):
                    m = V.max(ctop[0:r, h, b8], cf(h))
                link(m)
                for h in range(PH):
                    m = V.max_index(cidx[0:r, h, b8], ctop[0:r, h, b8], cf(h))
                link(m)
                g = gates[0:r, t, :].rearrange("p (h k) -> p h k", h=PH)
                V.tensor_tensor(g, ctop[0:r, :, :], ctop[0:r, :, 0:1].broadcast_to([r, PH, TOPK]),
                                ALU.subtract).then_inc(g_sub, 1)
                V.tensor_single_scalar(cint[0:r, 0, :, :], cidx[0:r, :, :], 4, ALU.logical_shift_right)
                link(V.tensor_single_scalar(cint[0:r, 1, :, :], cidx[0:r, :, :], 15, ALU.bitwise_and))
                link(V.tensor_copy(cflt[0:r, :, :, :], cint[0:r, :, :, :]))
                fv = topf[0:r, :, :].rearrange("p (h q) k -> p h q k", q=2)
                for q in range(2):
                    hv = hot[0:r, :, :, :]
                    link(V.tensor_tensor(hv, cflt[0:r, q, :, :].unsqueeze(3).broadcast_to(full),
                                         iota[0:r, :].unsqueeze(1).unsqueeze(1).broadcast_to(full), ALU.is_equal))
                    link(V.tensor_tensor(hv, hv, fv[:, :, q, :].unsqueeze(2).broadcast_to(full), ALU.mult))
                    link(V.tensor_reduce(esel[0:r, q, :, :], hv, AX, ALU.add))
                e1, e2 = (esel[0:r, q, :, :].rearrange("p h k -> p (h k)") for q in range(2))
                outs = ([idx_s[:, :, :].rearrange("p a c -> p (a c)")] if t == 0 else
                        [idx_all[:, s_ * TOPK:(s_ + 8) * TOPK] for s_, p in zip(STARTS, PHASES) if p[1] == t])
                for o in outs:
                    m = V.scalar_tensor_tensor(out=o, in0=e1, scalar=float(NK), in1=e2, op0=ALU.mult, op1=ALU.add)
                link(m)
                dve.wait_ge(g_exp, n + 1)
                link(V.tensor_reduce(ctop[0:r, :, 0], g, AX, ALU.add))
                link(V.reciprocal(ctop[0:r, :, 1], ctop[0:r, :, 0]))
                link(V.tensor_tensor(g, g, ctop[0:r, :, 1:2].broadcast_to([r, PH, TOPK]), ALU.mult))

            def stage(k, half, base=None):
                return V.tensor_scalar(idxc[:, half, :], idx_all[:, ds(k * TOPK, TOPK) if base is None else ds(base, TOPK)], 0, None, ALU.add)

            dve.wait_ge(sc_ok, 4)
            V.memset(idx_all[:, BLOCKS * TOPK:(BLOCKS + 1) * TOPK], 0)
            top16(0, 1)
            dve.wait_ge(sc_ok, 8)
            top16(1, 2)
            dve.wait_ge(sc_ok, 12)
            link(V.memset(yacc[:, :, :], 0.0))
            stage(0, 0).then_inc(idx_st, 1)
            V.memset(mx[:, 0:1], 0.0).then_inc(g_free, NSLOT)
            for n, ((kind, t, nb), k0) in enumerate(zip(PHASES, STARTS)):
                x = xt[:, t, :]
                y = yacc[:, t, :]
                if n == 2:
                    top16(2, 0)
                    V.memset(mx[:, 1:2], 0.0).then_inc(pack_rd, 1)
                if n == 3:
                    dve.wait_ge(pack_in, 16 * 6)
                if kind == "v":
                    m = [1, 2, 0].index(t)
                    dve.wait_ge(gelu_ok, m + 1)
                    w = 128 if t else 64
                    link(V.tensor_tensor(hdot[:, t, 0:w], hdot[:, t, 0:w], gates[:, t, 0:w], ALU.mult))
                if n == 2:
                    dve.wait_ge(pack_in, 16 * 6)
                base1, PER1 = step[0], 3
                with dve.Fori(0, nb // 2) as i:
                    step[0] = base1
                    ib = i * PER1
                    if kind == "v":
                        link(V.tensor_scalar(ablk[:, :], hdot[:, t, ds(i * 32, 32)], 1.0, None, ALU.mult), ib)
                    for half in range(2):
                        k = i * 2 + (k0 + half)
                        V.tensor_scalar(idxc[:, 1 - half, :], idx_all[:, ds(i * 32 + (k0 + half + 1) * TOPK, TOPK)], 0, None, ALU.add).then_inc(idx_st, 1)
                        for j in range(TOPK):
                            g = ring[:, j % NSLOT, :]
                            c = half * TOPK + j
                            dve.wait_ge(g_in[j % NSLOT], k * 32 + 16 * (j // NSLOT + 1))
                            if kind == "u":
                                V.scalar_tensor_tensor(out=g, in0=g, scalar=1.0, in1=x, op0=ALU.mult, op1=ALU.mult,
                                                       accum_out=hblk[:, c:c + 1]).then_inc(g_free, 1)
                            else:
                                dve.wait_ge(g_free, k * TOPK + (NSLOT + j))
                                V.scalar_tensor_tensor(out=y, in0=g, scalar=ablk[:, c:c + 1], in1=y,
                                                       op0=ALU.mult, op1=ALU.add).then_inc(g_free, 1)
                        dve.wait_ge(g_free, k * TOPK + (NSLOT + TOPK))
                    if kind == "u":
                        link(V.tensor_scalar(hdot[:, t, ds(i * 32, 32)], hblk[:, :], 1.0, None, ALU.mult), ib)
                    while step[0] < base1 + PER1:
                        link(V.memset(mx[:, 2:3], 0.0), ib)
                step[0] = base1 + PER1 * (nb // 2)
                if kind == "u":
                    V.memset(mx[:, 3:4], 0.0).then_inc(dots, 1)
            V.memset(mx[:, 0:1], 0.0).then_inc(fold_rd, 1)
            dve.wait_ge(ln2_in, 32)
            for n, t in enumerate((1, 2, 0)):
                r = TILES[t][1]
                if t == 0:
                    dve.wait_ge(fold_in, 16)
                    link(V.tensor_tensor(yacc[0:r, 0, :], yacc[0:r, 0, :], yhalf[:, :], ALU.add))
                link(V.scalar_tensor_tensor(out=xt[0:r, t, :], in0=xt[0:r, t, :], scalar=ALPHA, in1=yacc[0:r, t, :],
                                            op0=ALU.mult, op1=ALU.add))
                layer_norm(3 + n, t, ln2)
            transposed_lo(2)
            for c in range(4):
                for t in range(3):
                    n = c * 3 + t
                    r = TILES[t][1]
                    dve.wait_ge(ple_ps, n + 1)
                    V.tensor_scalar(pleo[0:r, t, c * CW:(c + 1) * CW], PS[0:r, n % 4, :], 1.0, None, ALU.mult).then_inc(ple_ok, 1)
            dve.wait_ge(ple_ok, 12)
            for c in range(4):
                dve.wait_ge(sig_ok, c + 1)
                cc = slice(c * CW, (c + 1) * CW)
                for t in range(3):
                    r = TILES[t][1]
                    m = V.tensor_tensor(gsig[0:r, t, :], gsig[0:r, t, :], pleo[0:r, t, cc], ALU.mult)
                link(m)
                for t in range(3):
                    r = TILES[t][1]
                    m = V.tensor_tensor(xt[0:r, t, cc], xt[0:r, t, cc], gsig[0:r, t, :], ALU.add)
                m.then_inc(fin_ok, 1)

        @block.tensor
        def _(pe):
            MM, TR = nc.tensor.matmul, nc.tensor.transpose

            def transposes(use):
                for n in range(12):
                    t, g = divmod(n, 4)
                    r = TILES[t][1]
                    if n >= 8:
                        pe.wait_ge(tl_ready, use * 12 + n - 7)
                    for j in range(4):
                        m = TR(PS[:, n % 8, 128 * j:128 * j + r], xt[0:r, t, (4 * g + j) * 128:(4 * g + j + 1) * 128],
                               ident[0:r, 0:r])
                    m.then_inc(tp_done, 1)

            def split_mm(out, lhs, rhs, start, stop):
                (lh, ll), (rh, rl) = lhs, rhs
                MM(out, lh, rh, start=start, stop=False)
                MM(out, lh, rl, start=False, stop=False)
                return MM(out, ll, rh, start=False, stop=stop)

            def token_piece(pc, k, bank):
                pe.wait_ge(w_lo_ready, pc + 1)
                s = k % 2
                for kk in range(KP):
                    q = k * KP + kk
                    for t in range(3):
                        c0 = TILES[t][0]
                        m = split_mm(PS[:, bank + t, :], (thi[:, q, c0:c0 + 128], tlo[:, q, c0:c0 + 128]),
                                     (whi[:, s, kk, :], wlo[:, s, kk, :]), q == 0, q == KT - 1)
                m.then_inc(w_used, 1)

            def feature_piece(pc, k, bank):
                pe.wait_ge(w_lo_ready, pc + 1)
                s = k % 2
                for kk in range(KP):
                    q = k * KP + kk
                    for j in range(4):
                        cc = slice(j * 128, (j + 1) * 128)
                        m = split_mm(PS[:, bank + j, 0:N], (whi[:, s, kk, cc], wlo[:, s, kk, cc]),
                                     (thi[:, q, :], tlo[:, q, :]), q == 0, q == KT - 1)
                m.then_inc(w_used, 1)

            def chunks(piece, cc0, pairs, free0):
                with pe.Fori(0, pairs) as i:
                    for h in range(2):
                        for k in range(PPC):
                            if k == 0 and free0:
                                pe.wait_ge(acc_free, i * 2 + (cc0 + h - 1))
                            piece(i * 8 + (cc0 * 4 + h * 4 + k), k, 4 * h)

            pe.wait_ge(x_in, 48)
            transposes(0)
            pe.wait_ge(c_in, 32)
            pe.wait_ge(tl_ready, 5)
            for f in range(8):
                m = TR(PS[:, 4, f * 16:(f + 1) * 16], crow[:, f * 128:(f + 1) * 128], ident[0:16, 0:16])
            m.then_inc(small_T, 1)
            pe.wait_ge(tl_ready, 6)
            for q in range(2):
                m = TR(PS[:, 5, q * 128:(q + 1) * 128], subn[:, q, :], ident[:, :])
            m.then_inc(small_T, 1)
            pe.wait_ge(tl_ready, 12)
            pe.wait_ge(small_ok, 2)
            for h in range(2):
                for k in range(PPC):
                    token_piece(h * 4 + k, k, 4 * h)
            chunks(token_piece, 2, 2, True)
            chunks(feature_piece, 6, 3, True)
            pe.wait_ge(acc_free, 12)
            pe.wait_ge(zl_ready, 1)
            for f in range(8):
                m = TR(PS[0:18, f // 4, (f % 4) * 128:(f % 4 + 1) * 128], zl[:, f, :], ident[:, :])
            m.then_inc(zl_T, 1)
            for j in range(16):
                if j >= 6:
                    pe.wait_ge(qk_ok, j - 5)
                col = (j % 2) * DA + (j // 2) * DH
                for t in range(3):
                    c0, r = TILES[t]
                    src = qkv_s[:, col:col + DH] if t == 0 else qkv_p[:, t - 1, col:col + DH]
                    m = TR(PS[:, 2 + j % 6, c0:c0 + r], src, ident[0:r, 0:r])
                m.then_inc(qk_T, 1)
            pe.wait_ge(qk_ok, 16)
            pe.wait_ge(zl_out, 1)

            def prompt_scores(h):
                e = h % 2
                for t in range(2):
                    m = MM(PS[:, e, 128 * t:128 * t + 128 * (t + 1)], qt[:, h, TS + 128 * t:TS + 128 * (t + 1)],
                           kt_[:, h, TS:TS + 128 * (t + 1)], start=True, stop=True)
                m.then_inc(s_score, 1)

            prompt_scores(0)
            prompt_scores(1)
            for h in range(HEADS):
                e = h % 2
                pe.wait_ge(s_prob, h + 1)
                for a in range(3):
                    m = TR(PS[:, 2 + e, a * 128:(a + 1) * 128], psm[:, e, a, :], ident[:, :])
                m.then_inc(s_pT, 1)
                if h + 2 < HEADS:
                    prompt_scores(h + 2)
                pe.wait_ge(s_pok, h + 1)
                if h >= 2:
                    pe.wait_ge(s_po, h - 1)
                vals = lambda t: qkv_p[:, t, 2 * DA + h * DH:2 * DA + (h + 1) * DH]
                MM(PS[:, 4 + e, 0:128], vals(0), ppt[:, e, 0, :], start=True, stop=True)
                MM(PS[:, 4 + e, 128:256], vals(0), ppt[:, e, 1, :], start=True, stop=False)
                MM(PS[:, 4 + e, 128:256], vals(1), ppt[:, e, 2, :], start=False, stop=True).then_inc(s_pv, 1)
            pe.wait_ge(s_po, HEADS)
            with pe.Fori(0, NB) as b:
                pe.wait_ge(k_in, b * 32 + 32)
                src = lambda n, j: (ka[:, n // 2, ((n % 2) * 4 + j) * DH:((n % 2) * 4 + j + 1) * DH] if n < 16
                                    else kb[:, (n - 16) // 2, ((n % 2) * 4 + j) * DH:((n % 2) * 4 + j + 1) * DH])

                def key_transposes(n):
                    w = GA if n < 16 else GB
                    for j in range(4):
                        m = TR(PS[:, 3 + n % 3, j * w:(j + 1) * w], src(n, j), ident[0:w, 0:w])
                    m.then_inc(kT_raw, 1)
                    return m

                def key_scores(n):
                    w = GA if n < 16 else GB
                    if n < 16:
                        r = n // 2
                        o = PS[0:64, 0, r * GA:(r + 1) * GA] if r < 5 else PS[0:64, 1, (r - 5) * GA:(r - 4) * GA]
                    else:
                        r = (n - 16) // 2
                        o = PS[0:64, 2, r * GB:(r + 1) * GB]
                    for j in range(4):
                        h = (n % 2) * 4 + j
                        m = MM(o, qpad[:, h, :], ktb[:, n % 2, j * w:(j + 1) * w], start=(h == 0), stop=(h == 7))
                    return m

                key_transposes(0)
                key_transposes(1)
                pe.wait_ge(q_pad, b + 1)
                for n in range(24):
                    pe.wait_ge(kT_ok, b * 24 + (n + 1))
                    key_scores(n)
                    if n + 2 < 24:
                        key_transposes(n + 2)
                    elif n == 22:
                        pass
                for h in range(HEADS):
                    m = MM(PS[0:64, 1, 288:352], qpad[:, h, :], kt_[:, h, 0:TS], start=(h == 0), stop=(h == 7))
                m.then_inc(d_score, 1)
                pe.wait_ge(d_prob, b + 1)
                MM(PS[0:GA, 6, 0:64], ssm[:, 0:GA], ident[0:64, 0:64], start=True, stop=True)
                for r in range(1, RA):
                    TR(PS[0:GA, 6, r * 64:(r + 1) * 64], ssm[:, r * GA:(r + 1) * GA], ident[0:64, 0:64])
                for r in range(RB):
                    TR(PS[:, 7, r * 64:(r + 1) * 64], ssm[:, 832 + r * GB:832 + (r + 1) * GB], ident[0:64, 0:64])
                TR(PS[0:TS, 7, 256:320], ssm[:, 768:832], ident[0:64, 0:64]).then_inc(d_pT, 1)
                pe.wait_ge(d_pok, b + 1)
                pe.wait_ge(v_in, b * 32 + 32)
                for h in range(HEADS):
                    hc = slice(h * DH, (h + 1) * DH)
                    o = PS[:, 7, 384 + h * NS:384 + (h + 1) * NS]
                    qc = slice(h * NS, (h + 1) * NS)
                    for r in range(RA):
                        MM(o, va[:, r, hc], pta[:, r, qc], start=(r == 0), stop=False)
                    for r in range(RB):
                        MM(o, vb[:, r, hc], ptb[:, r, qc], start=False, stop=False)
                    m = MM(o, qkv_s[:, 2 * DA + h * DH:2 * DA + (h + 1) * DH], ptc[:, qc], start=False, stop=True)
                m.then_inc(v_used, 1)
            pe.wait_ge(att_ok, 1)
            for h in range(2):
                for k in range(PPC):
                    token_piece(48 + h * 4 + k, k, 4 * h)
            for h in range(2):
                pe.wait_ge(acc_free, 13 + h)
                for k in range(PPC):
                    token_piece(56 + h * 4 + k, k, 4 * h)
            pe.wait_ge(ln_ok, 3)
            transposes(1)
            pe.wait_ge(tl_ready, 24)
            chunks(feature_piece, 16, 2, True)
            pe.wait_ge(acc_free, 20)
            for n in range(12):
                t, g = divmod(n, 4)
                c0, r = TILES[(1, 2, 0)[t]]
                if n >= 8:
                    pe.wait_ge(sc_ok, n - 7)
                for j in range(4):
                    f = 4 * g + j
                    m = MM(PS[0:r, n % 8, j * 128:(j + 1) * 128], qpt[:, f, c0:c0 + r], subT[:, f % 2, :],
                           start=True, stop=True)
                m.then_inc(sc_psum, 1)
            pe.wait_ge(ln_ok, 6)
            pe.wait_ge(sc_ok, 12)
            transposes(2)
            pe.wait_ge(ple_in, 48)
            pe.wait_ge(tl_ready, 36)
            for t in range(3):
                r = TILES[t][1]
                for q in range(2):
                    m = TR(PS[:, 4 + t, q * 128:q * 128 + r], pnat[0:r, t, q * 128:(q + 1) * 128], ident[0:r, 0:r])
                m.then_inc(pT_psum, 1)
            pe.wait_ge(pT_ok, 3)
            for n in range(12):
                c, t = divmod(n, 3)
                c0, r = TILES[t]
                if n >= 4:
                    pe.wait_ge(ple_ok, n - 3)
                for q in range(2):
                    m = MM(PS[0:r, n % 4, :], pT[:, q, c0:c0 + r], plew[:, q, c * CW:(c + 1) * CW],
                           start=(q == 0), stop=(q == 1))
                m.then_inc(ple_ps, 1)
            pe.wait_ge(ple_ok, 12)
            for c in range(4):
                if c >= 2:
                    pe.wait_ge(sig_ok, c - 1)
                for k in range(PPC):
                    token_piece(80 + c * 4 + k, k, 4 * (c % 2))


def _rope_tables():
    import numpy as np
    half = DH // 2
    inv = np.float32(10000.0) ** (-np.arange(half, dtype=np.float32) / np.float32(half))
    cos, sin = (np.zeros((128, 3, half), np.float32) for _ in range(2))
    pos = np.zeros((128, 3), np.float32)
    pos[:TS, 0] = PAST + np.arange(TS) % NS
    pos[:, 1] = np.arange(128)
    pos[:, 2] = 128 + np.arange(128)
    ang = (pos[:, :, None] * inv[None, None, :]).astype(np.float32)
    cos[...] = np.cos(ang)
    sin[...] = np.sin(ang)
    return cos, sin


def _branches(dist, ok=True):
    n = 0
    for w, d in ((128, 1), (512, 4), (2048, 16)):
        n = n + ((dist >= 0) & (dist <= w) & (dist % d == 0) & ok).astype(int)
    return n


def _masks():
    import numpy as np
    q, k = np.arange(128)[:, None], np.arange(128)[None, :]
    prompt = np.concatenate([_branches(q - k), _branches(128 + q - k), _branches(q - k)], 1)
    s = (np.arange(64) % NS)[:, None]
    r, g = np.divmod(np.arange(RA * GA), GA)
    old = _branches(PAST + s - (16 * g + r)[None, :])
    r, g = np.divmod(np.arange(RB * GB), GB)
    last = _branches(PAST + s - (OLD + RB * g + r)[None, :])
    decode = np.concatenate([old, np.zeros((64, TS), int), last], 1)
    b = np.arange(NB)[None, :, None]
    c = np.arange(TS)[None, None, :]
    new = _branches(s[:, :, None] - c % NS, c // NS == b)
    out = []
    for m in (prompt, decode, new):
        out += [np.where(m > 0, 0.0, -1e30).astype(np.dtype("bfloat16")), m.astype(np.dtype("bfloat16"))]
    return out


_INS = ["x_prompt", "x_sample", "state_attn_k", "state_attn_v", "state_conv", "p_prompt", "p_sample",
        "w_in", "w_conv", "w_out", "ln1_g", "ln1_b", "peer_wq", "peer_subkeys", "peer_u", "peer_v",
        "ln2_g", "ln2_b", "ple_gate", "ple_proj"]
_OUTS = [(1, TP, D), (NB, NS, D), (1, 1, TP, HEADS, DH), (1, 1, TP, HEADS, DH), (1, 1, 2, DC),
         (1, NB, PAST, HEADS, DH), (1, NB, PAST, HEADS, DH), (1, NB, 2, DC)]


def kernel(**inputs):
    import numpy as _np
    import concourse.bacc as _bacc
    from concourse import mybir as _mybir
    from concourse.bass_utils import run_bass_kernel_spmd as _run

    nc = _bacc.Bacc("TRN2", target_bir_lowering=False, num_devices=1)
    arrays, args = {}, []

    def give(name, a):
        a = _np.ascontiguousarray(a)
        arrays[name] = a
        args.append(nc.dram_tensor(name, a.shape, _mybir.dt.from_np(a.dtype), kind="ExternalInput").ap())

    for name in _INS:
        give(f"in_{name}", inputs[name])
    cos, sin = _rope_tables()
    consts = [_np.eye(128, dtype=_np.float32), cos, sin, *_masks(),
              _np.tile(_np.arange(TOPK, dtype=_np.float32), (128, 1))]
    for i, a in enumerate(consts):
        give(f"const_{i}", a)
    for i, shape in enumerate(_OUTS):
        args.append(nc.dram_tensor(f"out_{i}", shape, _mybir.dt.float32, kind="ExternalOutput").ap())
    decoder_step(nc, *args)
    r = _run(nc, [arrays], core_ids=[0])
    return tuple(r.results[0][f"out_{i}"] for i in range(len(_OUTS)))
```

```python
import concourse.bass as bass
from concourse import mybir
from contextlib import ExitStack

D = 2048
HEADS, DH = 8, 128
DA = HEADS * DH
DC = D - DA
TP, NB, NS = 256, 8, 8
TS = NB * NS
N = TS + TP
PAST = 2048
KT = D // 128
SCALE = float(DH) ** -0.5
ALPHA = 2.0 ** 0.25
EPS = 1e-5
TILES = [(0, TS), (TS, 128), (TS + 128, 128)]
PH, NK, TOPK = 8, 128, 16
NF = 2 * PH
PLE = 256
CW = 512
KP = 4
PPC = KT // KP
GA, RA = 96, 8
OLD = 16 * GA
GB, RB = 128, 4
K_PARTS = (8, 16, 24)
SCOLS = GA * RA + TS + GB * RB
ZW = 2 + TP + NB * (2 + NS)
Z0 = 2 + TP
NSLOT = 8
PHASES = [("u", 1, 8), ("u", 2, 8), ("v", 1, 8), ("u", 0, 4), ("v", 2, 8), ("v", 0, 4)]
STARTS = [sum(p[2] for p in PHASES[:n]) for n in range(len(PHASES))]
BLOCKS = sum(p[2] for p in PHASES)


def decoder_step(nc, x_p, x_s, st_k, st_v, st_c, p_p, p_s, w_in, w_conv, w_out, ln1_g, ln1_b,
                 wq, subkeys, peer_u, peer_v, ln2_g, ln2_b, w_gate, w_ple,
                 c_ident, c_cos, c_sin, c_mp_add, c_mp_mul, c_ms_add, c_ms_mul, c_mc_add, c_mc_mul,
                 c_iota,
                 y_p, y_s, o_kp, o_vp, o_cp, o_ks, o_vs, o_cs):
    f32, f32r, bf16, u32, i32 = (mybir.dt.float32, mybir.dt.float32r, mybir.dt.bfloat16,
                                 mybir.dt.uint32, mybir.dt.int32)
    ALU = mybir.AluOpType
    ACT = mybir.ActivationFunctionType
    AX = mybir.AxisListType.X
    ds = bass.ds
    KB = 1024

    xp_v = x_p.rearrange("a (t p) d -> p (a t) d", p=128)
    xs_v = x_s.rearrange("b s d -> (b s) d")
    pp_v = p_p.rearrange("a b (t p) d -> p (a b t) d", p=128)
    ps_v = p_s.rearrange("a b s d -> (a b s) d")
    kst = st_k.rearrange("a b n h d -> (a b) n (h d)")
    vst = st_v.rearrange("a b n h d -> (a b) n (h d)")
    oks = o_ks.rearrange("a b n h d -> (a b) n (h d)")
    ovs = o_vs.rearrange("a b n h d -> (a b) n (h d)")
    okp = o_kp.rearrange("a b (t p) h d -> p (a b t) (h d)", p=128)
    ovp = o_vp.rearrange("a b (t p) h d -> p (a b t) (h d)", p=128)
    wiew = lambda w: w.rearrange("a (k p) e -> p (a k) e", p=128)
    win_v, wout_v, wq_v, wg_v, wple_v = map(wiew, (w_in, w_out, wq, w_gate, w_ple))
    u_tab = peer_u.rearrange("a n d -> (a n) d")
    v_tab = peer_v.rearrange("a n d -> (a n) d")
    yp_v = y_p.rearrange("a (t p) d -> p (a t) d", p=128)
    ys_v = y_s.rearrange("b s d -> (b s) d")

    BASE = 16512
    used = []

    def at(name, shape, dt, off):
        used.append(name)
        return nc.alloc_sbuf_tensor_at(name, shape, dt, offset=BASE + off)

    raw = at("w_raw", [128, 2, KP, CW], f32, 0)
    whi = at("w_hi", [128, 2, KP, CW], f32r, 16 * KB)
    wlo = at("w_lo", [128, 2, KP, CW], f32r, 32 * KB)
    ka = at("keys_old", [GA, RA, DA], f32, 0)
    kb = at("keys_last", [GB, RB, DA], f32, 32 * KB)
    zrows = at("conv_rows_out", [2 + 2 * NB, DC], f32, 0)
    sc = at("peer_scores", [128, 3, NF, NK], f32, 0)
    cand = at("candidates", [128, PH, TOPK, TOPK], f32, 24 * KB)
    hot = at("one_hot", [128, PH, TOPK, TOPK], f32, 32 * KB)

    qkv_p = at("qkv_prompt", [128, 2, 3 * DA], f32, 48 * KB)
    ubuf = at("conv_u", [128, 8, ZW], f32, 72 * KB)
    zbuf = at("conv_z", [128, 8, ZW], f32, 72 * KB + 8 * ZW * 4)
    crow = at("conv_state_rows", [2 * NB, DC], f32, 72 * KB)
    va = at("values_old", [GA, RA, DA], f32, 48 * KB)
    vb = at("values_last", [GB, RB, DA], f32, 80 * KB)
    ln1 = at("ln1_gain_bias", [128, 2, D], f32, 48 * KB)
    qpt = at("peer_queries", [128, NF, N], f32, 64 * KB)
    ring = at("expert_rows", [128, NSLOT, D], f32, 48 * KB)
    plew = at("ple_weights", [128, 2, D], f32, 96 * KB)
    pleo = at("ple_out", [128, 3, D], f32, 48 * KB)
    gsig = at("gate_sigmoid", [128, 3, CW], f32, 72 * KB)

    qkv_s = at("qkv_decode", [TS, 3 * DA], f32, 96 * KB)
    qt = at("q_T", [128, HEADS, N], f32, 108 * KB)
    kt_ = at("k_T", [128, HEADS, N], f32, 118 * KB)
    ln2 = at("ln2_gain_bias", [128, 2, D], f32, 112 * KB)

    xt = at("x_tokens", [128, 3, D], f32, 128 * KB)
    rtmp = at("rope_products", [128, 4, DA], f32, 128 * KB)
    psm = at("prompt_scores", [128, 2, 3, 128], f32, 144 * KB)
    ppt = at("prompt_probs_T", [128, 2, 3, 128], f32, 147 * KB)
    ktb = at("old_k_T", [128, 2, 512], f32, 128 * KB)
    ssm = at("decode_scores", [64, SCOLS], f32, 132 * KB)
    pta = at("probs_T_old", [GA, RA, 64], f32, 138 * KB)
    ptb = at("probs_T_last", [GB, RB, 64], f32, 140 * KB)
    ptc = at("probs_T_new", [TS, 64], f32, 141 * KB)
    qpad = at("q_padded", [128, HEADS, 64], f32, 142 * KB)
    osb = at("decode_out", [128, 2 * DH], f32, 144 * KB)

    thi = at("act_T_hi", [128, KT, N], f32r, 152 * KB)
    tlo = at("act_T_lo", [128, KT, N], f32r, 172 * KB)
    yacc = at("expert_sums", [128, 3, D], f32, 152 * KB)
    yhalf = at("expert_sums_half", [TS, D], f32, 176 * KB)
    S0 = 184 * KB
    top = at("top_values", [128, NF, TOPK], f32, S0)
    topi = at("top_keys", [128, NF, TOPK], u32, S0 + 1 * KB)
    topf = at("top_keys_f", [128, NF, TOPK], f32, S0 + 2 * KB)
    ctop = at("cand_top", [128, PH, TOPK], f32, S0 + 3 * KB)
    cidx = at("cand_index", [128, PH, TOPK], u32, S0 + 3 * KB + 512)
    cint = at("cand_rank_int", [128, 2, PH, TOPK], u32, S0 + 4 * KB)
    cflt = at("cand_rank", [128, 2, PH, TOPK], f32, S0 + 5 * KB)
    esel = at("expert_part", [128, 2, PH, TOPK], f32, S0 + 6 * KB)

    M0 = 192 * KB
    off = [M0]

    def small(name, shape, dt, size):
        n = size
        for s in shape[1:]:
            n *= s
        t = at(name, shape, dt, off[0])
        off[0] += (n + 31) // 32 * 32
        return t

    ident = small("identity", [128, 128], f32, 4)
    subT = small("subkeys_T", [128, 2, NK], f32, 4)
    cosb = small("rope_cos", [128, 3, DH // 2], f32, 4)
    sinb = small("rope_sin", [128, 3, DH // 2], f32, 4)
    cw = small("conv_weights", [128, 3, 8], f32, 4)
    mx = small("row_max", [128, 4], f32, 4)
    nmx = small("neg_row_max", [128, 2, 2], f32, 4)
    rs = small("row_sum", [128, 4], f32, 4)
    bst = small("ln_stats", [128, 4, 6], f32, 4)
    mv = small("ln_mean_var", [128, 2], f32, 4)
    vst_ = small("ln_var_eps", [128, 1], f32, 4)
    std = small("ln_std", [128, 2], f32, 4)
    iota = small("iota16", [128, TOPK], f32, 4)
    tok = small("pool_token", [128, 1], f32, 4)
    idxc = small("block_experts", [128, 2, TOPK], u32, 4)
    hblk = small("block_dots", [128, 2 * TOPK], f32, 4)
    ablk = small("block_gates", [128, 2 * TOPK], f32, 4)
    zl = small("conv_last_rows_T", [128, 8, 2 + 2 * NB], f32, 4)
    mp_add = small("prompt_mask_add", [128, 384], bf16, 2)
    mp_mul = small("prompt_mask_mul", [128, 384], bf16, 2)
    shared = off[0]
    ms_add = small("decode_mask_add", [64, SCOLS], bf16, 2)
    ms_mul = small("decode_mask_mul", [64, SCOLS], bf16, 2)
    mc_add = small("new_mask_add", [64, NB, TS], bf16, 2)
    mc_mul = small("new_mask_mul", [64, NB, TS], bf16, 2)
    assert BASE + off[0] <= 229344, off[0]
    end_masks = off[0]
    off[0] = shared
    idx_all = small("experts", [128, (BLOCKS + 1) * TOPK], u32, 4)
    idx_s = small("experts_decode", [64, 2, 64], u32, 4)
    gates = small("gates", [128, 3, 128], f32, 4)
    hdot = small("dots", [128, 3, 128], f32, 4)
    assert off[0] <= end_masks
    pnat = at("ple_tokens", [128, 3, PLE], f32, 80 * KB)
    pT = at("ple_T", [128, 2, N], f32, 84 * KB)
    subn = at("subkeys_rows", [128, 2, 128], f32, 76 * KB + 512)

    ctx = ExitStack()
    with ctx:
        PS = ctx.enter_context(nc.psum_tensor("psum", [128, 8, 512], f32))
        sem = lambda name: ctx.enter_context(nc.semaphore(name))
        x_in, c_in, c2_in = sem("x_in"), sem("consts_in"), sem("late_consts_in")
        w_in_s = [sem("w_slot0_in"), sem("w_slot1_in")]
        w_hi_ready, w_lo_ready, w_used = sem("w_hi_ready"), sem("w_lo_ready"), sem("w_used")
        acc_free = sem("acc_free")
        tp_done, th_ready, tl_ready = sem("transposed"), sem("t_hi_ready"), sem("t_lo_ready")
        small_T, small_ok = sem("small_transposed"), sem("small_copied")
        dstep = sem("dve_step")
        z_pad = sem("z_pad_set")
        rope_ok = sem("rope_done")
        zl_ready, zl_T, zl_out = sem("conv_rows_ready"), sem("conv_rows_T"), sem("conv_rows_copied")
        conv_m, conv_hi = sem("conv_ready"), sem("conv_hi_ready")
        qk_T, qk_ok = sem("qk_transposed"), sem("qk_copied")
        s_score, s_neg, s_exp, s_prob = sem("p_scores"), sem("p_negmax"), sem("p_exp"), sem("p_probs")
        s_pT, s_pok, s_pv, s_po = sem("p_probs_T"), sem("p_probs_T_ok"), sem("p_out"), sem("p_out_copied")
        k_in = [sem(f"keys_part{i}_in") for i in range(3)]
        v_in, v_used = sem("values_in"), sem("values_used")
        q_pad, kT_raw, kT_ok = sem("q_pad_ready"), sem("old_kT_psum"), sem("old_kT_copied")
        d_score, d_neg, d_exp, d_prob = sem("d_scores"), sem("d_negmax"), sem("d_exp"), sem("d_probs")
        d_pT, d_pok = sem("d_probs_T"), sem("d_probs_T_ok")
        d_out, d_oT, d_oread = sem("d_out_copied"), sem("d_out_T"), sem("d_out_T_read")
        att_ok = sem("decode_att_done")
        var_ok, std_ok = sem("ln_var_ready"), sem("ln_std_ready")
        ln_ok = sem("ln_done")
        ln1_in, ln2_in = sem("ln1_in"), sem("ln2_in")
        sc_psum, sc_ok = sem("scores_psum"), sem("scores_copied")
        g_sub, g_exp = sem("gate_logits"), sem("gate_exp")
        g_free, g_token = sem("ring_free"), sem("pool_token_done")
        g_in = [sem(f"row_slot{i}_in") for i in range(NSLOT)]
        idx_st = sem("block_staged")
        dots, gelu_ok = sem("dots_ready"), sem("gelu_ready")
        pack_rd, pack_in = sem("pack_ready"), sem("packed_in")
        fold_rd, fold_in = sem("fold_ready"), sem("folded_in")
        ring_done = sem("ring_done")
        ple_in, pT_psum, pT_ok, ple_ps, ple_ok = (sem("ple_in"), sem("ple_T_psum"), sem("ple_T_ok"),
                                                  sem("ple_psum"), sem("ple_copied"))
        sig_ok, fin_ok = sem("sigmoid_ready"), sem("final_ready")
        out_s, kvcopy = sem("outputs_written"), sem("cache_copied")
        zrow_s = sem("conv_rows_written")

        def rows_of(buf, t):
            return buf[0:TILES[t][1], t, :]

        block = ctx.enter_context(nc.Block())

        @block.sync
        def _(sp):
            copies = [0]

            def copy_part(src, dst, b, j):
                n = (PAST - NS) * DA // 128
                s = src[b, NS:PAST, :] if isinstance(b, int) else src[ds(b, 1), NS:PAST, :].rearrange("a n d -> (a n) d")
                o = dst[b, 0:PAST - NS, :] if isinstance(b, int) else dst[ds(b, 1), 0:PAST - NS, :].rearrange("a n d -> (a n) d")
                s = s.rearrange("n d -> (n d)").rearrange("(p m) -> p m", m=n)
                o = o.rearrange("n d -> (n d)").rearrange("(p m) -> p m", m=n)
                sp.dma_start(o[16 * j:16 * j + 16, :], s[16 * j:16 * j + 16, :]).then_inc(kvcopy, 16)

            def copy_batch(src, dst, b):
                for j in range(8):
                    copy_part(src, dst, b, j)

            def load_piece(view, cols, pc, k):
                slot = k % 2
                if not (isinstance(pc, int) and pc < 2):
                    sp.wait_ge(w_lo_ready, pc - 1)
                sp.dma_start(raw[:, slot, :, :], view[:, k * KP:(k + 1) * KP, cols]).then_inc(w_in_s[slot], 16)

            def load_chunks(view, col0, pc0, pairs, src=None, dst=None, b0=0, peel=False, skip=0):
                if peel or skip:
                    for h in range(2):
                        for k in range(PPC):
                            if h * PPC + k >= skip:
                                load_piece(view, slice(col0 + h * CW, col0 + (h + 1) * CW), pc0 + h * PPC + k, k)
                            if src is not None:
                                copy_part(src, dst, b0, PPC * h + k)
                    col0, pc0, b0, pairs = col0 + 2 * CW, pc0 + 2 * PPC, b0 + 1, pairs - 1
                if pairs == 1:
                    for h in range(2):
                        for k in range(PPC):
                            load_piece(view, slice(col0 + h * CW, col0 + (h + 1) * CW), pc0 + h * PPC + k, k)
                            if src is not None:
                                copy_part(src, dst, b0, PPC * h + k)
                    return
                with sp.Fori(0, pairs) as i:
                    for h in range(2):
                        for k in range(PPC):
                            load_piece(view, ds(i * (2 * CW) + (col0 + h * CW), CW),
                                       i * (2 * PPC) + (pc0 + h * PPC + k), k)
                            if src is not None:
                                copy_part(src, dst, i + b0, PPC * h + k)

            sp.dma_start(ident[:, :], c_ident).then_inc(x_in, 16)
            sp.dma_start(xt[:, 1:3, :], xp_v).then_inc(x_in, 16)
            sp.dma_start(xt[0:TS, 0, :], xs_v).then_inc(x_in, 16)
            sp.dma_start(crow[:, :], st_c.rearrange("a b j d -> (a b j) d")).then_inc(c_in, 16)
            sp.dma_start(subn[:, :, :], subkeys.rearrange("a q k c -> k (a q) c")).then_inc(c_in, 16)
            for dst, src in ((cosb, c_cos), (sinb, c_sin), (mp_add, c_mp_add), (mp_mul, c_mp_mul),
                             (ms_add, c_ms_add), (ms_mul, c_ms_mul), (mc_add, c_mc_add),
                             (mc_mul, c_mc_mul), (iota, c_iota)):
                sp.dma_start(dst[...], src).then_inc(c2_in, 16)
            with nc.allow_non_contiguous_dma(reason="3072 weights, once"):
                sp.dma_start(cw[:, :, :], w_conv.rearrange("a j (f p) -> p (a j) f", p=128)).then_inc(c2_in, 16)
            load_chunks(win_v, 0, 0, 3, kst, oks, 0, peel=True)
            load_chunks(win_v, 3 * DA, 24, 1, kst, oks, 3)
            load_chunks(win_v, 3 * DA + 2 * DC, 32, 1, kst, oks, 4)
            load_chunks(win_v, 3 * DA + DC, 40, 1, kst, oks, 5)
            sp.wait_ge(rope_ok, 1)
            sp.dma_start(okp, qkv_p[:, :, DA:2 * DA]).then_inc(out_s, 16)
            sp.dma_start(ovp, qkv_p[:, :, 2 * DA:3 * DA]).then_inc(out_s, 16)
            for b in range(NB):
                sp.dma_start(oks[b, PAST - NS:PAST, :], qkv_s[b * NS:(b + 1) * NS, DA:2 * DA]).then_inc(out_s, 16)
                sp.dma_start(ovs[b, PAST - NS:PAST, :], qkv_s[b * NS:(b + 1) * NS, 2 * DA:3 * DA]).then_inc(out_s, 16)
            copy_batch(vst, ovs, 0)
            copy_batch(vst, ovs, 1)
            sp.wait_ge(zl_out, 1)
            sp.dma_start(o_cp.rearrange("a b j d -> (a b j) d"), zrows[0:2, :]).then_inc(zrow_s, 16)
            sp.dma_start(o_cs.rearrange("a b j d -> (a b j) d"), zrows[2:2 + 2 * NB, :]).then_inc(zrow_s, 16)
            sp.wait_ge(zrow_s, 32)

            def load_k(b):
                bb = ds(b, 1)
                for part, last in enumerate(K_PARTS):
                    if not (isinstance(b, int) and b == 0):
                        sp.wait_ge(kT_raw, (b - 1) * 24 + last)
                    rr = slice(4 * part, 4 * part + 4)
                    if part < 2:
                        sp.dma_start(ka[:, rr, :], kst[bb, 0:OLD, :].rearrange("a (g r) d -> (a g) r d", r=16)[:, rr, :]).then_inc(k_in[part], 16)
                    else:
                        sp.dma_start(kb[:, :, :], kst[bb, OLD:PAST, :].rearrange("a (g r) d -> (a g) r d", r=RB)).then_inc(k_in[part], 16)

            def load_v(b):
                bb = ds(b, 1)
                sp.dma_start(va[:, :, :], vst[bb, 0:OLD, :].rearrange("a (g r) d -> (a g) r d", r=16)[:, 0:RA, :]).then_inc(v_in, 16)
                sp.dma_start(vb[:, :, :], vst[bb, OLD:PAST, :].rearrange("a (g r) d -> (a g) r d", r=RB)).then_inc(v_in, 16)

            load_k(0)
            sp.wait_ge(out_s, 16 * (2 + 2 * NB))
            sp.wait_ge(s_po, HEADS)
            load_v(0)
            load_k(1)
            with sp.Fori(1, NB - 1) as b:
                load_k(b + 1)
                sp.wait_ge(v_used, b)
                load_v(b)
            sp.wait_ge(v_used, NB - 1)
            load_v(NB - 1)
            sp.wait_ge(kT_raw, NB * 24)
            for k in range(2):
                load_piece(wout_v, slice(0, CW), 48 + k, k)
            sp.wait_ge(att_ok, 1)
            for k in range(2, PPC):
                load_piece(wout_v, slice(0, CW), 48 + k, k)
            sp.dma_start(xt[:, 1:3, :], xp_v).then_inc(x_in, 16)
            sp.dma_start(xt[0:TS, 0, :], xs_v).then_inc(x_in, 16)
            sp.dma_start(ln1[:, 0, :], ln1_g.rearrange("a d -> (a d)").partition_broadcast(128)).then_inc(ln1_in, 16)
            sp.dma_start(ln1[:, 1, :], ln1_b.rearrange("a d -> (a d)").partition_broadcast(128)).then_inc(ln1_in, 16)
            load_chunks(wout_v, 0, 48, 2, kst, oks, 6, skip=PPC)
            for k in range(2):
                load_piece(wq_v, slice(0, CW), 64 + k, k)
            copy_batch(vst, ovs, 2)
            copy_batch(vst, ovs, 3)
            load_chunks(wq_v, 0, 64, 2, skip=2)
            for b in range(4, NB):
                copy_batch(vst, ovs, b)
            sp.dma_start(xt[TS:128, 0, :], xt[0:TS, 0, :]).then_inc(pack_in, 16)
            sp.wait_ge(sc_ok, 12)
            sp.dma_start(ln2[:, 0, :], ln2_g.rearrange("a d -> (a d)").partition_broadcast(128)).then_inc(ln2_in, 16)
            sp.dma_start(ln2[:, 1, :], ln2_b.rearrange("a d -> (a d)").partition_broadcast(128)).then_inc(ln2_in, 16)
            sp.wait_ge(pack_rd, 1)
            for n, s in enumerate([k for k, p in zip(STARTS, PHASES) if p[1] == 0]):
                for half in range(2):
                    sp.dma_start(idx_all[half * TS:(half + 1) * TS, s * TOPK:(s + 4) * TOPK],
                                 idx_s[:, half, :]).then_inc(pack_in, 16)
            sp.dma_start(gates[TS:128, 0, 0:64], gates[0:TS, 0, 64:128]).then_inc(pack_in, 16)
            sp.wait_ge(fold_rd, 1)
            sp.dma_start(yhalf[:, :], yacc[TS:128, 0, :]).then_inc(fold_in, 16)
            sp.dma_start(plew[:, :, :], wple_v).then_inc(ple_in, 16)
            sp.dma_start(pnat[:, 1:3, :], pp_v).then_inc(ple_in, 16)
            sp.dma_start(pnat[0:TS, 0, :], ps_v).then_inc(ple_in, 16)
            load_chunks(wg_v, 0, 80, 2)
            for c in range(4):
                sp.wait_ge(fin_ok, c + 1)
                cc = slice(c * CW, (c + 1) * CW)
                sp.dma_start(yp_v[:, :, cc], xt[:, 1:3, cc]).then_inc(out_s, 16)
                sp.dma_start(ys_v[:, cc], xt[0:TS, 0, cc]).then_inc(out_s, 16)
            sp.wait_ge(out_s, 16 * (2 + 2 * NB + 8))
            sp.wait_ge(kvcopy, 16 * 8 * 2 * NB)

        @block.gpsimd
        def _(pool):
            nc.gpsimd.memset(tok[:, :], 0.0).then_inc(g_token, 1)

            def low(pc, slot):
                pool.wait_ge(w_hi_ready, pc + 1)
                nc.gpsimd.tensor_tensor(wlo[:, slot, :, :], raw[:, slot, :, :],
                                        whi[:, slot, :, :].bitcast(f32), ALU.subtract).then_inc(w_lo_ready, 1)

            def lows(first, count):
                with pool.Fori(0, count // 2) as i:
                    for slot in range(2):
                        low(i * 2 + (first + slot), slot)

            lows(0, 80)

            def gathers(k, half, table):
                for j in range(TOPK):
                    if j % 4 == 0:
                        pool.wait_ge(g_token, k * 4 + (j // 4 + 1))
                        pool.wait_ge(idx_st, k + 1)
                        pool.wait_ge(g_free, k * TOPK + (j + 4))
                        nc.gpsimd.tensor_tensor(tok[:, :], tok[:, :], tok[:, :], ALU.add).then_inc(g_token, 1)
                    pool.indirect_dma_start(ring[:, j % NSLOT, :], None, table,
                                            bass.IndirectOffsetOnAxis(idxc[:, half, j:j + 1], 0)).then_inc(g_in[j % NSLOT], 16)

            for (kind, t, nb), k0 in zip(PHASES, STARTS):
                with pool.Fori(0, nb // 2) as i:
                    for half in range(2):
                        gathers(i * 2 + (k0 + half), half, u_tab if kind == "u" else v_tab)
            pool.wait_ge(fold_rd, 1)
            lows(80, 16)

        @block.scalar
        def _(act):
            A = nc.scalar.activation

            def hi(pc, slot):
                act.wait_ge(w_in_s[slot], (pc - slot) * 8 + 16)
                if not (isinstance(pc, int) and pc < 2):
                    act.wait_ge(w_used, pc - 1)
                A(whi[:, slot, :, :], raw[:, slot, :, :], ACT.Copy).then_inc(w_hi_ready, 1)

            def his(first, count):
                with act.Fori(0, count // 2) as i:
                    for slot in range(2):
                        hi(i * 2 + (first + slot), slot)

            def transposed_hi(use):
                for n in range(12):
                    t, g = divmod(n, 4)
                    c0, r = TILES[t]
                    act.wait_ge(tp_done, use * 12 + n + 1)
                    A(thi[:, 4 * g:4 * g + 4, c0:c0 + r],
                      PS[:, n % 8, :].rearrange("p (a c) -> p a c", a=4)[:, :, 0:r], ACT.Copy).then_inc(th_ready, 1)

            transposed_hi(0)
            act.wait_ge(small_T, 1)
            A(zbuf[:, :, Z0:ZW].rearrange("p f (b j) -> p f b j", b=NB)[:, :, :, 0:2],
              PS[:, 4, 0:128].rearrange("p (f b j) -> p f b j", f=8, b=NB), ACT.Copy).then_inc(small_ok, 1)
            act.wait_ge(small_T, 2)
            A(subT[:, :, :], PS[:, 5, 0:256].rearrange("p (a c) -> p a c", a=2), ACT.Copy).then_inc(small_ok, 1)
            hi(0, 0)
            hi(1, 1)
            his(2, 46)
            act.wait_ge(zl_T, 1)
            act.wait_ge(w_lo_ready, 48)
            A(zrows[:, :], PS[0:2 + 2 * NB, 0:2, :].rearrange("p a c -> p (a c)"), ACT.Copy).then_inc(zl_out, 1)
            act.wait_ge(conv_m, 1)
            A(thi[:, 8:16, TS:N], ubuf[:, :, 0:TP], ACT.Copy).then_inc(conv_hi, 1)
            for b in range(NB):
                A(thi[:, 8:16, b * NS:(b + 1) * NS], ubuf[:, :, Z0 + 10 * b:Z0 + 10 * b + NS], ACT.Copy).then_inc(conv_hi, 1)
            for j in range(16):
                act.wait_ge(qk_T, j + 1)
                dst = (qt, kt_)[j % 2]
                A(dst[:, j // 2, :], PS[:, 2 + j % 6, 0:N], ACT.Copy).then_inc(qk_ok, 1)
            for h in range(HEADS):
                e = h % 2
                act.wait_ge(s_neg, h + 1)
                A(psm[:, e, 0, :], psm[:, e, 0, :], ACT.Exp, bias=nmx[:, e, 0:1], scale=SCALE)
                A(psm[:, e, 1:3, :], psm[:, e, 1:3, :], ACT.Exp, bias=nmx[:, e, 1:2], scale=SCALE).then_inc(s_exp, 1)
                act.wait_ge(s_pT, h + 1)
                A(ppt[:, e, :, :].rearrange("p a c -> p (a c)"), PS[:, 2 + e, 0:384], ACT.Copy).then_inc(s_pok, 1)
            def key_copies(b):
                for n in range(24):
                    act.wait_ge(kT_raw, b * 24 + (n + 1))
                    w = 4 * (GA if n < 16 else GB)
                    A(ktb[:, n % 2, 0:w], PS[:, 3 + n % 2, 0:w], ACT.Copy).then_inc(kT_ok, 1)

            def exps(b):
                act.wait_ge(d_neg, b + 1)
                A(ssm[:, :], ssm[:, :], ACT.Exp, bias=nmx[0:64, 0, 0:1], scale=SCALE).then_inc(d_exp, 1)

            def prob_copies(b):
                act.wait_ge(d_pT, b + 1)
                A(pta[:, :, :].rearrange("p a c -> p (a c)"), PS[0:GA, 6, :], ACT.Copy)
                A(ptb[:, :, :].rearrange("p a c -> p (a c)"), PS[:, 7, 0:256], ACT.Copy)
                A(ptc[:, :], PS[0:TS, 7, 256:320], ACT.Copy).then_inc(d_pok, 1)

            def out_copies(b):
                act.wait_ge(v_used, b + 1)
                for i in range(4):
                    m = A(osb[32 * i:32 * i + 16, :], PS[32 * i:32 * i + 16, 5, 0:256], ACT.Copy)
                m.then_inc(d_out, 1)

            key_copies(0)
            exps(0)
            with act.Fori(1, NB) as b:
                key_copies(b)
                prob_copies(b - 1)
                exps(b)
                out_copies(b - 1)
            prob_copies(NB - 1)
            hi(48, 0)
            hi(49, 1)
            out_copies(NB - 1)

            def layer_norm_root(n):
                act.wait_ge(var_ok, n + 1)
                A(std[:, 0:1], vst_[:, :], ACT.Sqrt).then_inc(std_ok, 1)

            his(50, 14)
            for n in range(3):
                layer_norm_root(n)
            transposed_hi(1)
            his(64, 16)
            for n in range(12):
                act.wait_ge(sc_psum, n + 1)
                t, g = divmod(n, 4)
                r = TILES[(1, 2, 0)[t]][1]
                A(sc[0:r, (1, 2, 0)[t], 4 * g:4 * g + 4, :].rearrange("p a c -> p (a c)"),
                  PS[0:r, n % 8, :], ACT.Copy).then_inc(sc_ok, 1)
            def gate_exp(n, t):
                r = TILES[t][1]
                act.wait_ge(g_sub, n + 1)
                A(gates[0:r, t, :], gates[0:r, t, :], ACT.Exp).then_inc(g_exp, 1)

            def dots_gelu(n, t, w):
                act.wait_ge(dots, n + 1)
                A(hdot[:, t, 0:w], hdot[:, t, 0:w], ACT.Gelu).then_inc(gelu_ok, 1)

            gate_exp(0, 1)
            gate_exp(1, 2)
            dots_gelu(0, 1, 128)
            gate_exp(2, 0)
            dots_gelu(1, 2, 128)
            dots_gelu(2, 0, 64)
            for n in range(3, 6):
                layer_norm_root(n)
            transposed_hi(2)
            for t in range(3):
                c0, r = TILES[t]
                act.wait_ge(pT_psum, t + 1)
                A(pT[:, :, c0:c0 + r], PS[:, 4 + t, 0:256].rearrange("p (a c) -> p a c", a=2)[:, :, 0:r], ACT.Copy).then_inc(pT_ok, 1)

            def sigmoids(c, bank):
                act.wait_ge(w_used, c * PPC + 84)
                if not (isinstance(c, int) and c == 0):
                    act.wait_ge(fin_ok, c)
                for t in range(3):
                    r = TILES[t][1]
                    m = A(gsig[0:r, t, :], PS[0:r, bank + t, :], ACT.Sigmoid)
                m.then_inc(sig_ok, 1)

            act.wait_ge(fold_rd, 1)
            for c in range(4):
                for k in range(PPC):
                    hi(80 + c * PPC + k, k % 2)
                    if k == 1 and c > 0:
                        sigmoids(c - 1, 4 * ((c - 1) % 2))
            sigmoids(3, 4)

        @block.vector
        def _(dve):
            V = nc.vector
            step = [0]

            def link(ins, base=None):
                step[0] += 1
                ins.then_inc(dstep, 1)
                dve.wait_ge(dstep, step[0] if base is None else base + step[0])

            def transposed_lo(use):
                for n in range(12):
                    t, g = divmod(n, 4)
                    c0, r = TILES[t]
                    dve.wait_ge(th_ready, use * 12 + n + 1)
                    V.tensor_tensor(tlo[:, 4 * g:4 * g + 4, c0:c0 + r],
                                    PS[:, n % 8, :].rearrange("p (a c) -> p a c", a=4)[:, :, 0:r],
                                    thi[:, 4 * g:4 * g + 4, c0:c0 + r].bitcast(f32), ALU.subtract).then_inc(tl_ready, 1)

            def prompt_out(h):
                e = h % 2
                dve.wait_ge(s_pv, h + 1)
                link(V.tensor_scalar(thi[:, h, TS:N], PS[:, 4 + e, 0:TP], 1.0, None, ALU.mult))
                V.tensor_tensor(tlo[:, h, TS:N], PS[:, 4 + e, 0:TP], thi[:, h, TS:N].bitcast(f32), ALU.subtract).then_inc(s_po, 1)

            V.memset(zbuf[:, :, 0:2], 0.0).then_inc(z_pad, 1)
            transposed_lo(0)
            with dve.Fori(0, 3) as i:
                for h in range(2):
                    dve.wait_ge(w_used, i * 8 + 4 * (h + 1))
                    for t in range(3):
                        dst = (qkv_s[:, ds(i * DA + h * CW, CW)] if t == 0
                               else qkv_p[:, t - 1, ds(i * DA + h * CW, CW)])
                        m = V.tensor_scalar(dst, PS[0:TILES[t][1], 4 * h + t, :], 1.0, None, ALU.mult)
                    m.then_inc(acc_free, 1)
            dve.wait_ge(acc_free, 6)
            dve.wait_ge(c2_in, 160)
            for t in range(3):
                r = TILES[t][1]
                hd = 2 * HEADS
                src = (qkv_s[:, 0:2 * DA] if t == 0 else qkv_p[:, t - 1, 0:2 * DA]).rearrange("p (h d) -> p h d", h=hd)
                x1, x2 = src[:, :, 0:DH // 2], src[:, :, DH // 2:DH]
                cb = cosb[0:r, t, :].unsqueeze(1).broadcast_to([r, hd, DH // 2])
                sb_ = sinb[0:r, t, :].unsqueeze(1).broadcast_to([r, hd, DH // 2])
                tm = [rtmp[0:r, j, :].rearrange("p (h d) -> p h d", h=hd) for j in range(4)]
                for j, (a, b) in enumerate(((x1, cb), (x2, sb_), (x2, cb), (x1, sb_))):
                    m = V.tensor_tensor(tm[j], a, b, ALU.mult)
                link(m)
                V.tensor_tensor(x1, tm[0], tm[1], ALU.subtract)
                link(V.tensor_tensor(x2, tm[2], tm[3], ALU.add))
            V.memset(nmx[:, :, :], 0.0).then_inc(rope_ok, 1)
            for c in range(6, 8):
                dve.wait_ge(w_used, 4 * (c + 1))
                if c == 6:
                    dve.wait_ge(small_ok, 1)
                for j in range(4):
                    m = V.tensor_scalar(ubuf[:, 4 * (c - 6) + j, 0:N], PS[:, 4 * (c % 2) + j, 0:N], 1.0, None, ALU.mult)
                m.then_inc(acc_free, 1)
            dve.wait_ge(acc_free, 8)
            for c in range(8, 10):
                dve.wait_ge(w_used, 4 * (c + 1))
                for j in range(4):
                    f = 4 * (c - 8) + j
                    ps = PS[:, 4 * (c % 2) + j, :]
                    V.tensor_tensor(zbuf[:, f, 2:Z0], ps[:, TS:N], ubuf[:, f, TS:N], ALU.mult)
                    m = V.tensor_tensor(zbuf[:, f, Z0:ZW].rearrange("p (b j) -> p b j", b=NB)[:, :, 2:2 + NS],
                                        ps[:, 0:TS].rearrange("p (b s) -> p b s", b=NB),
                                        ubuf[:, f, 0:TS].rearrange("p (b s) -> p b s", b=NB), ALU.mult)
                m.then_inc(acc_free, 1)
            dve.wait_ge(acc_free, 10)
            V.tensor_copy(zl[:, :, 0:2], zbuf[:, :, TP:TP + 2])
            V.tensor_copy(zl[:, :, 2:2 + 2 * NB].rearrange("p f (b j) -> p f b j", b=NB),
                          zbuf[:, :, Z0:ZW].rearrange("p f (b j) -> p f b j", b=NB)[:, :, :, NS:NS + 2]).then_inc(zl_ready, 1)
            W2 = ZW - 2
            for j in range(3):
                for f in range(8):
                    o = ubuf[:, f, 0:W2]
                    if j == 0:
                        m = V.tensor_scalar(o, zbuf[:, f, 0:W2], cw[:, 0, f:f + 1], None, ALU.mult)
                    else:
                        m = V.scalar_tensor_tensor(out=o, in0=zbuf[:, f, j:j + W2], scalar=cw[:, j, f:f + 1], in1=o,
                                                   op0=ALU.mult, op1=ALU.add)
                link(m)
            for c in range(10, 12):
                dve.wait_ge(w_used, 4 * (c + 1))
                for j in range(4):
                    f = 4 * (c - 10) + j
                    ps = PS[:, 4 * (c % 2) + j, :]
                    V.tensor_tensor(ubuf[:, f, 0:TP], ps[:, TS:N], ubuf[:, f, 0:TP], ALU.mult)
                    o = ubuf[:, f, Z0:ZW].rearrange("p (b j) -> p b j", b=NB)[:, :, 0:NS]
                    m = V.tensor_tensor(o, ps[:, 0:TS].rearrange("p (b s) -> p b s", b=NB), o, ALU.mult)
                m.then_inc(acc_free, 1)
            dve.wait_ge(acc_free, 12)
            V.memset(rs[:, :], 0.0).then_inc(conv_m, 1)
            dve.wait_ge(conv_hi, 1 + NB)
            V.tensor_tensor(tlo[:, 8:16, TS:N], ubuf[:, :, 0:TP], thi[:, 8:16, TS:N].bitcast(f32), ALU.subtract)
            for b in range(NB):
                cc = slice(b * NS, (b + 1) * NS)
                m = V.tensor_tensor(tlo[:, 8:16, cc], ubuf[:, :, Z0 + 10 * b:Z0 + 10 * b + NS],
                                    thi[:, 8:16, cc].bitcast(f32), ALU.subtract)
            link(m)
            for h in range(HEADS):
                e = h % 2
                dve.wait_ge(s_score, h + 1)
                w = psm[:, e, :, :].rearrange("p a c -> p (a c)")
                link(V.tensor_tensor(w, PS[:, e, 0:384], mp_add[:, :], ALU.add))
                V.reduce_max(mx[:, 0:1], w[:, 0:128], AX)
                link(V.reduce_max(mx[:, 1:2], w[:, 128:384], AX))
                V.tensor_scalar(nmx[:, e, :], mx[:, 0:2], -SCALE, None, ALU.mult).then_inc(s_neg, 1)
                dve.wait_ge(s_exp, h + 1)
                for q, (a, b) in enumerate(((0, 128), (128, 384))):
                    m = V.scalar_tensor_tensor(out=w[:, a:b], in0=w[:, a:b], scalar=1.0, in1=mp_mul[:, a:b],
                                               op0=ALU.mult, op1=ALU.mult, accum_out=rs[:, q:q + 1])
                link(m)
                link(V.reciprocal(rs[:, 2:4], rs[:, 0:2]))
                V.tensor_scalar(w[:, 0:128], w[:, 0:128], rs[:, 2:3], None, ALU.mult)
                link(V.tensor_scalar(w[:, 128:384], w[:, 128:384], rs[:, 3:4], None, ALU.mult))
                V.memset(mx[:, 3:4], 0.0).then_inc(s_prob, 1)
                if h > 0:
                    prompt_out(h - 1)
            prompt_out(HEADS - 1)
            V.memset(osb[:, :], 0.0)
            link(V.memset(qpad[:, :, :], 0.0))

            def pad_queries(b, ib):
                col = slice(b * NS, (b + 1) * NS) if isinstance(b, int) else ds(b * NS, NS)
                bb = slice(b, b + 1) if isinstance(b, int) else ds(b, 1)
                for h in range(HEADS):
                    V.tensor_scalar(qpad[:, h, h * NS:(h + 1) * NS], qt[:, h, col], 1.0, None, ALU.mult)
                for m_, c_ in ((ms_add, mc_add), (ms_mul, mc_mul)):
                    m = V.tensor_scalar(m_[:, GA * RA:GA * RA + TS], c_[:, bb, :].rearrange("p a c -> p (a c)"),
                                        1.0, None, ALU.mult)
                link(m, ib)
                V.memset(mx[:, 2:3], 0.0).then_inc(q_pad, 1)

            def softmax(b, ib):
                dve.wait_ge(d_score, b + 1)
                if not isinstance(b, int):
                    dve.wait_ge(d_pT, b)
                V.tensor_tensor(ssm[:, 0:480], PS[0:64, 0, 0:480], ms_add[:, 0:480], ALU.add)
                V.tensor_tensor(ssm[:, 480:832], PS[0:64, 1, 0:352], ms_add[:, 480:832], ALU.add)
                link(V.tensor_tensor(ssm[:, 832:SCOLS], PS[0:64, 2, :], ms_add[:, 832:SCOLS], ALU.add), ib)
                link(V.reduce_max(mx[0:64, 0:1], ssm[:, :], AX), ib)
                V.tensor_scalar(nmx[0:64, 0, 0:1], mx[0:64, 0:1], -SCALE, None, ALU.mult).then_inc(d_neg, 1)
                dve.wait_ge(d_exp, b + 1)
                link(V.scalar_tensor_tensor(out=ssm[:, :], in0=ssm[:, :], scalar=1.0, in1=ms_mul[:, :],
                                            op0=ALU.mult, op1=ALU.mult, accum_out=rs[0:64, 0:1]), ib)
                link(V.reciprocal(rs[0:64, 1:2], rs[0:64, 0:1]), ib)
                link(V.tensor_scalar(ssm[:, :], ssm[:, :], rs[0:64, 1:2], None, ALU.mult), ib)
                V.memset(mx[:, 3:4], 0.0).then_inc(d_prob, 1)

            def decode_out(b, ib):
                dve.wait_ge(d_oT, b + 1)
                col = slice(b * NS, (b + 1) * NS) if isinstance(b, int) else ds(b * NS, NS)
                o = PS[:, 7, 384:448].rearrange("p (g i s) -> p i g s", g=2, s=NS)
                hi_ = thi[:, 0:8, col].rearrange("p (i g) s -> p i g s", i=4)
                lo_ = tlo[:, 0:8, col].rearrange("p (i g) s -> p i g s", i=4)
                link(V.tensor_scalar(hi_, o, 1.0, None, ALU.mult), ib)
                V.tensor_tensor(lo_, o, hi_.bitcast(f32), ALU.subtract).then_inc(d_oread, 1)
                dve.wait_ge(d_oread, b + 1)

            pad_queries(0, None)
            softmax(0, None)
            base0, PER = step[0], 7
            with dve.Fori(1, NB) as b:
                step[0] = base0
                ib = (b - 1) * PER
                pad_queries(b, ib)
                softmax(b, ib)
                decode_out(b - 1, ib)
                assert step[0] == base0 + PER
            step[0] = base0 + (NB - 1) * PER
            decode_out(NB - 1, None)
            V.memset(mx[:, 0:4], 0.0).then_inc(att_ok, 1)
            dve.wait_ge(x_in, 16 * 5)
            with dve.Fori(0, 2) as i:
                for h in range(2):
                    dve.wait_ge(w_used, i * 8 + (48 + 4 * (h + 1)))
                    for t in range(3):
                        o = xt[0:TILES[t][1], t, ds(i * (2 * CW) + h * CW, CW)]
                        m = V.scalar_tensor_tensor(out=o, in0=o, scalar=ALPHA, in1=PS[0:TILES[t][1], 4 * h + t, :],
                                                   op0=ALU.mult, op1=ALU.add)
                    m.then_inc(acc_free, 1)
            dve.wait_ge(acc_free, 16)

            def layer_norm(n, t, gb):
                r = TILES[t][1]
                x = xt[0:r, t, :]
                for c in range(4):
                    m = V.bn_stats(bst[0:r, c, :], x[:, c * 512:(c + 1) * 512])
                link(m)
                link(V.bn_aggr(mv[0:r, :], bst[0:r, :, :].rearrange("p a c -> p (a c)")))
                link(V.memset(vst_[:, :], 1.0))
                V.tensor_scalar(vst_[0:r, :], mv[0:r, 1:2], EPS, None, ALU.add).then_inc(var_ok, 1)
                dve.wait_ge(std_ok, n + 1)
                link(V.reciprocal(std[0:r, 1:2], std[0:r, 0:1]))
                link(V.tensor_scalar(x, x, mv[0:r, 0:1], std[0:r, 1:2], ALU.subtract, ALU.mult))
                link(V.tensor_tensor(x, x, gb[0:r, 0, :], ALU.mult))
                V.tensor_tensor(x, x, gb[0:r, 1, :], ALU.add).then_inc(ln_ok, 1)

            dve.wait_ge(ln1_in, 32)
            for n in range(3):
                layer_norm(n, n, ln1)
            transposed_lo(1)
            for c in range(4):
                dve.wait_ge(w_used, 64 + 4 * (c + 1))
                for j in range(4):
                    m = V.tensor_scalar(qpt[:, 4 * c + j, :], PS[:, 4 * (c % 2) + j, 0:N], 1.0, None, ALU.mult)
                m.then_inc(acc_free, 1)

            def top_keys(t):
                r = TILES[t][1]
                s = lambda f: sc[0:r, t, f, :]
                a8 = slice(0, 8)
                for f in range(NF):
                    m = V.max(top[0:r, f, a8], s(f))
                link(m)
                for f in range(NF):
                    m = V.max_index(topi[0:r, f, a8], top[0:r, f, a8], s(f))
                link(m)
                for f in range(NF):
                    m = V.match_replace(s(f), top[0:r, f, a8], s(f), -3e38)
                link(m)

            def top_keys_rest(t):
                r = TILES[t][1]
                s = lambda f: sc[0:r, t, f, :]
                b8 = slice(8, 16)
                for f in range(NF):
                    m = V.max(top[0:r, f, b8], s(f))
                link(m)
                for f in range(NF):
                    m = V.max_index(topi[0:r, f, b8], top[0:r, f, b8], s(f))
                link(m)

            def top_candidates(t):
                r = TILES[t][1]
                a8 = slice(0, 8)
                V.tensor_copy(topf[0:r, :, :], topi[0:r, :, :])
                tv = top[0:r, :, :].rearrange("p (h q) k -> p h q k", q=2)
                full = [r, PH, TOPK, TOPK]
                link(V.tensor_tensor(cand[0:r, :, :, :], tv[:, :, 0, :].unsqueeze(3).broadcast_to(full),
                                     tv[:, :, 1, :].unsqueeze(2).broadcast_to(full), ALU.add))
                cf = lambda h: cand[0:r, h, :, :].rearrange("p a c -> p (a c)")
                for h in range(PH):
                    m = V.max(ctop[0:r, h, a8], cf(h))
                link(m)
                for h in range(PH):
                    m = V.max_index(cidx[0:r, h, a8], ctop[0:r, h, a8], cf(h))
                link(m)
                for h in range(PH):
                    m = V.match_replace(cf(h), ctop[0:r, h, a8], cf(h), -3e38)
                link(m)

            def top_ranks(t):
                r = TILES[t][1]
                b8 = slice(8, 16)
                cf = lambda h: cand[0:r, h, :, :].rearrange("p a c -> p (a c)")
                for h in range(PH):
                    m = V.max(ctop[0:r, h, b8], cf(h))
                link(m)
                for h in range(PH):
                    m = V.max_index(cidx[0:r, h, b8], ctop[0:r, h, b8], cf(h))
                link(m)
                g = gates[0:r, t, :].rearrange("p (h k) -> p h k", h=PH)
                V.tensor_tensor(g, ctop[0:r, :, :], ctop[0:r, :, 0:1].broadcast_to([r, PH, TOPK]),
                                ALU.subtract).then_inc(g_sub, 1)
                V.tensor_single_scalar(cint[0:r, 0, :, :], cidx[0:r, :, :], 4, ALU.logical_shift_right)
                link(V.tensor_single_scalar(cint[0:r, 1, :, :], cidx[0:r, :, :], 15, ALU.bitwise_and))
                link(V.tensor_copy(cflt[0:r, :, :, :], cint[0:r, :, :, :]))

            def top_select(t, q):
                r = TILES[t][1]
                full = [r, PH, TOPK, TOPK]
                fv = topf[0:r, :, :].rearrange("p (h q) k -> p h q k", q=2)
                hv = hot[0:r, :, :, :]
                link(V.tensor_tensor(hv, cflt[0:r, q, :, :].unsqueeze(3).broadcast_to(full),
                                     iota[0:r, :].unsqueeze(1).unsqueeze(1).broadcast_to(full), ALU.is_equal))
                link(V.tensor_tensor(hv, hv, fv[:, :, q, :].unsqueeze(2).broadcast_to(full), ALU.mult))
                link(V.tensor_reduce(esel[0:r, q, :, :], hv, AX, ALU.add))

            def top_experts(n, t):
                r = TILES[t][1]
                g = gates[0:r, t, :].rearrange("p (h k) -> p h k", h=PH)
                e1, e2 = (esel[0:r, q, :, :].rearrange("p h k -> p (h k)") for q in range(2))
                outs = ([idx_s[:, :, :].rearrange("p a c -> p (a c)")] if t == 0 else
                        [idx_all[:, s_ * TOPK:(s_ + 8) * TOPK] for s_, p in zip(STARTS, PHASES) if p[1] == t])
                for o in outs:
                    m = V.scalar_tensor_tensor(out=o, in0=e1, scalar=float(NK), in1=e2, op0=ALU.mult, op1=ALU.add)
                link(m)
                dve.wait_ge(g_exp, n + 1)
                link(V.tensor_reduce(ctop[0:r, :, 0], g, AX, ALU.add))
                link(V.reciprocal(ctop[0:r, :, 1], ctop[0:r, :, 0]))
                link(V.tensor_tensor(g, g, ctop[0:r, :, 1:2].broadcast_to([r, PH, TOPK]), ALU.mult))

            dve.wait_ge(sc_ok, 12)
            V.memset(idx_all[:, BLOCKS * TOPK:(BLOCKS + 1) * TOPK], 0)
            top_keys(1)
            top_keys_rest(1)
            top_candidates(1)
            top_ranks(1)
            top_select(1, 0)
            top_select(1, 1)
            top_experts(0, 1)
            link(V.memset(yacc[:, :, :], 0.0))
            V.tensor_scalar(idxc[:, 0, :], idx_all[:, 0:TOPK], 0, None, ALU.add).then_inc(idx_st, 1)
            V.memset(mx[:, 0:1], 0.0).then_inc(g_free, NSLOT)

            def expert_blocks(kind, t, k0, first, pairs, middle=None):
                x = xt[:, t, :]
                y = yacc[:, t, :]
                base1 = step[0]

                def pair(i, ib):
                    if kind == "v":
                        link(V.tensor_scalar(ablk[:, :], hdot[:, t, ds(i * 32, 32)], 1.0, None, ALU.mult), ib)
                    for half in range(2):
                        k = i * 2 + (k0 + half)
                        V.tensor_scalar(idxc[:, 1 - half, :], idx_all[:, ds(i * 32 + (k0 + half + 1) * TOPK, TOPK)], 0, None, ALU.add).then_inc(idx_st, 1)
                        for j in range(TOPK):
                            g = ring[:, j % NSLOT, :]
                            c = half * TOPK + j
                            dve.wait_ge(g_in[j % NSLOT], k * 32 + 16 * (j // NSLOT + 1))
                            if kind == "u":
                                V.scalar_tensor_tensor(out=g, in0=g, scalar=1.0, in1=x, op0=ALU.mult, op1=ALU.mult,
                                                       accum_out=hblk[:, c:c + 1]).then_inc(g_free, 1)
                            else:
                                dve.wait_ge(g_free, k * TOPK + (NSLOT + j))
                                V.scalar_tensor_tensor(out=y, in0=g, scalar=ablk[:, c:c + 1], in1=y,
                                                       op0=ALU.mult, op1=ALU.add).then_inc(g_free, 1)
                        dve.wait_ge(g_free, k * TOPK + (NSLOT + TOPK))
                        if half == 0 and middle is not None:
                            middle()
                    if kind == "u":
                        link(V.tensor_scalar(hdot[:, t, ds(i * 32, 32)], hblk[:, :], 1.0, None, ALU.mult), ib)

                if pairs == 1:
                    pair(first, None)
                else:
                    with dve.Fori(first, first + pairs) as i:
                        step[0] = base1
                        pair(i, i - first)
                        assert step[0] == base1 + 1
                    step[0] = base1 + pairs

            for n, ((kind, t, nb), k0) in enumerate(zip(PHASES, STARTS)):
                if kind == "v":
                    m = [1, 2, 0].index(t)
                    dve.wait_ge(gelu_ok, m + 1)
                    w = 128 if t else 64
                    link(V.tensor_tensor(hdot[:, t, 0:w], hdot[:, t, 0:w], gates[:, t, 0:w], ALU.mult))
                if n < 2:
                    nt = (2, 0)[n]
                    expert_blocks(kind, t, k0, 0, 1, lambda: top_keys(nt))
                    top_keys_rest(nt)
                    expert_blocks(kind, t, k0, 1, 1, lambda: top_candidates(nt))
                    top_ranks(nt)
                    expert_blocks(kind, t, k0, 2, 1, lambda: top_select(nt, 0))
                    top_select(nt, 1)
                    top_experts(n + 1, nt)
                    if nt == 0:
                        V.memset(mx[:, 1:2], 0.0).then_inc(pack_rd, 1)
                    expert_blocks(kind, t, k0, 3, 1)
                else:
                    if n == 2:
                        dve.wait_ge(pack_in, 16 * 6)
                    expert_blocks(kind, t, k0, 0, nb // 2)
                if kind == "u":
                    V.memset(mx[:, 3:4], 0.0).then_inc(dots, 1)
            V.memset(mx[:, 0:1], 0.0).then_inc(fold_rd, 1)
            dve.wait_ge(ln2_in, 32)
            for n, t in enumerate((1, 2, 0)):
                r = TILES[t][1]
                if t == 0:
                    dve.wait_ge(fold_in, 16)
                    link(V.tensor_tensor(yacc[0:r, 0, :], yacc[0:r, 0, :], yhalf[:, :], ALU.add))
                link(V.scalar_tensor_tensor(out=xt[0:r, t, :], in0=xt[0:r, t, :], scalar=ALPHA, in1=yacc[0:r, t, :],
                                            op0=ALU.mult, op1=ALU.add))
                layer_norm(3 + n, t, ln2)
            transposed_lo(2)
            for c in range(4):
                for t in range(3):
                    n = c * 3 + t
                    r = TILES[t][1]
                    dve.wait_ge(ple_ps, n + 1)
                    V.tensor_scalar(pleo[0:r, t, c * CW:(c + 1) * CW], PS[0:r, n % 4, :], 1.0, None, ALU.mult).then_inc(ple_ok, 1)
            dve.wait_ge(ple_ok, 12)
            for c in range(4):
                dve.wait_ge(sig_ok, c + 1)
                cc = slice(c * CW, (c + 1) * CW)
                for t in range(3):
                    r = TILES[t][1]
                    m = V.tensor_tensor(gsig[0:r, t, :], gsig[0:r, t, :], pleo[0:r, t, cc], ALU.mult)
                link(m)
                for t in range(3):
                    r = TILES[t][1]
                    m = V.tensor_tensor(xt[0:r, t, cc], xt[0:r, t, cc], gsig[0:r, t, :], ALU.add)
                m.then_inc(fin_ok, 1)

        @block.tensor
        def _(pe):
            MM, TR = nc.tensor.matmul, nc.tensor.transpose

            def transposes(use):
                for n in range(12):
                    t, g = divmod(n, 4)
                    r = TILES[t][1]
                    if n >= 8:
                        pe.wait_ge(tl_ready, use * 12 + n - 7)
                    for j in range(4):
                        m = TR(PS[:, n % 8, 128 * j:128 * j + r], xt[0:r, t, (4 * g + j) * 128:(4 * g + j + 1) * 128],
                               ident[0:r, 0:r])
                    m.then_inc(tp_done, 1)

            def split_mm(out, lhs, rhs, start, stop):
                (lh, ll), (rh, rl) = lhs, rhs
                MM(out, lh, rh, start=start, stop=False)
                MM(out, lh, rl, start=False, stop=False)
                return MM(out, ll, rh, start=False, stop=stop)

            def token_piece(pc, k, bank):
                pe.wait_ge(w_lo_ready, pc + 1)
                s = k % 2
                for kk in range(KP):
                    q = k * KP + kk
                    for t in range(3):
                        c0 = TILES[t][0]
                        m = split_mm(PS[:, bank + t, :], (thi[:, q, c0:c0 + 128], tlo[:, q, c0:c0 + 128]),
                                     (whi[:, s, kk, :], wlo[:, s, kk, :]), q == 0, q == KT - 1)
                m.then_inc(w_used, 1)

            def feature_piece(pc, k, bank):
                pe.wait_ge(w_lo_ready, pc + 1)
                s = k % 2
                for kk in range(KP):
                    q = k * KP + kk
                    for j in range(4):
                        cc = slice(j * 128, (j + 1) * 128)
                        m = split_mm(PS[:, bank + j, 0:N], (whi[:, s, kk, cc], wlo[:, s, kk, cc]),
                                     (thi[:, q, :], tlo[:, q, :]), q == 0, q == KT - 1)
                m.then_inc(w_used, 1)

            def chunks(piece, cc0, pairs, free0):
                with pe.Fori(0, pairs) as i:
                    for h in range(2):
                        for k in range(PPC):
                            if k == 0 and free0:
                                pe.wait_ge(acc_free, i * 2 + (cc0 + h - 1))
                            piece(i * 8 + (cc0 * 4 + h * 4 + k), k, 4 * h)

            pe.wait_ge(x_in, 48)
            transposes(0)
            pe.wait_ge(c_in, 32)
            pe.wait_ge(tl_ready, 5)
            for f in range(8):
                m = TR(PS[:, 4, f * 16:(f + 1) * 16], crow[:, f * 128:(f + 1) * 128], ident[0:16, 0:16])
            m.then_inc(small_T, 1)
            pe.wait_ge(tl_ready, 6)
            for q in range(2):
                m = TR(PS[:, 5, q * 128:(q + 1) * 128], subn[:, q, :], ident[:, :])
            m.then_inc(small_T, 1)
            pe.wait_ge(tl_ready, 12)
            pe.wait_ge(small_ok, 2)
            for h in range(2):
                for k in range(PPC):
                    token_piece(h * 4 + k, k, 4 * h)
            chunks(token_piece, 2, 2, True)
            chunks(feature_piece, 6, 3, True)
            pe.wait_ge(acc_free, 12)
            pe.wait_ge(zl_ready, 1)
            for f in range(8):
                m = TR(PS[0:18, f // 4, (f % 4) * 128:(f % 4 + 1) * 128], zl[:, f, :], ident[:, :])
            m.then_inc(zl_T, 1)
            for j in range(16):
                if j >= 6:
                    pe.wait_ge(qk_ok, j - 5)
                col = (j % 2) * DA + (j // 2) * DH
                for t in range(3):
                    c0, r = TILES[t]
                    src = qkv_s[:, col:col + DH] if t == 0 else qkv_p[:, t - 1, col:col + DH]
                    m = TR(PS[:, 2 + j % 6, c0:c0 + r], src, ident[0:r, 0:r])
                m.then_inc(qk_T, 1)
            pe.wait_ge(qk_ok, 16)
            pe.wait_ge(zl_out, 1)

            def prompt_scores(h):
                e = h % 2
                for t in range(2):
                    m = MM(PS[:, e, 128 * t:128 * t + 128 * (t + 1)], qt[:, h, TS + 128 * t:TS + 128 * (t + 1)],
                           kt_[:, h, TS:TS + 128 * (t + 1)], start=True, stop=True)
                m.then_inc(s_score, 1)

            prompt_scores(0)
            prompt_scores(1)
            for h in range(HEADS):
                e = h % 2
                pe.wait_ge(s_prob, h + 1)
                for a in range(3):
                    m = TR(PS[:, 2 + e, a * 128:(a + 1) * 128], psm[:, e, a, :], ident[:, :])
                m.then_inc(s_pT, 1)
                if h + 2 < HEADS:
                    prompt_scores(h + 2)
                pe.wait_ge(s_pok, h + 1)
                if h >= 2:
                    pe.wait_ge(s_po, h - 1)
                vals = lambda t: qkv_p[:, t, 2 * DA + h * DH:2 * DA + (h + 1) * DH]
                MM(PS[:, 4 + e, 0:128], vals(0), ppt[:, e, 0, :], start=True, stop=True)
                MM(PS[:, 4 + e, 128:256], vals(0), ppt[:, e, 1, :], start=True, stop=False)
                MM(PS[:, 4 + e, 128:256], vals(1), ppt[:, e, 2, :], start=False, stop=True).then_inc(s_pv, 1)
            pe.wait_ge(s_po, HEADS)
            def key_transposes(n):
                w = GA if n < 16 else GB
                for j in range(4):
                    hc = slice(((n % 2) * 4 + j) * DH, ((n % 2) * 4 + j + 1) * DH)
                    src = ka[:, n // 2, hc] if n < 16 else kb[:, (n - 16) // 2, hc]
                    m = TR(PS[:, 3 + n % 2, j * w:(j + 1) * w], src, ident[0:w, 0:w])
                m.then_inc(kT_raw, 1)

            def key_scores(n):
                w = GA if n < 16 else GB
                if n < 16:
                    r = n // 2
                    o = PS[0:64, 0, r * GA:(r + 1) * GA] if r < 5 else PS[0:64, 1, (r - 5) * GA:(r - 4) * GA]
                else:
                    r = (n - 16) // 2
                    o = PS[0:64, 2, r * GB:(r + 1) * GB]
                for j in range(4):
                    h = (n % 2) * 4 + j
                    MM(o, qpad[:, h, :], ktb[:, n % 2, j * w:(j + 1) * w], start=(h == 0), stop=(h == 7))

            def batch_scores(b):
                pe.wait_ge(k_in[0], b * 16 + 16)
                key_transposes(0)
                key_transposes(1)
                pe.wait_ge(q_pad, b + 1)
                for n in range(24):
                    pe.wait_ge(kT_ok, b * 24 + (n + 1))
                    key_scores(n)
                    if n + 2 in K_PARTS[:2]:
                        pe.wait_ge(k_in[K_PARTS.index(n + 2) + 1], b * 16 + 16)
                    if n + 2 < 24:
                        key_transposes(n + 2)
                for h in range(HEADS):
                    m = MM(PS[0:64, 1, 288:352], qpad[:, h, :], kt_[:, h, 0:TS], start=(h == 0), stop=(h == 7))
                m.then_inc(d_score, 1)

            def batch_outputs(b):
                pe.wait_ge(d_prob, b + 1)
                MM(PS[0:GA, 6, 0:64], ssm[:, 0:GA], ident[0:64, 0:64], start=True, stop=True)
                for r in range(1, RA):
                    TR(PS[0:GA, 6, r * 64:(r + 1) * 64], ssm[:, r * GA:(r + 1) * GA], ident[0:64, 0:64])
                for r in range(RB):
                    TR(PS[:, 7, r * 64:(r + 1) * 64], ssm[:, 832 + r * GB:832 + (r + 1) * GB], ident[0:64, 0:64])
                TR(PS[0:TS, 7, 256:320], ssm[:, 768:832], ident[0:64, 0:64]).then_inc(d_pT, 1)
                pe.wait_ge(d_pok, b + 1)
                pe.wait_ge(v_in, b * 32 + 32)
                tiles = ([(pta[:, r, :], va[:, r, :]) for r in range(RA)] +
                         [(ptb[:, r, :], vb[:, r, :]) for r in range(RB)] +
                         [(ptc[:, :], qkv_s[:, 2 * DA:3 * DA])])
                for n, (p, v) in enumerate(tiles):
                    for i in range(4):
                        m = MM(PS[32 * i:32 * i + 16, 5, 0:256], p[:, 16 * i:16 * i + 16],
                               v[:, 256 * i:256 * (i + 1)], start=(n == 0), stop=(n == len(tiles) - 1))
                m.then_inc(v_used, 1)
                pe.wait_ge(d_out, b + 1)
                picks = ident[:, :].rearrange("p (i x) -> p i x", i=4)
                for g in range(2):
                    m = MM(PS[:, 7, 384 + 32 * g:416 + 32 * g], osb[:, g * DH:(g + 1) * DH],
                           picks[:, :, g * NS:(g + 1) * NS], start=True, stop=True)
                m.then_inc(d_oT, 1)

            batch_scores(0)
            with pe.Fori(1, NB) as b:
                batch_scores(b)
                batch_outputs(b - 1)
            pe.wait_ge(d_oread, NB - 1)
            batch_outputs(NB - 1)
            pe.wait_ge(att_ok, 1)
            for h in range(2):
                for k in range(PPC):
                    token_piece(48 + h * 4 + k, k, 4 * h)
            for h in range(2):
                pe.wait_ge(acc_free, 13 + h)
                for k in range(PPC):
                    token_piece(56 + h * 4 + k, k, 4 * h)
            pe.wait_ge(ln_ok, 3)
            transposes(1)
            pe.wait_ge(tl_ready, 24)
            chunks(feature_piece, 16, 2, True)
            pe.wait_ge(acc_free, 20)
            for n in range(12):
                t, g = divmod(n, 4)
                c0, r = TILES[(1, 2, 0)[t]]
                if n >= 8:
                    pe.wait_ge(sc_ok, n - 7)
                for j in range(4):
                    f = 4 * g + j
                    m = MM(PS[0:r, n % 8, j * 128:(j + 1) * 128], qpt[:, f, c0:c0 + r], subT[:, f % 2, :],
                           start=True, stop=True)
                m.then_inc(sc_psum, 1)
            pe.wait_ge(ln_ok, 6)
            pe.wait_ge(sc_ok, 12)
            transposes(2)
            pe.wait_ge(ple_in, 48)
            pe.wait_ge(tl_ready, 36)
            for t in range(3):
                r = TILES[t][1]
                for q in range(2):
                    m = TR(PS[:, 4 + t, q * 128:q * 128 + r], pnat[0:r, t, q * 128:(q + 1) * 128], ident[0:r, 0:r])
                m.then_inc(pT_psum, 1)
            pe.wait_ge(pT_ok, 3)
            for n in range(12):
                c, t = divmod(n, 3)
                c0, r = TILES[t]
                if n >= 4:
                    pe.wait_ge(ple_ok, n - 3)
                for q in range(2):
                    m = MM(PS[0:r, n % 4, :], pT[:, q, c0:c0 + r], plew[:, q, c * CW:(c + 1) * CW],
                           start=(q == 0), stop=(q == 1))
                m.then_inc(ple_ps, 1)
            pe.wait_ge(ple_ok, 12)
            for c in range(4):
                if c >= 2:
                    pe.wait_ge(sig_ok, c - 1)
                for k in range(PPC):
                    token_piece(80 + c * 4 + k, k, 4 * (c % 2))


def _rope_tables():
    import numpy as np
    half = DH // 2
    inv = np.float32(10000.0) ** (-np.arange(half, dtype=np.float32) / np.float32(half))
    cos, sin = (np.zeros((128, 3, half), np.float32) for _ in range(2))
    pos = np.zeros((128, 3), np.float32)
    pos[:TS, 0] = PAST + np.arange(TS) % NS
    pos[:, 1] = np.arange(128)
    pos[:, 2] = 128 + np.arange(128)
    ang = (pos[:, :, None] * inv[None, None, :]).astype(np.float32)
    cos[...] = np.cos(ang)
    sin[...] = np.sin(ang)
    return cos, sin


def _branches(dist, ok=True):
    n = 0
    for w, d in ((128, 1), (512, 4), (2048, 16)):
        n = n + ((dist >= 0) & (dist <= w) & (dist % d == 0) & ok).astype(int)
    return n


def _masks():
    import numpy as np
    q, k = np.arange(128)[:, None], np.arange(128)[None, :]
    prompt = np.concatenate([_branches(q - k), _branches(128 + q - k), _branches(q - k)], 1)
    s = (np.arange(64) % NS)[:, None]
    r, g = np.divmod(np.arange(RA * GA), GA)
    old = _branches(PAST + s - (16 * g + r)[None, :])
    r, g = np.divmod(np.arange(RB * GB), GB)
    last = _branches(PAST + s - (OLD + RB * g + r)[None, :])
    decode = np.concatenate([old, np.zeros((64, TS), int), last], 1)
    b = np.arange(NB)[None, :, None]
    c = np.arange(TS)[None, None, :]
    new = _branches(s[:, :, None] - c % NS, c // NS == b)
    out = []
    for m in (prompt, decode, new):
        out += [np.where(m > 0, 0.0, -1e30).astype(np.dtype("bfloat16")), m.astype(np.dtype("bfloat16"))]
    return out


_INS = ["x_prompt", "x_sample", "state_attn_k", "state_attn_v", "state_conv", "p_prompt", "p_sample",
        "w_in", "w_conv", "w_out", "ln1_g", "ln1_b", "peer_wq", "peer_subkeys", "peer_u", "peer_v",
        "ln2_g", "ln2_b", "ple_gate", "ple_proj"]
_OUTS = [(1, TP, D), (NB, NS, D), (1, 1, TP, HEADS, DH), (1, 1, TP, HEADS, DH), (1, 1, 2, DC),
         (1, NB, PAST, HEADS, DH), (1, NB, PAST, HEADS, DH), (1, NB, 2, DC)]


def kernel(**inputs):
    import numpy as _np
    import concourse.bacc as _bacc
    from concourse import mybir as _mybir
    from concourse.bass_utils import run_bass_kernel_spmd as _run

    nc = _bacc.Bacc("TRN2", target_bir_lowering=False, num_devices=1)
    arrays, args = {}, []

    def give(name, a):
        a = _np.ascontiguousarray(a)
        arrays[name] = a
        args.append(nc.dram_tensor(name, a.shape, _mybir.dt.from_np(a.dtype), kind="ExternalInput").ap())

    for name in _INS:
        give(f"in_{name}", inputs[name])
    cos, sin = _rope_tables()
    consts = [_np.eye(128, dtype=_np.float32), cos, sin, *_masks(),
              _np.tile(_np.arange(TOPK, dtype=_np.float32), (128, 1))]
    for i, a in enumerate(consts):
        give(f"const_{i}", a)
    for i, shape in enumerate(_OUTS):
        args.append(nc.dram_tensor(f"out_{i}", shape, _mybir.dt.float32, kind="ExternalOutput").ap())
    decoder_step(nc, *args)
    r = _run(nc, [arrays], core_ids=[0])
    return tuple(r.results[0][f"out_{i}"] for i in range(len(_OUTS)))
```

```python
import concourse.bass as bass
from concourse import mybir
from contextlib import ExitStack

D = 2048
HEADS, DH = 8, 128
DA = HEADS * DH
DC = D - DA
TP, NB, NS = 256, 8, 8
TS = NB * NS
N = TS + TP
PAST = 2048
KT = D // 128
SCALE = float(DH) ** -0.5
ALPHA = 2.0 ** 0.25
EPS = 1e-5
TILES = [(0, TS), (TS, 128), (TS + 128, 128)]
PH, NK, TOPK = 8, 128, 16
NF = 2 * PH
PLE = 256
CW = 512
KP = 4
PPC = KT // KP
GA, RA = 96, 8
OLD = 16 * GA
GB, RB = 128, 4
K_PARTS = (8, 16, 24)
SCOLS = GA * RA + TS + GB * RB
ZW = 2 + TP + NB * (2 + NS)
Z0 = 2 + TP
KT_BANKS = (3, 4, 7)
NSLOT = 8
PHASES = [("u", 1, 8), ("u", 2, 8), ("v", 1, 8), ("u", 0, 4), ("v", 2, 8), ("v", 0, 4)]
STARTS = [sum(p[2] for p in PHASES[:n]) for n in range(len(PHASES))]
BLOCKS = sum(p[2] for p in PHASES)


T_ALL = [(t, g, (4 * t + g) % 8) for t in range(3) for g in range(4)]
T_MID = [(t, g, g + (4 if t else 0)) for t in range(3) for g in range(4)]
T_LAST = [(t, g, g + (0 if t else 4)) for t in (1, 2, 0) for g in range(4)]
SCORES = ([(1, g, 4 * (g % 2)) for g in range(4)] + [(2, g, 4 + g) for g in range(4)] +
          [(0, g, g) for g in range(4)])
T_ROUNDS = [(T_ALL, 8), (T_MID, 4), (T_LAST, 4)]


def decoder_step(nc, x_p, x_s, st_k, st_v, st_c, p_p, p_s, w_in, w_conv, w_out, ln1_g, ln1_b,
                 wq, subkeys, peer_u, peer_v, ln2_g, ln2_b, w_gate, w_ple,
                 c_ident, c_cos, c_sin, c_mp_add, c_mp_mul, c_ms_add, c_ms_mul, c_mc_add, c_mc_mul,
                 c_iota,
                 y_p, y_s, o_kp, o_vp, o_cp, o_ks, o_vs, o_cs):
    f32, f32r, bf16, u32 = mybir.dt.float32, mybir.dt.float32r, mybir.dt.bfloat16, mybir.dt.uint32
    ALU = mybir.AluOpType
    ACT = mybir.ActivationFunctionType
    AX = mybir.AxisListType.X
    ds = bass.ds
    KB = 1024

    xp_v = x_p.rearrange("a (t p) d -> p (a t) d", p=128)
    xs_v = x_s.rearrange("b s d -> (b s) d")
    pp_v = p_p.rearrange("a b (t p) d -> p (a b t) d", p=128)
    ps_v = p_s.rearrange("a b s d -> (a b s) d")
    kst = st_k.rearrange("a b n h d -> (a b) n (h d)")
    vst = st_v.rearrange("a b n h d -> (a b) n (h d)")
    oks = o_ks.rearrange("a b n h d -> (a b) n (h d)")
    ovs = o_vs.rearrange("a b n h d -> (a b) n (h d)")
    okp = o_kp.rearrange("a b (t p) h d -> p (a b t) (h d)", p=128)
    ovp = o_vp.rearrange("a b (t p) h d -> p (a b t) (h d)", p=128)
    wiew = lambda w: w.rearrange("a (k p) e -> p (a k) e", p=128)
    win_v, wout_v, wq_v, wg_v, wple_v = map(wiew, (w_in, w_out, wq, w_gate, w_ple))
    u_tab = peer_u.rearrange("a n d -> (a n) d")
    v_tab = peer_v.rearrange("a n d -> (a n) d")
    yp_v = y_p.rearrange("a (t p) d -> p (a t) d", p=128)
    ys_v = y_s.rearrange("b s d -> (b s) d")

    BASE = 16512
    used = []

    def at(name, shape, dt, off):
        used.append(name)
        return nc.alloc_sbuf_tensor_at(name, shape, dt, offset=BASE + off)

    raw = at("w_raw", [128, 2, KP, CW], f32, 0)
    whi = at("w_hi", [128, 2, KP, CW], f32r, 16 * KB)
    wlo = at("w_lo", [128, 2, KP, CW], f32r, 32 * KB)
    ka = at("keys_old", [GA, RA, DA], f32, 0)
    kb = at("keys_last", [GB, RB, DA], f32, 32 * KB)
    zrows = at("conv_rows_out", [2 + 2 * NB, DC], f32, 0)
    sc = at("peer_scores", [128, 2, NF, NK], f32, 0)
    cand = at("candidates", [128, PH, TOPK, TOPK], f32, 24 * KB)
    hot = at("one_hot", [128, PH, TOPK, TOPK], f32, 32 * KB)

    qkv_p = at("qkv_prompt", [128, 2, 3 * DA], f32, 48 * KB)
    ubuf = at("conv_u", [128, 8, ZW], f32, 72 * KB)
    zbuf = at("conv_z", [128, 8, ZW], f32, 72 * KB + 8 * ZW * 4)
    crow = at("conv_state_rows", [2 * NB, DC], f32, 72 * KB)
    va = at("values_old", [GA, RA, DA], f32, 48 * KB)
    vb = at("values_last", [GB, RB, DA], f32, 80 * KB)
    ln1 = at("ln1_gain_bias", [128, 2, D], f32, 48 * KB)
    qpt = at("peer_queries", [128, NF, N], f32, 64 * KB)
    ring = at("expert_rows", [128, NSLOT, D], f32, 48 * KB)
    pleo = at("ple_out", [128, 3, D], f32, 0)
    plew = at("ple_weights", [128, 2, D], f32, 24 * KB)
    pnat = at("ple_tokens", [128, 3, PLE], f32, 40 * KB)
    pT = at("ple_T", [128, 2, N], f32, 43 * KB)
    graw = at("gate_w_raw", [128, 2, KP, CW], f32, 24 * KB)
    ghi = at("gate_w_hi", [128, 2, KP, CW], f32r, 40 * KB)
    yup = at("expert_sums_upper", [128, D], f32, 56 * KB)
    yhalf = at("expert_sums_half", [TS, D], f32, 64 * KB)
    glo = at("gate_w_lo", [128, 2, KP, CW], f32r, 72 * KB)
    gsig = at("gate_sigmoid", [128, 3, CW], f32, 88 * KB)

    qkv_s = at("qkv_decode", [TS, 3 * DA], f32, 96 * KB)
    qt = at("q_T", [128, HEADS, N], f32, 108 * KB)
    kt_ = at("k_T", [128, HEADS, N], f32, 118 * KB)
    ln2 = at("ln2_gain_bias", [128, 2, D], f32, 112 * KB)

    xt = at("x_tokens", [128, 3, D], f32, 128 * KB)
    rtmp = at("rope_products", [128, 4, DA], f32, 128 * KB)
    psm = at("prompt_scores", [128, 2, 3, 128], f32, 144 * KB)
    ppt = at("prompt_probs_T", [128, 2, 3, 128], f32, 147 * KB)
    ktb = at("old_k_T", [128, 3, 512], f32, 128 * KB)
    ssm = at("decode_scores", [128, SCOLS], f32, 134 * KB)
    pta = at("probs_T_old", [GA, RA, 64], f32, 140 * KB)
    ptb = at("probs_T_last", [GB, RB, 64], f32, 142 * KB)
    ptc = at("probs_T_new", [TS, 64], f32, 143 * KB)
    qpad = at("q_padded", [128, HEADS, 32], f32, 144 * KB)
    osb = at("decode_out", [128, 2 * DH], f32, 145 * KB)

    thi = at("act_T_hi", [128, KT, N], f32r, 152 * KB)
    tlo = at("act_T_lo", [128, KT, N], f32r, 172 * KB)
    yacc = at("expert_sums", [128, 2, D], f32, 152 * KB)
    S0 = 184 * KB
    top = at("top_values", [128, NF, TOPK], f32, S0)
    topi = at("top_keys", [128, NF, TOPK], u32, S0 + 1 * KB)
    topf = at("top_keys_f", [128, NF, TOPK], f32, S0 + 2 * KB)
    ctop = at("cand_top", [128, PH, TOPK], f32, S0 + 3 * KB)
    cidx = at("cand_index", [128, PH, TOPK], u32, S0 + 3 * KB + 512)
    cint = at("cand_rank_int", [128, 2, PH, TOPK], u32, S0 + 4 * KB)
    cflt = at("cand_rank", [128, 2, PH, TOPK], f32, S0 + 5 * KB)
    esel = at("expert_part", [128, 2, PH, TOPK], f32, S0 + 6 * KB)

    sel_b = (top, topi, topf, ctop, cidx, cint, cflt, esel, cand, hot)
    A0 = 84 * KB
    sc1 = at("first_peer_scores", [128, NF, NK], f32, 92 * KB)
    SEL = {0: (sc[:, 0],) + sel_b, 2: (sc[:, 1],) + sel_b,
           1: (sc1[:, :, :],
               at("first_top_values", [128, NF, TOPK], f32, A0),
               at("first_top_keys", [128, NF, TOPK], u32, A0 + 1 * KB),
               at("first_top_keys_f", [128, NF, TOPK], f32, A0 + 2 * KB),
               at("first_cand_top", [128, PH, TOPK], f32, A0 + 3 * KB),
               at("first_cand_index", [128, PH, TOPK], u32, A0 + 3 * KB + 512),
               at("first_cand_rank_int", [128, 2, PH, TOPK], u32, A0 + 4 * KB),
               at("first_cand_rank", [128, 2, PH, TOPK], f32, A0 + 5 * KB),
               at("first_expert_part", [128, 2, PH, TOPK], f32, A0 + 6 * KB),
               at("first_candidates", [128, PH, TOPK, TOPK], f32, 48 * KB),
               at("first_one_hot", [128, PH, TOPK, TOPK], f32, 56 * KB))}

    M0 = 192 * KB
    off = [M0]

    def small(name, shape, dt, size):
        n = size
        for s in shape[1:]:
            n *= s
        t = at(name, shape, dt, off[0])
        off[0] += (n + 31) // 32 * 32
        return t

    ident = small("identity", [128, 128], f32, 4)
    subT = small("subkeys_T", [128, 2, NK], f32, 4)
    cosb = small("rope_cos", [128, 3, DH // 2], f32, 4)
    sinb = small("rope_sin", [128, 3, DH // 2], f32, 4)
    cw = small("conv_weights", [128, 3, 8], f32, 4)
    mx = small("row_max", [128, 4], f32, 4)
    nmx = small("neg_row_max", [128, 2, 2], f32, 4)
    rs = small("row_sum", [128, 4], f32, 4)
    bst = small("ln_stats", [128, 3, 4, 6], f32, 4)
    mv = small("ln_mean_var", [128, 2], f32, 4)
    vst_ = small("ln_var_eps", [128, 1], f32, 4)
    std = small("ln_std", [128, 2], f32, 4)
    iota = small("iota16", [128, TOPK], f32, 4)
    tok = small("pool_token", [128, 1], f32, 4)
    idxc = small("block_experts", [128, 2, TOPK], u32, 4)
    hblk = small("block_dots", [128, 2 * TOPK], f32, 4)
    ablk = small("block_gates", [128, 2 * TOPK], f32, 4)
    zl = small("conv_last_rows_T", [128, 8, 2 + 2 * NB], f32, 4)
    mp_add = small("prompt_mask_add", [128, 384], bf16, 2)
    mp_mul = small("prompt_mask_mul", [128, 384], bf16, 2)
    shared = off[0]
    ms_add = small("decode_mask_add", [128, SCOLS], bf16, 2)
    ms_mul = small("decode_mask_mul", [128, SCOLS], bf16, 2)
    mc_add = small("new_mask_add", [128, NB, TS], bf16, 2)
    mc_mul = small("new_mask_mul", [128, NB, TS], bf16, 2)
    assert BASE + off[0] <= 229344, off[0]
    end_masks = off[0]
    off[0] = shared
    idx_all = small("experts", [128, (BLOCKS + 1) * TOPK], u32, 4)
    idx_s = small("experts_decode", [64, 2, 64], u32, 4)
    gates = small("gates", [128, 3, 128], f32, 4)
    hdot = small("dots", [128, 3, 128], f32, 4)
    assert off[0] <= end_masks
    subn = at("subkeys_rows", [128, 2, 128], f32, 76 * KB + 512)

    ctx = ExitStack()
    with ctx:
        PS = ctx.enter_context(nc.psum_tensor("psum", [128, 8, 512], f32))
        sem = lambda name: ctx.enter_context(nc.semaphore(name))
        xd_in = sem("x_decode_in")
        x_in, c_in, c2_in = sem("x_in"), sem("consts_in"), sem("late_consts_in")
        w_in_s = [sem("w_slot0_in"), sem("w_slot1_in")]
        w_hi_ready, w_lo_ready, w_used = sem("w_hi_ready"), sem("w_lo_ready"), sem("w_used")
        acc_free = sem("acc_free")
        tp_done, th_ready, tl_ready = sem("transposed"), sem("t_hi_ready"), sem("t_lo_ready")
        small_T, small_ok = sem("small_transposed"), sem("small_copied")
        dstep = sem("dve_step")
        z_pad = sem("z_pad_set")
        rope_ok = sem("rope_done")
        zl_ready, zl_T, zl_out = sem("conv_rows_ready"), sem("conv_rows_T"), sem("conv_rows_copied")
        conv_m, conv_hi = sem("conv_ready"), sem("conv_hi_ready")
        qk_T, qk_ok = sem("qk_transposed"), sem("qk_copied")
        s_score, s_neg, s_exp, s_prob = sem("p_scores"), sem("p_negmax"), sem("p_exp"), sem("p_probs")
        s_pT, s_pok, s_pv, s_po = sem("p_probs_T"), sem("p_probs_T_ok"), sem("p_out"), sem("p_out_copied")
        k_in = [sem(f"keys_part{i}_in") for i in range(3)]
        v_in, v_used = ([sem(f"values_part{i}_{what}") for i in range(2)] for what in ("in", "used"))
        q_pad, kT_raw, kT_ok = sem("q_pad_ready"), sem("old_kT_psum"), sem("old_kT_copied")
        d_score, d_neg, d_exp, d_prob = sem("d_scores"), sem("d_negmax"), sem("d_exp"), sem("d_probs")
        d_pT, d_pok = sem("d_probs_T"), sem("d_probs_T_ok")
        d_out, d_oT, d_oread = sem("d_out_copied"), sem("d_out_T"), sem("d_out_T_read")
        att_ok = sem("decode_att_done")
        var_ok, std_ok = sem("ln_var_ready"), sem("ln_std_ready")
        ln_ok = sem("ln_done")
        ln1_in, ln2_in = sem("ln1_in"), sem("ln2_in")
        sc_psum, sc_ok = sem("scores_psum"), sem("scores_copied")
        g_sub, g_exp = sem("gate_logits"), sem("gate_exp")
        g_free, g_token = sem("ring_free"), sem("pool_token_done")
        g_in = [sem(f"row_slot{i}_in") for i in range(NSLOT)]
        idx_st = sem("block_staged")
        dots, gelu_ok = sem("dots_ready"), sem("gelu_ready")
        pack_rd, pack_in = sem("pack_ready"), sem("packed_in")
        fold_rd, fold_in = sem("fold_ready"), sem("folded_in")
        ring_done = sem("ring_done")
        ple_in, pT_psum, pT_ok, ple_ps, ple_ok = (sem("ple_in"), sem("ple_T_psum"), sem("ple_T_ok"),
                                                  sem("ple_psum"), sem("ple_copied"))
        sig_ok, fin_ok = sem("sigmoid_ready"), sem("final_ready")
        out_s, kvcopy = sem("outputs_written"), sem("cache_copied")
        zrow_s = sem("conv_rows_written")

        W_MAIN, W_GATE = (raw, whi, wlo), (graw, ghi, glo)
        ydec = PS[:, 4:8, :].rearrange("p a c -> p (a c)")

        block = ctx.enter_context(nc.Block())

        @block.sync
        def _(sp):
            copies = [0]

            def copy_part(src, dst, b, j):
                n = (PAST - NS) * DA // 128
                s = src[b, NS:PAST, :] if isinstance(b, int) else src[ds(b, 1), NS:PAST, :].rearrange("a n d -> (a n) d")
                o = dst[b, 0:PAST - NS, :] if isinstance(b, int) else dst[ds(b, 1), 0:PAST - NS, :].rearrange("a n d -> (a n) d")
                s = s.rearrange("n d -> (n d)").rearrange("(p m) -> p m", m=n)
                o = o.rearrange("n d -> (n d)").rearrange("(p m) -> p m", m=n)
                sp.dma_start(o[16 * j:16 * j + 16, :], s[16 * j:16 * j + 16, :]).then_inc(kvcopy, 16)

            def copy_batch(src, dst, b, first=0, last=8):
                for j in range(first, last):
                    copy_part(src, dst, b, j)

            def load_piece(view, cols, pc, k, bufs=W_MAIN):
                slot = k % 2
                if not (isinstance(pc, int) and pc < 2):
                    sp.wait_ge(w_lo_ready, pc - 1)
                sp.dma_start(bufs[0][:, slot, :, :], view[:, k * KP:(k + 1) * KP, cols]).then_inc(w_in_s[slot], 16)

            def load_chunks(view, col0, pc0, pairs, src=None, dst=None, b0=0, skip=0, bufs=W_MAIN, part0=0, extra=0):
                def pair(i, first):
                    for x in range(first, 2 * PPC):
                        c = i * (2 * CW) + (col0 + x // PPC * CW)
                        load_piece(view, slice(c, c + CW) if isinstance(i, int) else ds(c, CW),
                                   i * (2 * PPC) + (pc0 + x), x % PPC, bufs)
                        if src is not None and x >= part0:
                            copy_part(src, dst, i + b0, x)
                        if x % 2 == 1 and x // 2 < extra:
                            copy_part(vst, ovs, i + b0, x // 2)

                if skip or pairs == 1:
                    pair(0, skip)
                if pairs - bool(skip) == 1 and pairs > 1:
                    pair(1, 0)
                elif pairs > 1:
                    with sp.Fori(int(bool(skip)), pairs) as i:
                        pair(i, 0)

            sp.dma_start(ident[:, :], c_ident).then_inc(xd_in, 16)
            sp.dma_start(xt[0:TS, 0, :], xs_v).then_inc(xd_in, 16)
            load_piece(win_v, slice(0, CW), 0, 0)
            sp.dma_start(xt[:, 1:3, :], xp_v).then_inc(x_in, 16)
            load_piece(win_v, slice(0, CW), 1, 1)
            sp.dma_start(crow[:, :], st_c.rearrange("a b j d -> (a b j) d")).then_inc(c_in, 16)
            sp.dma_start(subn[:, :, :], subkeys.rearrange("a q k c -> k (a q) c")).then_inc(c_in, 16)
            for dst, src in ((cosb, c_cos), (sinb, c_sin), (mp_add, c_mp_add), (mp_mul, c_mp_mul),
                             (ms_add, c_ms_add), (ms_mul, c_ms_mul), (mc_add, c_mc_add),
                             (mc_mul, c_mc_mul), (iota, c_iota)):
                sp.dma_start(dst[...], src).then_inc(c2_in, 16)
            with nc.allow_non_contiguous_dma(reason="3072 weights, once"):
                sp.dma_start(cw[:, :, :], w_conv.rearrange("a j (f p) -> p (a j) f", p=128)).then_inc(c2_in, 16)
            copy_batch(kst, oks, 0, 0, 2)
            copy_batch(vst, ovs, 0, 0, 1)
            load_chunks(win_v, 0, 0, 3, kst, oks, 0, skip=2, extra=3)
            load_chunks(win_v, 3 * DA, 24, 1, kst, oks, 3, extra=1)
            load_chunks(win_v, 3 * DA + 2 * DC, 32, 1, kst, oks, 4, extra=1)
            load_chunks(win_v, 3 * DA + DC, 40, 1, kst, oks, 5, extra=1)
            sp.wait_ge(rope_ok, 1)
            sp.dma_start(okp, qkv_p[:, :, DA:2 * DA]).then_inc(out_s, 16)
            sp.dma_start(ovp, qkv_p[:, :, 2 * DA:3 * DA]).then_inc(out_s, 16)
            for b in range(NB):
                sp.dma_start(oks[b, PAST - NS:PAST, :], qkv_s[b * NS:(b + 1) * NS, DA:2 * DA]).then_inc(out_s, 16)
                sp.dma_start(ovs[b, PAST - NS:PAST, :], qkv_s[b * NS:(b + 1) * NS, 2 * DA:3 * DA]).then_inc(out_s, 16)
            sp.wait_ge(zl_out, 1)
            sp.dma_start(o_cp.rearrange("a b j d -> (a b j) d"), zrows[0:2, :]).then_inc(zrow_s, 16)
            sp.dma_start(o_cs.rearrange("a b j d -> (a b j) d"), zrows[2:2 + 2 * NB, :]).then_inc(zrow_s, 16)
            sp.wait_ge(zrow_s, 32)

            def load_k(b):
                bb = ds(b, 1)
                for part, last in enumerate(K_PARTS):
                    if not (isinstance(b, int) and b == 0):
                        sp.wait_ge(kT_raw, (b - 1) * 24 + last)
                    rr = slice(4 * part, 4 * part + 4)
                    if part < 2:
                        sp.dma_start(ka[:, rr, :], kst[bb, 0:OLD, :].rearrange("a (g r) d -> (a g) r d", r=16)[:, rr, :]).then_inc(k_in[part], 16)
                    else:
                        sp.dma_start(kb[:, :, :], kst[bb, OLD:PAST, :].rearrange("a (g r) d -> (a g) r d", r=RB)).then_inc(k_in[part], 16)

            def load_v(b):
                bb = ds(b, 1)
                first = isinstance(b, int) and b == 0
                if not first:
                    sp.wait_ge(v_used[0], b)
                sp.dma_start(va[:, :, :], vst[bb, 0:OLD, :].rearrange("a (g r) d -> (a g) r d", r=16)[:, 0:RA, :]).then_inc(v_in[0], 16)
                if not first:
                    sp.wait_ge(v_used[1], b)
                sp.dma_start(vb[:, :, :], vst[bb, OLD:PAST, :].rearrange("a (g r) d -> (a g) r d", r=RB)).then_inc(v_in[1], 16)

            load_k(0)
            copy_batch(vst, ovs, 0, 3)
            sp.wait_ge(out_s, 16 * (2 + 2 * NB))
            sp.wait_ge(s_po, HEADS)
            load_v(0)
            load_k(1)
            copy_batch(vst, ovs, 3, 1, 4)
            with sp.Fori(1, NB - 1) as b:
                load_k(b + 1)
                load_v(b)
            sp.wait_ge(kT_raw, NB * 24)
            for k in range(2):
                load_piece(wout_v, slice(0, CW), 48 + k, k)
            load_v(NB - 1)
            copy_batch(vst, ovs, 1, 3)
            sp.wait_ge(att_ok, 1)
            for k in range(2, PPC):
                load_piece(wout_v, slice(0, CW), 48 + k, k)
            sp.dma_start(xt[:, 1:3, :], xp_v).then_inc(x_in, 16)
            sp.dma_start(xt[0:TS, 0, :], xs_v).then_inc(x_in, 16)
            load_chunks(wout_v, 0, 48, 2, kst, oks, 6, skip=PPC)
            sp.dma_start(ln1[:, 0, :], ln1_g.rearrange("a d -> (a d)").partition_broadcast(128)).then_inc(ln1_in, 16)
            sp.dma_start(ln1[:, 1, :], ln1_b.rearrange("a d -> (a d)").partition_broadcast(128)).then_inc(ln1_in, 16)
            sp.dma_start(ln2[:, 0, :], ln2_g.rearrange("a d -> (a d)").partition_broadcast(128)).then_inc(ln2_in, 16)
            sp.dma_start(ln2[:, 1, :], ln2_b.rearrange("a d -> (a d)").partition_broadcast(128)).then_inc(ln2_in, 16)
            for k in range(2):
                load_piece(wq_v, slice(0, CW), 64 + k, k)
            copy_batch(kst, oks, 6, 0, PPC)
            copy_batch(vst, ovs, 2, 3)
            copy_batch(vst, ovs, 3, 4, 6)
            copy_batch(vst, ovs, 4, 1, 2)
            load_chunks(wq_v, 0, 64, 2, vst, ovs, 4, skip=2, part0=1)
            sp.dma_start(xt[TS:128, 0, :], xt[0:TS, 0, :]).then_inc(pack_in, 16)
            copy_batch(vst, ovs, 3, 6)
            for b in range(6, NB):
                copy_batch(vst, ovs, b, 0, PPC)
            sp.wait_ge(pack_rd, 1)
            for n, s in enumerate([k for k, p in zip(STARTS, PHASES) if p[1] == 0]):
                for half in range(2):
                    sp.dma_start(idx_all[half * TS:(half + 1) * TS, s * TOPK:(s + 4) * TOPK],
                                 idx_s[:, half, :]).then_inc(pack_in, 16)
            sp.dma_start(gates[TS:128, 0, 0:64], gates[0:TS, 0, 64:128]).then_inc(pack_in, 16)
            sp.dma_start(plew[:, :, :], wple_v).then_inc(ple_in, 16)
            sp.dma_start(pnat[:, 1:3, :], pp_v).then_inc(ple_in, 16)
            sp.dma_start(pnat[0:TS, 0, :], ps_v).then_inc(ple_in, 16)
            sp.wait_ge(ple_ok, 12)
            for k in range(2):
                load_piece(wg_v, slice(0, CW), 80 + k, k, W_GATE)
            sp.wait_ge(fold_rd, 1)
            sp.dma_start(yhalf[:, :], yup[TS:128, :]).then_inc(fold_in, 16)
            load_chunks(wg_v, 0, 80, 2, vst, ovs, 6, skip=2, bufs=W_GATE, part0=PPC)
            for c in range(4):
                sp.wait_ge(fin_ok, c + 1)
                cc = slice(c * CW, (c + 1) * CW)
                sp.dma_start(yp_v[:, :, cc], xt[:, 1:3, cc]).then_inc(out_s, 16)
                sp.dma_start(ys_v[:, cc], xt[0:TS, 0, cc]).then_inc(out_s, 16)
            sp.wait_ge(out_s, 16 * (2 + 2 * NB + 8))
            sp.wait_ge(kvcopy, 16 * 8 * 2 * NB)

        @block.gpsimd
        def _(pool):
            nc.gpsimd.memset(tok[:, :], 0.0).then_inc(g_token, 1)

            def low(pc, slot, bufs):
                pool.wait_ge(w_hi_ready, pc + 1)
                r_, h_, l_ = (b[:, slot, :, :] for b in bufs)
                nc.gpsimd.tensor_tensor(l_, r_, h_.bitcast(f32), ALU.subtract).then_inc(w_lo_ready, 1)

            def lows(first, count, bufs=W_MAIN):
                with pool.Fori(0, count // 2) as i:
                    for slot in range(2):
                        low(i * 2 + (first + slot), slot, bufs)

            lows(0, 80)

            def gathers(k, half, table):
                for j in range(TOPK):
                    if j % 4 == 0:
                        pool.wait_ge(g_token, k * 4 + (j // 4 + 1))
                        pool.wait_ge(idx_st, k + 1)
                        pool.wait_ge(g_free, k * TOPK + (j + 4))
                        nc.gpsimd.tensor_tensor(tok[:, :], tok[:, :], tok[:, :], ALU.add).then_inc(g_token, 1)
                    pool.indirect_dma_start(ring[:, j % NSLOT, :], None, table,
                                            bass.IndirectOffsetOnAxis(idxc[:, half, j:j + 1], 0)).then_inc(g_in[j % NSLOT], 16)

            for (kind, t, nb), k0 in zip(PHASES, STARTS):
                with pool.Fori(0, nb // 2) as i:
                    for half in range(2):
                        gathers(i * 2 + (k0 + half), half, u_tab if kind == "u" else v_tab)
            pool.wait_ge(ring_done, 1)
            lows(80, 16, W_GATE)

        @block.scalar
        def _(act):
            A = nc.scalar.activation

            def hi(pc, slot, bufs=W_MAIN):
                act.wait_ge(w_in_s[slot], (pc - slot) * 8 + 16)
                if not (isinstance(pc, int) and pc < 2):
                    act.wait_ge(w_used, pc - 1)
                A(bufs[1][:, slot, :, :], bufs[0][:, slot, :, :], ACT.Copy).then_inc(w_hi_ready, 1)

            def his(first, count):
                with act.Fori(0, count // 2) as i:
                    for slot in range(2):
                        hi(i * 2 + (first + slot), slot)

            def transposed_hi(use, first=0, last=12):
                for n in range(first, last):
                    t, g, bank = T_ROUNDS[use][0][n]
                    c0, r = TILES[t]
                    act.wait_ge(tp_done, use * 12 + n + 1)
                    A(thi[:, 4 * g:4 * g + 4, c0:c0 + r],
                      PS[:, bank, :].rearrange("p (a c) -> p a c", a=4)[:, :, 0:r], ACT.Copy).then_inc(th_ready, 1)

            transposed_hi(0, 0, 4)
            hi(0, 0)
            transposed_hi(0, 4, 12)
            act.wait_ge(small_T, 1)
            A(zbuf[:, :, Z0:ZW].rearrange("p f (b j) -> p f b j", b=NB)[:, :, :, 0:2],
              PS[:, 4, 0:128].rearrange("p (f b j) -> p f b j", f=8, b=NB), ACT.Copy).then_inc(small_ok, 1)
            act.wait_ge(small_T, 2)
            A(subT[:, :, :], PS[:, 5, 0:256].rearrange("p (a c) -> p a c", a=2), ACT.Copy).then_inc(small_ok, 1)
            hi(1, 1)
            his(2, 46)
            act.wait_ge(zl_T, 1)
            act.wait_ge(w_lo_ready, 48)
            A(zrows[:, :], PS[0:2 + 2 * NB, 0:2, :].rearrange("p a c -> p (a c)"), ACT.Copy).then_inc(zl_out, 1)
            act.wait_ge(conv_m, 1)
            A(thi[:, 8:16, TS:N], ubuf[:, :, 0:TP], ACT.Copy).then_inc(conv_hi, 1)
            for b in range(NB):
                A(thi[:, 8:16, b * NS:(b + 1) * NS], ubuf[:, :, Z0 + 10 * b:Z0 + 10 * b + NS], ACT.Copy).then_inc(conv_hi, 1)
            for j in range(16):
                act.wait_ge(qk_T, j + 1)
                dst = (qt, kt_)[j % 2]
                A(dst[:, j // 2, :], PS[:, 2 + j % 6, 0:N], ACT.Copy).then_inc(qk_ok, 1)
            def prompt_exp(h):
                e = h % 2
                act.wait_ge(s_neg, h + 1)
                A(psm[:, e, 0, :], psm[:, e, 0, :], ACT.Exp, bias=nmx[:, e, 0:1], scale=SCALE)
                A(psm[:, e, 1:3, :], psm[:, e, 1:3, :], ACT.Exp, bias=nmx[:, e, 1:2], scale=SCALE).then_inc(s_exp, 1)

            prompt_exp(0)
            for h in range(HEADS):
                e = h % 2
                if h + 1 < HEADS:
                    prompt_exp(h + 1)
                act.wait_ge(s_pT, h + 1)
                A(ppt[:, e, :, :].rearrange("p a c -> p (a c)"), PS[:, 2 + e, 0:384], ACT.Copy).then_inc(s_pok, 1)
            def key_copies(b):
                for n in range(24):
                    act.wait_ge(kT_raw, b * 24 + (n + 1))
                    w = 4 * (GA if n < 16 else GB)
                    A(ktb[:, n % 3, 0:w], PS[:, KT_BANKS[n % 3], 0:w], ACT.Copy).then_inc(kT_ok, 1)

            def exps(b):
                act.wait_ge(d_neg, b + 1)
                A(ssm[:, :], ssm[:, :], ACT.Exp, bias=nmx[:, 0, 0:1], scale=SCALE).then_inc(d_exp, 1)

            def prob_copies(b):
                act.wait_ge(d_pT, b + 1)
                A(pta[:, :, :].rearrange("p a c -> p (a c)"), PS[0:GA, 6, :], ACT.Copy)
                A(ptb[:, :, :].rearrange("p a c -> p (a c)"), PS[:, 5, 0:256], ACT.Copy)
                A(ptc[:, :], PS[0:TS, 5, 256:320], ACT.Copy).then_inc(d_pok, 1)

            def out_copies(b):
                act.wait_ge(v_used[1], b + 1)
                for i in range(4):
                    m = A(osb[32 * i:32 * i + 16, :], PS[32 * i:32 * i + 16, 6, 0:256], ACT.Copy)
                m.then_inc(d_out, 1)

            key_copies(0)
            exps(0)
            with act.Fori(1, NB) as b:
                key_copies(b)
                prob_copies(b - 1)
                exps(b)
                out_copies(b - 1)
            prob_copies(NB - 1)
            hi(48, 0)
            hi(49, 1)
            out_copies(NB - 1)

            def layer_norm_root(n):
                act.wait_ge(var_ok, n + 1)
                A(std[:, 0:1], vst_[:, :], ACT.Sqrt).then_inc(std_ok, 1)

            his(50, 14)
            hi(64, 0)
            hi(65, 1)
            layer_norm_root(0)
            layer_norm_root(1)
            transposed_hi(1, 0, 8)
            layer_norm_root(2)
            transposed_hi(1, 8, 12)

            def score_copy(n):
                act.wait_ge(sc_psum, n + 1)
                t, g, bank = SCORES[n]
                r = TILES[t][1]
                A(SEL[t][0][0:r, 4 * g:4 * g + 4, :].rearrange("p a c -> p (a c)"), PS[0:r, bank, :], ACT.Copy).then_inc(sc_ok, 1)

            for c in range(4):
                for k in range(PPC):
                    if c > 0 or k > 1:
                        hi(64 + c * PPC + k, k % 2)
                    if k == 2 and c > 0:
                        score_copy(c - 1)
            for n in range(3, 12):
                score_copy(n)

            def gate_exp(n, t):
                r = TILES[t][1]
                act.wait_ge(g_sub, n + 1)
                A(gates[0:r, t, :], gates[0:r, t, :], ACT.Exp).then_inc(g_exp, 1)

            def dots_gelu(n, t, w):
                act.wait_ge(dots, n + 1)
                A(hdot[:, t, 0:w], hdot[:, t, 0:w], ACT.Gelu).then_inc(gelu_ok, 1)

            gate_exp(0, 1)
            gate_exp(1, 2)
            dots_gelu(0, 1, 128)
            gate_exp(2, 0)
            dots_gelu(1, 2, 128)
            for t in range(3):
                c0, r = TILES[t]
                act.wait_ge(pT_psum, t + 1)
                A(pT[:, :, c0:c0 + r], PS[:, t, 0:256].rearrange("p (a c) -> p a c", a=2)[:, :, 0:r], ACT.Copy).then_inc(pT_ok, 1)
            for n in range(12):
                c, t = divmod(n, 3)
                r = TILES[t][1]
                act.wait_ge(ple_ps, n + 1)
                A(pleo[0:r, t, c * CW:(c + 1) * CW], PS[0:r, n % 4, :], ACT.Copy).then_inc(ple_ok, 1)
            dots_gelu(2, 0, 64)
            for n in range(3, 5):
                layer_norm_root(n)
            transposed_hi(2, 0, 8)
            hi(80, 0, W_GATE)
            act.wait_ge(ring_done, 1)
            hi(81, 1, W_GATE)
            layer_norm_root(5)
            transposed_hi(2, 8, 12)

            def sigmoids(c, bank):
                act.wait_ge(w_used, c * PPC + 84)
                if not (isinstance(c, int) and c == 0):
                    act.wait_ge(fin_ok, c)
                for t in range(3):
                    r = TILES[t][1]
                    m = A(gsig[0:r, t, :], PS[0:r, bank + t, :], ACT.Sigmoid)
                m.then_inc(sig_ok, 1)

            for c in range(4):
                for k in range(PPC):
                    if c > 0 or k > 1:
                        hi(80 + c * PPC + k, k % 2, W_GATE)
                    if k == 1 and c > 0:
                        sigmoids(c - 1, 4 * ((c - 1) % 2))
            sigmoids(3, 4)

        @block.vector
        def _(dve):
            V = nc.vector
            step = [0]

            def link(ins, base=None):
                step[0] += 1
                ins.then_inc(dstep, 1)
                dve.wait_ge(dstep, step[0] if base is None else base + step[0])

            def transposed_lo(use, first=0, last=12):
                for n in range(first, last):
                    t, g, bank = T_ROUNDS[use][0][n]
                    c0, r = TILES[t]
                    dve.wait_ge(th_ready, use * 12 + n + 1)
                    V.tensor_tensor(tlo[:, 4 * g:4 * g + 4, c0:c0 + r],
                                    PS[:, bank, :].rearrange("p (a c) -> p a c", a=4)[:, :, 0:r],
                                    thi[:, 4 * g:4 * g + 4, c0:c0 + r].bitcast(f32), ALU.subtract).then_inc(tl_ready, 1)

            def prompt_out(h):
                e = h % 2
                dve.wait_ge(s_pv, h + 1)
                link(V.tensor_scalar(thi[:, h, TS:N], PS[:, 4 + e, 0:TP], 1.0, None, ALU.mult))
                V.tensor_tensor(tlo[:, h, TS:N], PS[:, 4 + e, 0:TP], thi[:, h, TS:N].bitcast(f32), ALU.subtract).then_inc(s_po, 1)

            V.memset(zbuf[:, :, 0:2], 0.0).then_inc(z_pad, 1)
            transposed_lo(0)
            with dve.Fori(0, 3) as i:
                for h in range(2):
                    dve.wait_ge(w_used, i * 8 + 4 * (h + 1))
                    for t in range(3):
                        dst = (qkv_s[:, ds(i * DA + h * CW, CW)] if t == 0
                               else qkv_p[:, t - 1, ds(i * DA + h * CW, CW)])
                        m = V.tensor_scalar(dst, PS[0:TILES[t][1], 4 * h + t, :], 1.0, None, ALU.mult)
                    m.then_inc(acc_free, 1)
            dve.wait_ge(acc_free, 6)
            dve.wait_ge(c2_in, 160)
            for t in range(3):
                r = TILES[t][1]
                hd = 2 * HEADS
                src = (qkv_s[:, 0:2 * DA] if t == 0 else qkv_p[:, t - 1, 0:2 * DA]).rearrange("p (h d) -> p h d", h=hd)
                x1, x2 = src[:, :, 0:DH // 2], src[:, :, DH // 2:DH]
                cb = cosb[0:r, t, :].unsqueeze(1).broadcast_to([r, hd, DH // 2])
                sb_ = sinb[0:r, t, :].unsqueeze(1).broadcast_to([r, hd, DH // 2])
                tm = [rtmp[0:r, j, :].rearrange("p (h d) -> p h d", h=hd) for j in range(4)]
                for j, (a, b) in enumerate(((x1, cb), (x2, sb_), (x2, cb), (x1, sb_))):
                    m = V.tensor_tensor(tm[j], a, b, ALU.mult)
                link(m)
                V.tensor_tensor(x1, tm[0], tm[1], ALU.subtract)
                link(V.tensor_tensor(x2, tm[2], tm[3], ALU.add))
            V.memset(nmx[:, :, :], 0.0).then_inc(rope_ok, 1)
            for c in range(6, 8):
                dve.wait_ge(w_used, 4 * (c + 1))
                if c == 6:
                    dve.wait_ge(small_ok, 1)
                for j in range(4):
                    m = V.tensor_scalar(ubuf[:, 4 * (c - 6) + j, 0:N], PS[:, 4 * (c % 2) + j, 0:N], 1.0, None, ALU.mult)
                m.then_inc(acc_free, 1)
            dve.wait_ge(acc_free, 8)
            for c in range(8, 10):
                dve.wait_ge(w_used, 4 * (c + 1))
                for j in range(4):
                    f = 4 * (c - 8) + j
                    ps = PS[:, 4 * (c % 2) + j, :]
                    V.tensor_tensor(zbuf[:, f, 2:Z0], ps[:, TS:N], ubuf[:, f, TS:N], ALU.mult)
                    m = V.tensor_tensor(zbuf[:, f, Z0:ZW].rearrange("p (b j) -> p b j", b=NB)[:, :, 2:2 + NS],
                                        ps[:, 0:TS].rearrange("p (b s) -> p b s", b=NB),
                                        ubuf[:, f, 0:TS].rearrange("p (b s) -> p b s", b=NB), ALU.mult)
                m.then_inc(acc_free, 1)
            dve.wait_ge(acc_free, 10)
            V.tensor_copy(zl[:, :, 0:2], zbuf[:, :, TP:TP + 2])
            V.tensor_copy(zl[:, :, 2:2 + 2 * NB].rearrange("p f (b j) -> p f b j", b=NB),
                          zbuf[:, :, Z0:ZW].rearrange("p f (b j) -> p f b j", b=NB)[:, :, :, NS:NS + 2]).then_inc(zl_ready, 1)
            W2 = ZW - 2
            for j in range(3):
                for f in range(8):
                    o = ubuf[:, f, 0:W2]
                    if j == 0:
                        m = V.tensor_scalar(o, zbuf[:, f, 0:W2], cw[:, 0, f:f + 1], None, ALU.mult)
                    else:
                        m = V.scalar_tensor_tensor(out=o, in0=zbuf[:, f, j:j + W2], scalar=cw[:, j, f:f + 1], in1=o,
                                                   op0=ALU.mult, op1=ALU.add)
                link(m)
            for c in range(10, 12):
                dve.wait_ge(w_used, 4 * (c + 1))
                for j in range(4):
                    f = 4 * (c - 10) + j
                    ps = PS[:, 4 * (c % 2) + j, :]
                    V.tensor_tensor(ubuf[:, f, 0:TP], ps[:, TS:N], ubuf[:, f, 0:TP], ALU.mult)
                    o = ubuf[:, f, Z0:ZW].rearrange("p (b j) -> p b j", b=NB)[:, :, 0:NS]
                    m = V.tensor_tensor(o, ps[:, 0:TS].rearrange("p (b s) -> p b s", b=NB), o, ALU.mult)
                m.then_inc(acc_free, 1)
            dve.wait_ge(acc_free, 12)
            V.memset(rs[:, :], 0.0).then_inc(conv_m, 1)
            dve.wait_ge(conv_hi, 1 + NB)
            V.tensor_tensor(tlo[:, 8:16, TS:N], ubuf[:, :, 0:TP], thi[:, 8:16, TS:N].bitcast(f32), ALU.subtract)
            for b in range(NB):
                cc = slice(b * NS, (b + 1) * NS)
                m = V.tensor_tensor(tlo[:, 8:16, cc], ubuf[:, :, Z0 + 10 * b:Z0 + 10 * b + NS],
                                    thi[:, 8:16, cc].bitcast(f32), ALU.subtract)
            link(m)
            def prompt_max(h):
                e = h % 2
                dve.wait_ge(s_score, h + 1)
                w = psm[:, e, :, :].rearrange("p a c -> p (a c)")
                link(V.tensor_tensor(w, PS[:, e, 0:384], mp_add[:, :], ALU.add))
                V.reduce_max(mx[:, 0:1], w[:, 0:128], AX)
                link(V.reduce_max(mx[:, 1:2], w[:, 128:384], AX))
                V.tensor_scalar(nmx[:, e, :], mx[:, 0:2], -SCALE, None, ALU.mult).then_inc(s_neg, 1)

            prompt_max(0)
            for h in range(HEADS):
                e = h % 2
                w = psm[:, e, :, :].rearrange("p a c -> p (a c)")
                if h + 1 < HEADS:
                    if h > 0:
                        dve.wait_ge(s_pT, h)
                    dve.wait_ge(s_neg, h + 1)
                    prompt_max(h + 1)
                dve.wait_ge(s_exp, h + 1)
                for q, (a, b) in enumerate(((0, 128), (128, 384))):
                    m = V.scalar_tensor_tensor(out=w[:, a:b], in0=w[:, a:b], scalar=1.0, in1=mp_mul[:, a:b],
                                               op0=ALU.mult, op1=ALU.mult, accum_out=rs[:, q:q + 1])
                link(m)
                link(V.reciprocal(rs[:, 2:4], rs[:, 0:2]))
                V.tensor_scalar(w[:, 0:128], w[:, 0:128], rs[:, 2:3], None, ALU.mult)
                link(V.tensor_scalar(w[:, 128:384], w[:, 128:384], rs[:, 3:4], None, ALU.mult))
                V.memset(mx[:, 3:4], 0.0).then_inc(s_prob, 1)
                if h > 0:
                    prompt_out(h - 1)
            prompt_out(HEADS - 1)
            V.memset(osb[:, :], 0.0)
            link(V.memset(qpad[:, :, :], 0.0))
            V.memset(mx[:, 1:2], 0.0).then_inc(d_oread, 1)

            def pad_queries(b, ib):
                col = slice(b * NS, (b + 1) * NS) if isinstance(b, int) else ds(b * NS, NS)
                for h in range(HEADS):
                    m = V.tensor_scalar(qpad[:, h, (h % 2) * NS:(h % 2 + 1) * NS], qt[:, h, col], 1.0, None, ALU.mult)
                link(m, ib)
                V.memset(mx[:, 2:3], 0.0).then_inc(q_pad, 1)

            def new_masks(b, ib):
                bb = slice(b, b + 1) if isinstance(b, int) else ds(b, 1)
                for m_, c_ in ((ms_add, mc_add), (ms_mul, mc_mul)):
                    m = V.tensor_scalar(m_[:, GA * RA:GA * RA + TS], c_[:, bb, :].rearrange("p a c -> p (a c)"),
                                        1.0, None, ALU.mult)
                link(m, ib)

            def softmax(b, ib, pad_next=True):
                dve.wait_ge(d_score, b + 1)
                if not (isinstance(b, int) and b == 0):
                    dve.wait_ge(d_pT, b)
                V.tensor_tensor(ssm[:, 0:480], PS[:, 0, 0:480], ms_add[:, 0:480], ALU.add)
                V.tensor_tensor(ssm[:, 480:832], PS[:, 1, 0:352], ms_add[:, 480:832], ALU.add)
                link(V.tensor_tensor(ssm[:, 832:SCOLS], PS[:, 2, :], ms_add[:, 832:SCOLS], ALU.add), ib)
                link(V.reduce_max(mx[:, 0:1], ssm[:, :], AX), ib)
                V.tensor_scalar(nmx[:, 0, 0:1], mx[:, 0:1], -SCALE, None, ALU.mult).then_inc(d_neg, 1)
                if pad_next:
                    pad_queries(b + 1, ib)
                dve.wait_ge(d_exp, b + 1)
                link(V.scalar_tensor_tensor(out=ssm[:, :], in0=ssm[:, :], scalar=1.0, in1=ms_mul[:, :],
                                            op0=ALU.mult, op1=ALU.mult, accum_out=rs[:, 0:1]), ib)
                if pad_next:
                    new_masks(b + 1, ib)
                link(V.reciprocal(rs[:, 1:2], rs[:, 0:1]), ib)
                link(V.tensor_scalar(ssm[:, :], ssm[:, :], rs[:, 1:2], None, ALU.mult), ib)
                V.memset(mx[:, 3:4], 0.0).then_inc(d_prob, 1)

            def decode_out(b, ib):
                dve.wait_ge(d_oT, b + 1)
                col = slice(b * NS, (b + 1) * NS) if isinstance(b, int) else ds(b * NS, NS)
                o = PS[:, 5, 384:448].rearrange("p (g i s) -> p i g s", g=2, s=NS)
                hi_ = thi[:, 0:8, col].rearrange("p (i g) s -> p i g s", i=4)
                lo_ = tlo[:, 0:8, col].rearrange("p (i g) s -> p i g s", i=4)
                link(V.tensor_scalar(hi_, o, 1.0, None, ALU.mult), ib)
                V.tensor_tensor(lo_, o, hi_.bitcast(f32), ALU.subtract).then_inc(d_oread, 1)
                dve.wait_ge(d_oread, b + 2)

            pad_queries(0, None)
            new_masks(0, None)
            softmax(0, None)
            base0, PER = step[0], 8
            with dve.Fori(1, NB - 1) as b:
                step[0] = base0
                ib = (b - 1) * PER
                softmax(b, ib)
                decode_out(b - 1, ib)
                assert step[0] == base0 + PER
            step[0] = base0 + (NB - 2) * PER
            softmax(NB - 1, None, False)
            decode_out(NB - 2, None)
            decode_out(NB - 1, None)
            V.memset(mx[:, 0:4], 0.0).then_inc(att_ok, 1)
            dve.wait_ge(x_in, 16 * 3)
            for c in range(4):
                dve.wait_ge(w_used, 48 + 4 * (c + 1))
                cc = slice(c * CW, (c + 1) * CW)
                for t in range(3):
                    o = xt[0:TILES[t][1], t, cc]
                    m = V.scalar_tensor_tensor(out=o, in0=o, scalar=ALPHA, in1=PS[0:TILES[t][1], 4 * (c % 2) + t, :],
                                               op0=ALU.mult, op1=ALU.add)
                m.then_inc(acc_free, 1)
                dve.wait_ge(acc_free, 13 + c)
                for t in range(3):
                    m = V.bn_stats(bst[0:TILES[t][1], t, c, :], xt[0:TILES[t][1], t, cc])
            link(m)

            def layer_norm(n, t, gb, stats=True):
                r = TILES[t][1]
                x = xt[0:r, t, :]
                if stats:
                    for c in range(4):
                        m = V.bn_stats(bst[0:r, t, c, :], x[:, c * 512:(c + 1) * 512])
                    link(m)
                link(V.bn_aggr(mv[0:r, :], bst[0:r, t, :, :].rearrange("p a c -> p (a c)")))
                link(V.memset(vst_[:, :], 1.0))
                V.tensor_scalar(vst_[0:r, :], mv[0:r, 1:2], EPS, None, ALU.add).then_inc(var_ok, 1)
                dve.wait_ge(std_ok, n + 1)
                link(V.reciprocal(std[0:r, 1:2], std[0:r, 0:1]))
                link(V.tensor_scalar(x, x, mv[0:r, 0:1], std[0:r, 1:2], ALU.subtract, ALU.mult))
                link(V.tensor_tensor(x, x, gb[0:r, 0, :], ALU.mult))
                V.tensor_tensor(x, x, gb[0:r, 1, :], ALU.add).then_inc(ln_ok, 1)

            dve.wait_ge(ln1_in, 32)
            layer_norm(0, 0, ln1, False)
            layer_norm(1, 1, ln1, False)
            transposed_lo(1, 0, 8)
            layer_norm(2, 2, ln1, False)
            transposed_lo(1, 8, 12)

            def top_keys(t, h0=0, h1=PH):
                r = TILES[t][1]
                scores, top, topi, *_ = SEL[t]
                for f in range(2 * h0, 2 * h1):
                    m = V.max(top[0:r, f, 0:8], scores[0:r, f, :])
                link(m)
                for f in range(2 * h0, 2 * h1):
                    m = V.max_index(topi[0:r, f, 0:8], top[0:r, f, 0:8], scores[0:r, f, :])
                link(m)
                for f in range(2 * h0, 2 * h1):
                    m = V.match_replace(scores[0:r, f, :], top[0:r, f, 0:8], scores[0:r, f, :], -3e38)
                link(m)

            def top_keys_rest(t, h0=0, h1=PH):
                r = TILES[t][1]
                scores, top, topi, *_ = SEL[t]
                for f in range(2 * h0, 2 * h1):
                    m = V.max(top[0:r, f, 8:16], scores[0:r, f, :])
                link(m)
                for f in range(2 * h0, 2 * h1):
                    m = V.max_index(topi[0:r, f, 8:16], top[0:r, f, 8:16], scores[0:r, f, :])
                link(m)

            def top_candidates(t, h0=0, h1=PH):
                r = TILES[t][1]
                _, top, topi, topf, ctop, cidx, _, _, _, cand, _ = SEL[t]
                fs = slice(2 * h0, 2 * h1)
                V.tensor_copy(topf[0:r, fs, :], topi[0:r, fs, :])
                tv = top[0:r, fs, :].rearrange("p (h q) k -> p h q k", q=2)
                full = [r, h1 - h0, TOPK, TOPK]
                link(V.tensor_tensor(cand[0:r, h0:h1, :, :], tv[:, :, 0, :].unsqueeze(3).broadcast_to(full),
                                     tv[:, :, 1, :].unsqueeze(2).broadcast_to(full), ALU.add))
                cf = lambda h: cand[0:r, h, :, :].rearrange("p a c -> p (a c)")
                for h in range(h0, h1):
                    m = V.max(ctop[0:r, h, 0:8], cf(h))
                link(m)
                for h in range(h0, h1):
                    m = V.max_index(cidx[0:r, h, 0:8], ctop[0:r, h, 0:8], cf(h))
                link(m)
                for h in range(h0, h1):
                    m = V.match_replace(cf(h), ctop[0:r, h, 0:8], cf(h), -3e38)
                link(m)

            def top_ranks(t, h0=0, h1=PH):
                r = TILES[t][1]
                _, _, _, _, ctop, cidx, cint, cflt, _, cand, _ = SEL[t]
                cf = lambda h: cand[0:r, h, :, :].rearrange("p a c -> p (a c)")
                for h in range(h0, h1):
                    m = V.max(ctop[0:r, h, 8:16], cf(h))
                link(m)
                for h in range(h0, h1):
                    m = V.max_index(cidx[0:r, h, 8:16], ctop[0:r, h, 8:16], cf(h))
                link(m)
                V.tensor_single_scalar(cint[0:r, 0, h0:h1, :], cidx[0:r, h0:h1, :], 4, ALU.logical_shift_right)
                link(V.tensor_single_scalar(cint[0:r, 1, h0:h1, :], cidx[0:r, h0:h1, :], 15, ALU.bitwise_and))
                link(V.tensor_copy(cflt[0:r, :, h0:h1, :], cint[0:r, :, h0:h1, :]))

            def top_select(t, q, h0=0, h1=PH):
                r = TILES[t][1]
                _, _, _, topf, _, _, _, cflt, esel, _, hot = SEL[t]
                full = [r, h1 - h0, TOPK, TOPK]
                fv = topf[0:r, 2 * h0:2 * h1, :].rearrange("p (h q) k -> p h q k", q=2)
                hv = hot[0:r, h0:h1, :, :]
                link(V.tensor_tensor(hv, cflt[0:r, q, h0:h1, :].unsqueeze(3).broadcast_to(full),
                                     iota[0:r, :].unsqueeze(1).unsqueeze(1).broadcast_to(full), ALU.is_equal))
                link(V.tensor_tensor(hv, hv, fv[:, :, q, :].unsqueeze(2).broadcast_to(full), ALU.mult))
                link(V.tensor_reduce(esel[0:r, q, h0:h1, :], hv, AX, ALU.add))

            def top_experts(n, t, go=False):
                r = TILES[t][1]
                ctop, esel = SEL[t][4], SEL[t][8]
                g = gates[0:r, t, :].rearrange("p (h k) -> p h k", h=PH)
                V.tensor_tensor(g, ctop[0:r, :, :], ctop[0:r, :, 0:1].broadcast_to([r, PH, TOPK]),
                                ALU.subtract).then_inc(g_sub, 1)
                e1, e2 = (esel[0:r, q, :, :].rearrange("p h k -> p (h k)") for q in range(2))
                outs = ([idx_s[:, :, :].rearrange("p a c -> p (a c)")] if t == 0 else
                        [idx_all[:, s_ * TOPK:(s_ + 8) * TOPK] for s_, p in zip(STARTS, PHASES) if p[1] == t])
                for o in outs:
                    m = V.scalar_tensor_tensor(out=o, in0=e1, scalar=float(NK), in1=e2, op0=ALU.mult, op1=ALU.add)
                link(m)
                if go:
                    dve.wait_ge(sc_ok, 12)
                    V.tensor_scalar(idxc[:, 0, :], idx_all[:, 0:TOPK], 0, None, ALU.add).then_inc(idx_st, 1)
                    V.memset(mx[:, 0:1], 0.0).then_inc(g_free, NSLOT)
                dve.wait_ge(g_exp, n + 1)
                sums = SEL[0][4]
                link(V.tensor_reduce(sums[0:r, :, 0], g, AX, ALU.add))
                link(V.reciprocal(sums[0:r, :, 1], sums[0:r, :, 0]))
                link(V.tensor_tensor(g, g, sums[0:r, :, 1:2].broadcast_to([r, PH, TOPK]), ALU.mult))

            def select_first(c):
                dve.wait_ge(sc_ok, c + 1)
                hs = (2 * c, 2 * c + 2)
                top_keys(1, *hs)
                top_keys_rest(1, *hs)
                top_candidates(1, *hs)
                top_ranks(1, *hs)
                top_select(1, 0, *hs)
                top_select(1, 1, *hs)

            for c in range(4):
                dve.wait_ge(w_used, 64 + 4 * (c + 1))
                for j in range(4):
                    m = V.tensor_scalar(qpt[:, 4 * c + j, :], PS[:, 4 * (c % 2) + j, 0:N], 1.0, None, ALU.mult)
                m.then_inc(acc_free, 1)
                if c > 0:
                    select_first(c - 1)
            select_first(3)
            V.memset(idx_all[:, BLOCKS * TOPK:(BLOCKS + 1) * TOPK], 0)
            top_experts(0, 1, True)
            V.memset(ydec, 0.0)
            link(V.memset(yacc[:, :, :], 0.0))

            def expert_blocks(kind, t, k0, first, pairs, middle=None):
                x = xt[:, t, :]
                y = yacc[:, t - 1, :] if t else ydec
                base1 = step[0]

                def pair(i, ib):
                    if kind == "v":
                        link(V.tensor_scalar(ablk[:, :], hdot[:, t, ds(i * 32, 32)], 1.0, None, ALU.mult), ib)
                    for half in range(2):
                        k = i * 2 + (k0 + half)
                        V.tensor_scalar(idxc[:, 1 - half, :], idx_all[:, ds(i * 32 + (k0 + half + 1) * TOPK, TOPK)], 0, None, ALU.add).then_inc(idx_st, 1)
                        for j in range(TOPK):
                            g = ring[:, j % NSLOT, :]
                            c = half * TOPK + j
                            dve.wait_ge(g_in[j % NSLOT], k * 32 + 16 * (j // NSLOT + 1))
                            if kind == "u":
                                V.scalar_tensor_tensor(out=g, in0=g, scalar=1.0, in1=x, op0=ALU.mult, op1=ALU.mult,
                                                       accum_out=hblk[:, c:c + 1]).then_inc(g_free, 1)
                            else:
                                dve.wait_ge(g_free, k * TOPK + (NSLOT + j))
                                V.scalar_tensor_tensor(out=y, in0=g, scalar=ablk[:, c:c + 1], in1=y,
                                                       op0=ALU.mult, op1=ALU.add).then_inc(g_free, 1)
                        dve.wait_ge(g_free, k * TOPK + (NSLOT + TOPK))
                        if half == 0 and middle is not None:
                            middle()
                    if kind == "u":
                        link(V.tensor_scalar(hdot[:, t, ds(i * 32, 32)], hblk[:, :], 1.0, None, ALU.mult), ib)

                if pairs == 1:
                    pair(first, None)
                else:
                    with dve.Fori(first, first + pairs) as i:
                        step[0] = base1
                        pair(i, i - first)
                        assert step[0] == base1 + 1
                    step[0] = base1 + pairs

            def add_experts(t):
                x = xt[:, t, :]
                link(V.scalar_tensor_tensor(out=x, in0=x, scalar=ALPHA, in1=yacc[:, t - 1, :],
                                            op0=ALU.mult, op1=ALU.add))

            for n, ((kind, t, nb), k0) in enumerate(zip(PHASES, STARTS)):
                if kind == "v":
                    m = [1, 2, 0].index(t)
                    dve.wait_ge(gelu_ok, m + 1)
                    w = 128 if t else 64
                    link(V.tensor_tensor(hdot[:, t, 0:w], hdot[:, t, 0:w], gates[:, t, 0:w], ALU.mult))
                if n < 2:
                    nt = (2, 0)[n]
                    expert_blocks(kind, t, k0, 0, 1, lambda: top_keys(nt))
                    top_keys_rest(nt)
                    expert_blocks(kind, t, k0, 1, 1, lambda: top_candidates(nt))
                    top_ranks(nt)
                    expert_blocks(kind, t, k0, 2, 1, lambda: top_select(nt, 0))
                    top_select(nt, 1)
                    top_experts(n + 1, nt)
                    if nt == 0:
                        V.memset(mx[:, 1:2], 0.0).then_inc(pack_rd, 1)
                    expert_blocks(kind, t, k0, 3, 1)
                elif n < 4:
                    if n == 2:
                        dve.wait_ge(pack_in, 16 * 6)
                    expert_blocks(kind, t, k0, 0, nb // 2)
                elif n == 4:
                    dve.wait_ge(ln2_in, 32)
                    expert_blocks(kind, t, k0, 0, 1, lambda: add_experts(1))
                    layer_norm(3, 1, ln2)
                    expert_blocks(kind, t, k0, 1, 3)
                else:
                    expert_blocks(kind, t, k0, 0, 1, lambda: add_experts(2))
                    layer_norm(4, 2, ln2)
                    expert_blocks(kind, t, k0, 1, 1, lambda: transposed_lo(2, 0, 8))
                if kind == "u":
                    V.memset(mx[:, 3:4], 0.0).then_inc(dots, 1)
            V.memset(mx[:, 0:1], 0.0).then_inc(ring_done, 1)
            V.tensor_scalar(yup[TS:128, :], PS[TS:128, 4:8, :].rearrange("p a c -> p (a c)"), 1.0, None, ALU.mult).then_inc(fold_rd, 1)
            xd = xt[0:TS, 0, :]
            link(V.scalar_tensor_tensor(out=xd, in0=xd, scalar=ALPHA, in1=PS[0:TS, 4:8, :].rearrange("p a c -> p (a c)"),
                                        op0=ALU.mult, op1=ALU.add))
            dve.wait_ge(fold_in, 16)
            link(V.tensor_tensor(xd, xd, yhalf[:, :], ALU.add))
            layer_norm(5, 0, ln2)
            transposed_lo(2, 8, 12)
            for c in range(4):
                dve.wait_ge(sig_ok, c + 1)
                cc = slice(c * CW, (c + 1) * CW)
                for t in range(3):
                    r = TILES[t][1]
                    m = V.tensor_tensor(gsig[0:r, t, :], gsig[0:r, t, :], pleo[0:r, t, cc], ALU.mult)
                link(m)
                for t in range(3):
                    r = TILES[t][1]
                    m = V.tensor_tensor(xt[0:r, t, cc], xt[0:r, t, cc], gsig[0:r, t, :], ALU.add)
                m.then_inc(fin_ok, 1)

        @block.tensor
        def _(pe):
            MM, TR = nc.tensor.matmul, nc.tensor.transpose

            def transposes(use, first=0, last=12):
                plan, again = T_ROUNDS[use]
                for n in range(first, last):
                    t, g, bank = plan[n]
                    r = TILES[t][1]
                    if n >= again and plan[n][2] == plan[n - again][2]:
                        pe.wait_ge(tl_ready, use * 12 + n - again + 1)
                    for j in range(4):
                        m = TR(PS[:, bank, 128 * j:128 * j + r], xt[0:r, t, (4 * g + j) * 128:(4 * g + j + 1) * 128],
                               ident[0:r, 0:r])
                    m.then_inc(tp_done, 1)

            def split_mm(out, lhs, rhs, start, stop):
                (lh, ll), (rh, rl) = lhs, rhs
                MM(out, lh, rh, start=start, stop=False)
                MM(out, lh, rl, start=False, stop=False)
                return MM(out, ll, rh, start=False, stop=stop)

            def token_piece(pc, k, bank, bufs=W_MAIN, tiles=(0, 1, 2)):
                pe.wait_ge(w_lo_ready, pc + 1)
                s = k % 2
                _, whi, wlo = bufs
                for kk in range(KP):
                    q = k * KP + kk
                    for t in tiles:
                        c0 = TILES[t][0]
                        m = split_mm(PS[:, bank + t, :], (thi[:, q, c0:c0 + 128], tlo[:, q, c0:c0 + 128]),
                                     (whi[:, s, kk, :], wlo[:, s, kk, :]), q == 0, q == KT - 1)
                if 0 in tiles:
                    m.then_inc(w_used, 1)

            def feature_piece(pc, k, bank):
                pe.wait_ge(w_lo_ready, pc + 1)
                s = k % 2
                for kk in range(KP):
                    q = k * KP + kk
                    for j in range(4):
                        cc = slice(j * 128, (j + 1) * 128)
                        m = split_mm(PS[:, bank + j, 0:N], (whi[:, s, kk, cc], wlo[:, s, kk, cc]),
                                     (thi[:, q, :], tlo[:, q, :]), q == 0, q == KT - 1)
                m.then_inc(w_used, 1)

            def chunks(piece, cc0, pairs, free0):
                with pe.Fori(0, pairs) as i:
                    for h in range(2):
                        for k in range(PPC):
                            if k == 0 and free0:
                                pe.wait_ge(acc_free, i * 2 + (cc0 + h - 1))
                            piece(i * 8 + (cc0 * 4 + h * 4 + k), k, 4 * h)

            pe.wait_ge(xd_in, 32)
            transposes(0, 0, 4)
            pe.wait_ge(x_in, 16)
            transposes(0, 4, 12)
            pe.wait_ge(c_in, 32)
            pe.wait_ge(tl_ready, 5)
            for f in range(8):
                m = TR(PS[:, 4, f * 16:(f + 1) * 16], crow[:, f * 128:(f + 1) * 128], ident[0:16, 0:16])
            m.then_inc(small_T, 1)
            pe.wait_ge(tl_ready, 6)
            for q in range(2):
                m = TR(PS[:, 5, q * 128:(q + 1) * 128], subn[:, q, :], ident[:, :])
            m.then_inc(small_T, 1)
            pe.wait_ge(tl_ready, 12)
            pe.wait_ge(small_ok, 2)
            for h in range(2):
                for k in range(PPC):
                    token_piece(h * 4 + k, k, 4 * h)
            chunks(token_piece, 2, 2, True)
            chunks(feature_piece, 6, 3, True)
            pe.wait_ge(acc_free, 12)
            pe.wait_ge(zl_ready, 1)
            for f in range(8):
                m = TR(PS[0:18, f // 4, (f % 4) * 128:(f % 4 + 1) * 128], zl[:, f, :], ident[:, :])
            m.then_inc(zl_T, 1)
            for j in range(16):
                if j >= 6:
                    pe.wait_ge(qk_ok, j - 5)
                col = (j % 2) * DA + (j // 2) * DH
                for t in range(3):
                    c0, r = TILES[t]
                    src = qkv_s[:, col:col + DH] if t == 0 else qkv_p[:, t - 1, col:col + DH]
                    m = TR(PS[:, 2 + j % 6, c0:c0 + r], src, ident[0:r, 0:r])
                m.then_inc(qk_T, 1)
            pe.wait_ge(qk_ok, 16)
            pe.wait_ge(zl_out, 1)

            def prompt_scores(h):
                e = h % 2
                for t in range(2):
                    m = MM(PS[:, e, 128 * t:128 * t + 128 * (t + 1)], qt[:, h, TS + 128 * t:TS + 128 * (t + 1)],
                           kt_[:, h, TS:TS + 128 * (t + 1)], start=True, stop=True)
                m.then_inc(s_score, 1)

            prompt_scores(0)
            prompt_scores(1)
            pe.wait_ge(s_neg, 1)
            prompt_scores(2)
            for h in range(HEADS):
                e = h % 2
                if h + 3 < HEADS:
                    pe.wait_ge(s_neg, h + 2)
                    prompt_scores(h + 3)
                pe.wait_ge(s_prob, h + 1)
                for a in range(3):
                    m = TR(PS[:, 2 + e, a * 128:(a + 1) * 128], psm[:, e, a, :], ident[:, :])
                m.then_inc(s_pT, 1)
                pe.wait_ge(s_pok, h + 1)
                if h >= 2:
                    pe.wait_ge(s_po, h - 1)
                vals = lambda t: qkv_p[:, t, 2 * DA + h * DH:2 * DA + (h + 1) * DH]
                MM(PS[:, 4 + e, 0:128], vals(0), ppt[:, e, 0, :], start=True, stop=True)
                MM(PS[:, 4 + e, 128:256], vals(0), ppt[:, e, 1, :], start=True, stop=False)
                MM(PS[:, 4 + e, 128:256], vals(1), ppt[:, e, 2, :], start=False, stop=True).then_inc(s_pv, 1)
            pe.wait_ge(s_po, HEADS)
            def key_transposes(n):
                w = GA if n < 16 else GB
                for j in range(4):
                    hc = slice((2 * j + n % 2) * DH, (2 * j + n % 2 + 1) * DH)
                    src = ka[:, n // 2, hc] if n < 16 else kb[:, (n - 16) // 2, hc]
                    m = TR(PS[:, KT_BANKS[n % 3], j * w:(j + 1) * w], src, ident[0:w, 0:w])
                m.then_inc(kT_raw, 1)

            def key_scores(n):
                w = GA if n < 16 else GB
                r = n // 2 if n < 16 else (n - 16) // 2
                bank, c0 = (2, r * GB) if n >= 16 else (0, r * GA) if r < 5 else (1, (r - 5) * GA)
                for j in range(4):
                    MM(PS[32 * j:32 * j + 32, bank, c0:c0 + w], qpad[:, 2 * j + n % 2, :],
                       ktb[:, n % 3, j * w:(j + 1) * w], start=(n % 2 == 0), stop=(n % 2 == 1))

            def batch_scores(b):
                pe.wait_ge(k_in[0], b * 16 + 16)
                for n in range(3):
                    key_transposes(n)
                pe.wait_ge(q_pad, b + 1)
                for n in range(24):
                    pe.wait_ge(kT_ok, b * 24 + (n + 1))
                    key_scores(n)
                    if n + 3 in K_PARTS[:2]:
                        pe.wait_ge(k_in[K_PARTS.index(n + 3) + 1], b * 16 + 16)
                    if n + 3 < 24:
                        key_transposes(n + 3)
                for g in range(2):
                    for j in range(4):
                        m = MM(PS[32 * j:32 * j + 32, 1, 288:352], qpad[:, 2 * j + g, :], kt_[:, 2 * j + g, 0:TS],
                               start=(g == 0), stop=(g == 1))
                m.then_inc(d_score, 1)

            def batch_outputs(b):
                pe.wait_ge(d_oread, b + 1)
                pe.wait_ge(d_prob, b + 1)
                rows = ident[:, :].rearrange("p (i x) -> p i x", i=4)[:, :, 0:2 * NS]
                for r in range(RA):
                    MM(PS[0:GA, 6, r * 64:(r + 1) * 64], ssm[:, r * GA:(r + 1) * GA], rows, start=True, stop=True)
                for r in range(RB):
                    MM(PS[:, 5, r * 64:(r + 1) * 64], ssm[:, 832 + r * GB:832 + (r + 1) * GB], rows, start=True, stop=True)
                MM(PS[0:TS, 5, 256:320], ssm[:, 768:832], rows, start=True, stop=True).then_inc(d_pT, 1)
                pe.wait_ge(d_pok, b + 1)
                pe.wait_ge(v_in[0], b * 16 + 16)
                tiles = ([(pta[:, r, :], va[:, r, :]) for r in range(RA)] +
                         [(ptb[:, r, :], vb[:, r, :]) for r in range(RB)] +
                         [(ptc[:, :], qkv_s[:, 2 * DA:3 * DA])])
                for n, (p, v) in enumerate(tiles):
                    if n == RA:
                        m.then_inc(v_used[0], 1)
                        pe.wait_ge(v_in[1], b * 16 + 16)
                    for i in range(4):
                        m = MM(PS[32 * i:32 * i + 16, 6, 0:256], p[:, 16 * i:16 * i + 16],
                               v[:, 256 * i:256 * (i + 1)], start=(n == 0), stop=(n == len(tiles) - 1))
                m.then_inc(v_used[1], 1)
                pe.wait_ge(d_out, b + 1)
                picks = ident[:, :].rearrange("p (i x) -> p i x", i=4)
                for g in range(2):
                    m = MM(PS[:, 5, 384 + 32 * g:416 + 32 * g], osb[:, g * DH:(g + 1) * DH],
                           picks[:, :, g * NS:(g + 1) * NS], start=True, stop=True)
                m.then_inc(d_oT, 1)

            batch_scores(0)
            with pe.Fori(1, NB) as b:
                batch_scores(b)
                batch_outputs(b - 1)
            batch_outputs(NB - 1)
            pe.wait_ge(att_ok, 1)
            for h in range(2):
                for k in range(PPC):
                    token_piece(48 + h * 4 + k, k, 4 * h)
            for h in range(2):
                pe.wait_ge(acc_free, 13 + h)
                for k in range(PPC):
                    token_piece(56 + h * 4 + k, k, 4 * h)
            for t in range(3):
                pe.wait_ge(ln_ok, t + 1)
                transposes(1, 4 * t, 4 * t + 4)
            pe.wait_ge(tl_ready, 24)

            def peer_scores(n):
                t, g, bank = SCORES[n]
                c0, r = TILES[t]
                for j in range(4):
                    f = 4 * g + j
                    m = MM(PS[0:r, bank, j * 128:(j + 1) * 128], qpt[:, f, c0:c0 + r], subT[:, f % 2, :],
                           start=True, stop=True)
                m.then_inc(sc_psum, 1)

            for c in range(4):
                pe.wait_ge(acc_free, 15 + c)
                if c >= 2:
                    pe.wait_ge(sc_ok, c - 1)
                for k in range(PPC):
                    feature_piece(64 + c * PPC + k, k, 4 * (c % 2))
                    if k == 1 and c > 0:
                        pe.wait_ge(acc_free, 16 + c)
                        peer_scores(c - 1)
            pe.wait_ge(acc_free, 20)
            peer_scores(3)
            pe.wait_ge(sc_ok, 4)
            for n in range(4, 12):
                peer_scores(n)
            pe.wait_ge(sc_ok, 12)
            pe.wait_ge(ple_in, 48)
            for t in range(3):
                r = TILES[t][1]
                for q in range(2):
                    m = TR(PS[:, t, q * 128:q * 128 + r], pnat[0:r, t, q * 128:(q + 1) * 128], ident[0:r, 0:r])
                m.then_inc(pT_psum, 1)
            pe.wait_ge(pT_ok, 3)
            for n in range(12):
                c, t = divmod(n, 3)
                c0, r = TILES[t]
                if n >= 4:
                    pe.wait_ge(ple_ok, n - 3)
                for q in range(2):
                    m = MM(PS[0:r, n % 4, :], pT[:, q, c0:c0 + r], plew[:, q, c * CW:(c + 1) * CW],
                           start=(q == 0), stop=(q == 1))
                m.then_inc(ple_ps, 1)
            pe.wait_ge(ple_ok, 12)
            pe.wait_ge(ln_ok, 5)
            transposes(2, 0, 8)
            pe.wait_ge(tl_ready, 32)
            for k in range(2):
                token_piece(80 + k, k, 0, W_GATE, (1, 2))
            pe.wait_ge(ln_ok, 6)
            transposes(2, 8, 12)
            pe.wait_ge(tl_ready, 36)
            for k in range(2):
                token_piece(80 + k, k, 0, W_GATE, (0,))
            for c in range(4):
                if c >= 2:
                    pe.wait_ge(sig_ok, c - 1)
                for k in range(PPC):
                    if c > 0 or k > 1:
                        token_piece(80 + c * 4 + k, k, 4 * (c % 2), W_GATE)


def _rope_tables():
    import numpy as np
    half = DH // 2
    inv = np.float32(10000.0) ** (-np.arange(half, dtype=np.float32) / np.float32(half))
    cos, sin = (np.zeros((128, 3, half), np.float32) for _ in range(2))
    pos = np.zeros((128, 3), np.float32)
    pos[:TS, 0] = PAST + np.arange(TS) % NS
    pos[:, 1] = np.arange(128)
    pos[:, 2] = 128 + np.arange(128)
    ang = (pos[:, :, None] * inv[None, None, :]).astype(np.float32)
    cos[...] = np.cos(ang)
    sin[...] = np.sin(ang)
    return cos, sin


def _branches(dist, ok=True):
    n = 0
    for w, d in ((128, 1), (512, 4), (2048, 16)):
        n = n + ((dist >= 0) & (dist <= w) & (dist % d == 0) & ok).astype(int)
    return n


def _masks():
    import numpy as np
    q, k = np.arange(128)[:, None], np.arange(128)[None, :]
    prompt = np.concatenate([_branches(q - k), _branches(128 + q - k), _branches(q - k)], 1)
    s = (np.arange(128) % NS)[:, None]
    r, g = np.divmod(np.arange(RA * GA), GA)
    old = _branches(PAST + s - (16 * g + r)[None, :])
    r, g = np.divmod(np.arange(RB * GB), GB)
    last = _branches(PAST + s - (OLD + RB * g + r)[None, :])
    decode = np.concatenate([old, np.zeros((128, TS), int), last], 1)
    b = np.arange(NB)[None, :, None]
    c = np.arange(TS)[None, None, :]
    new = _branches(s[:, :, None] - c % NS, c // NS == b)
    out = []
    for m in (prompt, decode, new):
        out += [np.where(m > 0, 0.0, -1e30).astype(np.dtype("bfloat16")), m.astype(np.dtype("bfloat16"))]
    return out


_INS = ["x_prompt", "x_sample", "state_attn_k", "state_attn_v", "state_conv", "p_prompt", "p_sample",
        "w_in", "w_conv", "w_out", "ln1_g", "ln1_b", "peer_wq", "peer_subkeys", "peer_u", "peer_v",
        "ln2_g", "ln2_b", "ple_gate", "ple_proj"]
_OUTS = [(1, TP, D), (NB, NS, D), (1, 1, TP, HEADS, DH), (1, 1, TP, HEADS, DH), (1, 1, 2, DC),
         (1, NB, PAST, HEADS, DH), (1, NB, PAST, HEADS, DH), (1, NB, 2, DC)]


def kernel(**inputs):
    import numpy as _np
    import concourse.bacc as _bacc
    from concourse import mybir as _mybir
    from concourse.bass_utils import run_bass_kernel_spmd as _run

    nc = _bacc.Bacc("TRN2", target_bir_lowering=False, num_devices=1)
    arrays, args = {}, []

    def give(name, a):
        a = _np.ascontiguousarray(a)
        arrays[name] = a
        args.append(nc.dram_tensor(name, a.shape, _mybir.dt.from_np(a.dtype), kind="ExternalInput").ap())

    for name in _INS:
        give(f"in_{name}", inputs[name])
    cos, sin = _rope_tables()
    consts = [_np.eye(128, dtype=_np.float32), cos, sin, *_masks(),
              _np.tile(_np.arange(TOPK, dtype=_np.float32), (128, 1))]
    for i, a in enumerate(consts):
        give(f"const_{i}", a)
    for i, shape in enumerate(_OUTS):
        args.append(nc.dram_tensor(f"out_{i}", shape, _mybir.dt.float32, kind="ExternalOutput").ap())
    decoder_step(nc, *args)
    r = _run(nc, [arrays], core_ids=[0])
    return tuple(r.results[0][f"out_{i}"] for i in range(len(_OUTS)))
```
